# Optimizing a Trainium2 kernel written in Bass

```python
import math
import jax, jax.numpy as jnp
from jax import lax
import numpy as np

D_MODEL = 1024
BATCH = 1
SEQ = 1024
DEPTH = 1

ATTN_HEADS = 8
NOPE_DIM = 64
ROPE_DIM = 32
QK_DIM = NOPE_DIM + ROPE_DIM
V_DIM = 64
Q_RANK = 384
KV_RANK = 256
ATTN_WIDTH = ATTN_HEADS * V_DIM
Q_BLOCK = 128
ROPE_THETA = 10000.0
SG_GROUPS = 4
SG_CH = 64
SG_WIDTH = SG_GROUPS * SG_CH
SG_CHUNK = 128
SSM_GROUPS = 16
SSM_CH = 16
SSM_WIDTH = SSM_GROUPS * SSM_CH
SSM_STATE = 64
MIX_WIDTH = ATTN_WIDTH + SG_WIDTH + SSM_WIDTH
IN_COLS = Q_RANK + KV_RANK + ROPE_DIM + 2 * SG_WIDTH + SSM_WIDTH
OFF_KV = Q_RANK
OFF_KR = OFF_KV + KV_RANK
OFF_SG = OFF_KR + ROPE_DIM
OFF_SSM = OFF_SG + 2 * SG_WIDTH
MOE_GROUPS = 4
EXPERTS_PER_GROUP = 8
N_EXPERTS = MOE_GROUPS * EXPERTS_PER_GROUP
TOP_K = 2
D_EXPERT = 256
MOE_BLOCK = 128
PLE_DIM = 256
EPS = 1e-6

kernel_name = 'hybrid_mla_gmlp_s5_hmoe_trunk'

def rms_norm(x, g):
    xf = x.astype(jnp.float32)
    y = xf * lax.rsqrt(jnp.mean(xf * xf, axis=-1, keepdims=True) + EPS)
    return (y * g.astype(jnp.float32)).astype(x.dtype)

def layer_norm(x, g, b):
    xf = x.astype(jnp.float32)
    mu = jnp.mean(xf, axis=-1, keepdims=True)
    xc = xf - mu
    y = xc * lax.rsqrt(jnp.mean(xc * xc, axis=-1, keepdims=True) + EPS)
    return (y * g.astype(jnp.float32) + b.astype(jnp.float32)).astype(x.dtype)

def rope_tables(seq):
    inv = 1.0 / (ROPE_THETA ** (jnp.arange(0, ROPE_DIM, 2, dtype=jnp.float32) / ROPE_DIM))
    ang = jnp.arange(seq, dtype=jnp.float32)[:, None] * inv[None, :]
    return jnp.cos(ang), jnp.sin(ang)

def apply_rope(x, cos, sin):
    x1, x2 = jnp.split(x.astype(jnp.float32), 2, axis=-1)
    c = cos[None, :, None, :]
    s = sin[None, :, None, :]
    return jnp.concatenate([x1 * c - x2 * s, x1 * s + x2 * c], axis=-1).astype(x.dtype)

def mla_attention(z_q, z_kv, k_rope, g_cq, g_ckv, w_uq, w_ukv, g_qh, g_kh, cos, sin):
    B, S, _ = z_q.shape
    q = (rms_norm(z_q, g_cq) @ w_uq).reshape(B, S, ATTN_HEADS, QK_DIM)
    kv = (rms_norm(z_kv, g_ckv) @ w_ukv).reshape(B, S, ATTN_HEADS, NOPE_DIM + V_DIM)
    k_nope, v = kv[..., :NOPE_DIM], kv[..., NOPE_DIM:]
    k_r = jnp.broadcast_to(k_rope[:, :, None, :], (B, S, ATTN_HEADS, ROPE_DIM))
    k = jnp.concatenate([k_nope, k_r], axis=-1)
    q = rms_norm(q, g_qh)
    k = rms_norm(k, g_kh)
    q = jnp.concatenate([q[..., :NOPE_DIM], apply_rope(q[..., NOPE_DIM:], cos, sin)], axis=-1)
    k = jnp.concatenate([k[..., :NOPE_DIM], apply_rope(k[..., NOPE_DIM:], cos, sin)], axis=-1)
    scale = QK_DIM ** -0.5
    n_blk = S // Q_BLOCK
    qb = q.reshape(B, n_blk, Q_BLOCK, ATTN_HEADS, QK_DIM).transpose(1, 0, 2, 3, 4)
    kpos = jnp.arange(S)

    def block(args):
        qi, bi = args
        qpos = bi * Q_BLOCK + jnp.arange(Q_BLOCK)
        s = jnp.einsum('bqhd,bkhd->bhqk', qi, k, preferred_element_type=jnp.float32) * scale
        s = jnp.where(kpos[None, :] <= qpos[:, None], s, -jnp.inf)
        pr = jax.nn.softmax(s, axis=-1)
        return jnp.einsum('bhqk,bkhd->bqhd', pr.astype(v.dtype), v)

    o = lax.map(block, (qb, jnp.arange(n_blk)))
    return o.transpose(1, 0, 2, 3, 4).reshape(B, S, ATTN_WIDTH)

def spatial_gating(z, ln_g, ln_b, w_s, b_s):
    B, S, _ = z.shape
    z = jax.nn.gelu(z)
    u, v = z[..., :SG_WIDTH], z[..., SG_WIDTH:]
    v = layer_norm(v.reshape(B, S, SG_GROUPS, SG_CH),
                   ln_g.reshape(SG_GROUPS, SG_CH), ln_b.reshape(SG_GROUPS, SG_CH))
    vc = v.reshape(B, S // SG_CHUNK, SG_CHUNK, SG_GROUPS, SG_CH)
    causal = jnp.tril(jnp.ones((SG_CHUNK, SG_CHUNK), dtype=w_s.dtype))
    w = w_s * causal[None]
    mixed = jnp.einsum('gts,bcsgd->bctgd', w, vc) + b_s.T[None, None, :, :, None]
    return u * mixed.reshape(B, S, SG_WIDTH)

def _ssm_combine(e1, e2):
    a1r, a1i, b1r, b1i = e1
    a2r, a2i, b2r, b2i = e2
    return (a2r * a1r - a2i * a1i,
            a2r * a1i + a2i * a1r,
            a2r * b1r - a2i * b1i + b2r,
            a2r * b1i + a2i * b1r + b2i)

def s5_mixer(u, lam_re, lam_im, log_dt, b_re, b_im, c_re, c_im, d_skip, w_glu, b_glu):
    B, S, _ = u.shape
    f32 = jnp.float32
    x = u.reshape(B, S, SSM_GROUPS, SSM_CH).astype(f32)
    lr = jnp.minimum(lam_re.astype(f32), -1e-4)
    li = lam_im.astype(f32)
    dt = jnp.exp(log_dt.astype(f32))
    mag = jnp.exp(lr * dt)
    ab_re, ab_im = mag * jnp.cos(li * dt), mag * jnp.sin(li * dt)
    den = lr * lr + li * li
    nr, ni = ab_re - 1.0, ab_im
    fr = (nr * lr + ni * li) / den
    fi = (ni * lr - nr * li) / den
    br, bi = b_re.astype(f32), b_im.astype(f32)
    bb_re = fr[..., None] * br - fi[..., None] * bi
    bb_im = fr[..., None] * bi + fi[..., None] * br
    bu_re = jnp.einsum('gnc,bsgc->bsgn', bb_re, x)
    bu_im = jnp.einsum('gnc,bsgc->bsgn', bb_im, x)
    a_re = jnp.broadcast_to(ab_re, bu_re.shape)
    a_im = jnp.broadcast_to(ab_im, bu_im.shape)
    _, _, h_re, h_im = lax.associative_scan(_ssm_combine, (a_re, a_im, bu_re, bu_im), axis=1)
    y = (jnp.einsum('gcn,bsgn->bsgc', c_re.astype(f32), h_re)
         - jnp.einsum('gcn,bsgn->bsgc', c_im.astype(f32), h_im)
         + d_skip.astype(f32) * x)
    g = jax.nn.gelu(y.reshape(B, S, SSM_WIDTH)).astype(u.dtype)
    return g * jax.nn.sigmoid(g @ w_glu + b_glu)

def hierarchical_moe(h, w_rg, b_rg, w_rexp, b_rexp, w1, w3, w2):
    B, S, D = h.shape
    T = B * S
    xf = h.reshape(T, D)
    g_logits = (xf @ w_rg + b_rg).astype(jnp.float32)
    g_sel = jnp.argmax(g_logits, axis=-1)
    g_w = jnp.take_along_axis(jax.nn.softmax(g_logits, axis=-1), g_sel[:, None], axis=-1)[:, 0]
    e_logits = (xf @ w_rexp + b_rexp).astype(jnp.float32).reshape(T, MOE_GROUPS, EXPERTS_PER_GROUP)
    e_in = jnp.take_along_axis(e_logits, g_sel[:, None, None], axis=1)[:, 0]
    top_v, top_i = lax.top_k(e_in, TOP_K)
    e_w = jax.nn.softmax(top_v, axis=-1) * g_w[:, None]
    e_idx = g_sel[:, None].astype(jnp.int32) * EXPERTS_PER_GROUP + top_i.astype(jnp.int32)

    TK = T * TOP_K
    flat_e = e_idx.reshape(TK)
    flat_w = e_w.reshape(TK)
    flat_tok = jnp.repeat(jnp.arange(T, dtype=jnp.int32), TOP_K)
    order = jnp.argsort(flat_e)
    se = flat_e[order]
    counts = jnp.bincount(flat_e, length=N_EXPERTS)
    start = jnp.cumsum(counts) - counts
    pcounts = (counts + MOE_BLOCK - 1) // MOE_BLOCK * MOE_BLOCK
    pend = jnp.cumsum(pcounts)
    pstart = pend - pcounts
    dest = pstart[se] + (jnp.arange(TK, dtype=jnp.int32) - start[se])
    n_blocks = -(-(TK + N_EXPERTS * (MOE_BLOCK - 1)) // MOE_BLOCK)
    NP = n_blocks * MOE_BLOCK
    row_tok = jnp.full((NP,), T, dtype=jnp.int32).at[dest].set(flat_tok[order])
    row_w = jnp.zeros((NP,), jnp.float32).at[dest].set(flat_w[order])
    blk_e = jnp.minimum(jnp.searchsorted(pend, jnp.arange(n_blocks) * MOE_BLOCK, side='right'),
                        N_EXPERTS - 1)
    xpad = jnp.concatenate([xf, jnp.zeros((1, D), xf.dtype)], axis=0)

    def expert_block(args):
        tok, e = args
        xb = xpad[tok]
        hb = jax.nn.silu(xb @ w1[e]) * (xb @ w3[e])
        return hb @ w2[e]

    yb = lax.map(expert_block, (row_tok.reshape(n_blocks, MOE_BLOCK), blk_e))
    y = jnp.zeros((T + 1, D), jnp.float32).at[row_tok].add(
        yb.reshape(NP, D).astype(jnp.float32) * row_w[:, None])
    return y[:T].reshape(B, S, D).astype(h.dtype)

def setup_inputs(seed: int = 0) -> dict:
    key = jax.random.key(seed)
    ks = iter(jax.random.split(key, 48))
    f32 = jnp.float32

    def nrm(shape, scale):
        return jax.random.normal(next(ks), shape, f32) * scale

    def gain(shape):
        return 1.0 + nrm(shape, 0.02)

    L = DEPTH
    inp = {}
    inp['x'] = nrm((BATCH, SEQ, D_MODEL), 1.0)
    inp['p'] = nrm((DEPTH, BATCH, SEQ, PLE_DIM), 1.0)
    inp['ln1'] = gain((L, D_MODEL))
    inp['w_in'] = nrm((L, D_MODEL, IN_COLS), D_MODEL ** -0.5)
    inp['g_cq'] = gain((L, Q_RANK))
    inp['g_ckv'] = gain((L, KV_RANK))
    inp['w_uq'] = nrm((L, Q_RANK, ATTN_HEADS * QK_DIM), Q_RANK ** -0.5)
    inp['w_ukv'] = nrm((L, KV_RANK, ATTN_HEADS * (NOPE_DIM + V_DIM)), KV_RANK ** -0.5)
    inp['g_qh'] = gain((L, QK_DIM))
    inp['g_kh'] = gain((L, QK_DIM))
    inp['sg_ln_g'] = gain((L, SG_WIDTH))
    inp['sg_ln_b'] = nrm((L, SG_WIDTH), 0.02)
    inp['sg_w'] = nrm((L, SG_GROUPS, SG_CHUNK, SG_CHUNK), 0.5 * SG_CHUNK ** -0.5)
    inp['sg_b'] = 1.0 + nrm((L, SG_GROUPS, SG_CHUNK), 0.1)
    inp['lam_re'] = -0.5 + nrm((L, SSM_GROUPS, SSM_STATE), 0.01)
    inp['lam_im'] = (math.pi * jnp.arange(SSM_STATE, dtype=f32))[None, None, :] + nrm((L, SSM_GROUPS, SSM_STATE), 0.01)
    inp['log_dt'] = jax.random.uniform(next(ks), (L, SSM_GROUPS, SSM_STATE), f32, math.log(1e-3), math.log(1e-1))
    inp['ssm_b_re'] = nrm((L, SSM_GROUPS, SSM_STATE, SSM_CH), (2.0 * SSM_CH) ** -0.5)
    inp['ssm_b_im'] = nrm((L, SSM_GROUPS, SSM_STATE, SSM_CH), (2.0 * SSM_CH) ** -0.5)
    inp['ssm_c_re'] = nrm((L, SSM_GROUPS, SSM_CH, SSM_STATE), (2.0 * SSM_STATE) ** -0.5)
    inp['ssm_c_im'] = nrm((L, SSM_GROUPS, SSM_CH, SSM_STATE), (2.0 * SSM_STATE) ** -0.5)
    inp['ssm_d'] = nrm((L, SSM_GROUPS, SSM_CH), 1.0)
    inp['w_glu'] = nrm((L, SSM_WIDTH, SSM_WIDTH), SSM_WIDTH ** -0.5)
    inp['b_glu'] = nrm((L, SSM_WIDTH), 0.02)
    inp['g_mix'] = gain((L, MIX_WIDTH))
    inp['w_out'] = nrm((L, MIX_WIDTH, D_MODEL), MIX_WIDTH ** -0.5)
    inp['ln2'] = gain((L, D_MODEL))
    inp['w_rg'] = nrm((L, D_MODEL, MOE_GROUPS), D_MODEL ** -0.5)
    inp['b_rg'] = nrm((L, MOE_GROUPS), 0.01)
    inp['w_rexp'] = nrm((L, D_MODEL, N_EXPERTS), D_MODEL ** -0.5)
    inp['b_rexp'] = nrm((L, N_EXPERTS), 0.01)
    inp['w1'] = nrm((L, N_EXPERTS, D_MODEL, D_EXPERT), D_MODEL ** -0.5)
    inp['w3'] = nrm((L, N_EXPERTS, D_MODEL, D_EXPERT), D_MODEL ** -0.5)
    inp['w2'] = nrm((L, N_EXPERTS, D_EXPERT, D_MODEL), D_EXPERT ** -0.5)
    inp['w_pg'] = nrm((L, D_MODEL, D_MODEL), D_MODEL ** -0.5)
    inp['b_pg'] = nrm((L, D_MODEL), 0.02)
    inp['w_ple'] = nrm((L, PLE_DIM, D_MODEL), PLE_DIM ** -0.5)
    return inp

def reference(x, p, ln1, w_in, g_cq, g_ckv, w_uq, w_ukv, g_qh, g_kh, sg_ln_g, sg_ln_b, sg_w, sg_b,
              lam_re, lam_im, log_dt, ssm_b_re, ssm_b_im, ssm_c_re, ssm_c_im, ssm_d, w_glu, b_glu,
              g_mix, w_out, ln2, w_rg, b_rg, w_rexp, b_rexp, w1, w3, w2, w_pg, b_pg, w_ple):
    cos, sin = rope_tables(x.shape[1])
    h = x
    for i in range(DEPTH):
        z = rms_norm(h, ln1[i]) @ w_in[i]
        a = mla_attention(z[..., :OFF_KV], z[..., OFF_KV:OFF_KR], z[..., OFF_KR:OFF_SG],
                          g_cq[i], g_ckv[i], w_uq[i], w_ukv[i], g_qh[i], g_kh[i], cos, sin)
        g = spatial_gating(z[..., OFF_SG:OFF_SSM], sg_ln_g[i], sg_ln_b[i], sg_w[i], sg_b[i])
        s = s5_mixer(z[..., OFF_SSM:], lam_re[i], lam_im[i], log_dt[i], ssm_b_re[i], ssm_b_im[i],
                     ssm_c_re[i], ssm_c_im[i], ssm_d[i], w_glu[i], b_glu[i])
        gm = g_mix[i]
        mix = jnp.concatenate([
            rms_norm(a, gm[:ATTN_WIDTH]),
            rms_norm(g, gm[ATTN_WIDTH:ATTN_WIDTH + SG_WIDTH]),
            rms_norm(s, gm[ATTN_WIDTH + SG_WIDTH:]),
        ], axis=-1)
        h = h + mix @ w_out[i]
        h = h + hierarchical_moe(rms_norm(h, ln2[i]), w_rg[i], b_rg[i], w_rexp[i], b_rexp[i],
                                 w1[i], w3[i], w2[i])
        h = h + jax.nn.sigmoid(h @ w_pg[i] + b_pg[i]) * (p[i] @ w_ple[i])
    return h


_drawn_inputs = setup_inputs


def setup_inputs(seed=0):
    import zlib

    import numpy as np

    out = dict(_drawn_inputs(seed))
    spreads = {}
    factors = {'g_cq': 3.434,
     'g_qh': 2.883,
     'g_kh': 3.13,
     'sg_ln_g': 8.0,
     'sg_ln_b': 8.0,
     'lam_re': 64.0,
     'b_glu': 5.13,
     'ln2': 2.737,
     'b_rg': 23.115,
     'b_rexp': 8.0,
     'b_pg': 64.0}
    for name, (base, spread) in spreads.items():
        noise = np.random.default_rng([zlib.crc32(name.encode()), seed]).standard_normal(out[name].shape)
        drawn = base * np.exp(spread * noise) if base else spread * noise
        out[name] = __import__('jax').numpy.asarray(drawn.astype(out[name].dtype))
    for name, factor in factors.items():
        out[name] = (out[name] * factor).astype(out[name].dtype)
    return out
```

```python
import concourse.bass as bass
from concourse import mybir
from contextlib import ExitStack
import math
import numpy as np

P = 128
S, D = 1024, 1024
NT, KD = S // P, D // P
H, NOPE, ROPE, VD = 8, 64, 32, 64
QK = NOPE + ROPE
RQ, RKV = 384, 256
SG, SGG = 256, 4
SSM, G, C, NS = 256, 16, 16, 64
COLS = RQ + RKV + ROPE + 2 * SG + SSM
ZC = COLS // 3
O_KR = RQ + RKV
O_SG = O_KR + ROPE
O_SSM = O_SG + 2 * SG
LC, NC = 8, S // 8
E, EG, EPG, F = 32, 4, 8, 256
PLE = 256
EPS = 1e-6
SCALE = QK ** -0.5
NEG = -1e30
OVER = (2 * S) // P - 1

fp32 = mybir.dt.float32
bf16 = mybir.dt.bfloat16
u32 = mybir.dt.uint32
i32 = mybir.dt.int32
ALU = mybir.AluOpType
ACT = mybir.ActivationFunctionType
AX = mybir.AxisListType

ROWS = {}
_n = 0
for _name, _k in (("ln1", 8), ("g_cq", 3), ("g_ckv", 2), ("g_mix", 8), ("ln2", 8), ("b_glu", 2), ("sg_b", 4)):
    ROWS[_name] = (_n, _k)
    _n += _k
NROWS = _n


def trunk_kernel(nc, x, p, ln1, w_in, g_cq, g_ckv, w_uq, w_ukv, g_qh, g_kh, sg_ln_g, sg_ln_b, sg_w,
                 sg_b, lam_re, lam_im, log_dt, ssm_b_re, ssm_b_im, ssm_c_re, ssm_c_im, ssm_d, w_glu,
                 b_glu, g_mix, w_out, ln2, w_rg, b_rg, w_rexp, b_rexp, w1, w3, w2, w_pg, b_pg,
                 w_ple, rope_cos, rope_sin, out):
    x, p, out = x[0], p[0, 0], out[0]
    (ln1, w_in, g_cq, g_ckv, w_uq, w_ukv, g_qh, g_kh, sg_ln_g, sg_ln_b, sg_w, sg_b, lam_re, lam_im,
     log_dt, ssm_b_re, ssm_b_im, ssm_c_re, ssm_c_im, ssm_d, w_glu, b_glu, g_mix, w_out, ln2, w_rg,
     b_rg, w_rexp, b_rexp, w1, w3, w2, w_pg, b_pg, w_ple) = [a[0] for a in (
         ln1, w_in, g_cq, g_ckv, w_uq, w_ukv, g_qh, g_kh, sg_ln_g, sg_ln_b, sg_w, sg_b, lam_re,
         lam_im, log_dt, ssm_b_re, ssm_b_im, ssm_c_re, ssm_c_im, ssm_d, w_glu, b_glu, g_mix, w_out,
         ln2, w_rg, b_rg, w_rexp, b_rexp, w1, w3, w2, w_pg, b_pg, w_ple)]
    ctx = ExitStack()
    with ctx:
        def sb(name, shape, dt=fp32):
            return ctx.enter_context(nc.sbuf_tensor(name, shape, dt))

        def sem(name):
            return ctx.enter_context(nc.semaphore(name))

        phase = []
        s, L = {}, {}

        def signals(letter, names, prefix=""):
            if phase:
                nc.clear_and_free_semaphores(phase)
                phase.clear()
                nc.all_engine_barrier()
            for n in names:
                s[prefix + n] = nc.alloc_semaphore(name=letter + "_" + n)
                phase.append(s[prefix + n])

        def dram(name, shape, dt=fp32):
            return nc.dram_tensor(name, shape, dt).ap()

        zs_d = dram("zs_scratch", [S, SSM])
        ys_d = dram("ys_scratch", [SSM, LC, NC])
        xs_d = dram("xs_scratch", [SSM, LC, NC])
        xf_d = dram("xf_scratch", [S, D])
        tok_d = dram("tok_scratch", [E * S, 1])
        y_d = dram("y_scratch", [2 * S, D])

        R1 = sb("R1", [P, KD * COLS])
        RQKV = sb("RQKV", [P, 20480])
        R3 = sb("R3", [P, 8192])
        R2 = sb("R2", [P, 10176])
        ident = sb("ident", [P, P])
        vecs = sb("vecs", [P, NROWS])
        small = sb("small", [P, 1400])
        PS = ctx.enter_context(nc.psum_tensor("PS", [P, 8, 512], fp32))

        def vec(name):
            a, k = ROWS[name]
            return vecs[:, a:a + k]

        def row_bcast(a):
            return a.unsqueeze(0).broadcast_to((P, a.shape[0]))

        o = [0]

        def take(n):
            o[0] += n
            return small[:, o[0] - n:o[0]]
        cos_sb = take(NT * 16).rearrange("p (t r) -> p t r", t=NT)
        sin_sb = take(NT * 16).rearrange("p (t r) -> p t r", t=NT)
        gq_b, gk_b = take(QK), take(QK)
        stat = take(96)
        eps = take(1)
        tril = take(P)
        rows_sb = take(P)
        wts = take(2 * NT).rearrange("p (t c) -> p t c", t=NT)
        dest = take(2 * NT).bitcast(u32).rearrange("p (t c) -> p t c", t=NT)

        QT = RQKV[:, 0:8192].rearrange("p (h t) -> p h t", h=H)
        KT = RQKV[:, 8192:16384].rearrange("p (h t) -> p h t", h=H)
        V = RQKV[:, 16384:20480].rearrange("p (t c) -> p t c", t=NT)
        ZG = R3[:, 4096:8192].rearrange("p (t c) -> p t c", t=NT)
        xt = [R3[:, 0:1024], R3[:, 1024:2048]]
        xT = [R3[:, 2048:3072], R3[:, 3072:4096]]
        win = R1[:, :].rearrange("p (k n) -> p k n", k=KD)
        a2 = [0]

        def in2(n):
            a2[0] += n
            return R2[:, a2[0] - n:a2[0]]
        wuq = in2(3 * 768).rearrange("p (k n) -> p k n", k=3)
        wukv = in2(2 * 1024).rearrange("p (k n) -> p k n", k=2)
        z = [in2(COLS), in2(COLS)]
        cT = in2(640)
        sq = in2(768)
        qn = in2(768).rearrange("p (h c) -> p h c", h=H)
        kn = in2(768).rearrange("p (h c) -> p h c", h=H)
        rt = small[:, 1040:1040 + 256].rearrange("p (a h c) -> p a h c", a=2, h=H)
        assert o[0] <= 1040
        sgv = sb("sgv", [P, 512])

        zp = [PS[:, c, 0:ZC] for c in range(3)]
        tA = PS[:, 3:5, :].rearrange("p b n -> p (b n)")
        tB = PS[:, 5:7, :].rearrange("p b n -> p (b n)")
        qp = PS[:, 5:7, 0:384]

        signals("a", (
            "ident", "x_loaded0", "x_loaded1", "rows_loaded", "rows_psum", "vecs", "tables_loaded", "win_loaded", "wu_loaded",
            "x_psum", "xT", "x_square", "x_rstd", "z_psum", "z", "c_square", "c_rstd", "c", "c_psum", "cT",
            "q_psum", "kv_psum", "q_square", "q_scaled", "k_square", "k_scaled", "v", "qn", "kn", "qT_psum", "kT_psum", "qT", "kT",
            "zg", "zs_stored0", "zs_stored1", "dve", "act", "pool", "tril", "k_stat", "q_stat", "x_rms", "c_rms", "q_rms", "k_rms"))

        def link(eng, name, ins, by=1):
            L[name] = L.get(name, 0) + by
            ins.then_inc(s[name], by)
            eng.wait_ge(s[name], L[name])

        with nc.Block() as block:
            @block.sync
            def _(sp):
                sp.dma_start(xt[0], x[0:P, :]).then_inc(s["x_loaded0"], 16)
                for v, a in ((ln1, "ln1"), (g_cq, "g_cq"), (g_ckv, "g_ckv"), (g_mix, "g_mix"), (ln2, "ln2"), (b_glu, "b_glu")):
                    at, k = ROWS[a]
                    sp.dma_start(rows_sb[at:at + k, :], v.rearrange("(k p) -> k p", p=P)).then_inc(s["rows_loaded"], 16)
                at, k = ROWS["sg_b"]
                sp.dma_start(rows_sb[at:at + k, :], sg_b).then_inc(s["rows_loaded"], 16)
                sp.dma_start(xt[1], x[P:2 * P, :]).then_inc(s["x_loaded1"], 16)
                for k in range(KD):
                    sp.dma_start(win[:, k, :], w_in[k * P:(k + 1) * P, :]).then_inc(s["win_loaded"], 16)
                for t in range(2, NT + 2):
                    if t < NT:
                        sp.wait_ge(s["x_psum"], t - 1)
                        sp.wait_ge(s["x_square"], t - 1)
                        sp.dma_start(xt[t % 2], x[t * P:(t + 1) * P, :]).then_inc(s["x_loaded%d" % (t % 2)], 16)
                    sp.wait_ge(s["z"], 3 * (t - 1))
                    sp.dma_start(zs_d[(t - 2) * P:(t - 1) * P, :], z[t % 2][:, O_SSM:COLS]).then_inc(s["zs_stored%d" % (t % 2)], 16)
                for u in range(2):
                    sp.wait_ge(s["zs_stored%d" % u], 16 * (NT // 2))

            @block.gpsimd
            def _(pool):
                link(pool, "pool", pool.memset(eps, EPS))
                link(pool, "pool", pool.memset(ident[:], 0.0))
                pool.affine_select(out=ident[:], in_=ident[:], compare_op=ALU.not_equal, fill=1.0, base=0,
                                   pattern=[[-1, P]], channel_multiplier=1).then_inc(s["ident"], 1)
                link(pool, "pool", pool.memset(tril, 0.0))
                pool.affine_select(out=tril, in_=tril, compare_op=ALU.is_ge, fill=NEG, base=0,
                                   pattern=[[-1, P]], channel_multiplier=1).then_inc(s["tril"], 1)
                pool.wait_ge(s["tables_loaded"], 16 * 6)
                link(pool, "pool", pool.tensor_scalar(gq_b, gq_b, SCALE, None, ALU.mult))
                for t in range(NT):
                    pool.wait_ge(s["z"], 3 * (t + 1))
                    pool.tensor_copy(ZG[:, t, :], z[t % 2][:, O_SG:O_SSM]).then_inc(s["zg"], 1)
                    for n, ready, gain, done in ((qn, "q_scaled", gq_b, "qn"), (kn, "k_scaled", gk_b, "kn")):
                        pool.wait_ge(s[ready], t + 1)
                        link(pool, "pool", pool.tensor_tensor(n, n, gain.unsqueeze(1).broadcast_to((P, H, QK)), ALU.mult))
                        x1, x2 = n[:, :, NOPE:NOPE + 16], n[:, :, NOPE + 16:QK]
                        co = cos_sb[:, t, :].unsqueeze(1).broadcast_to((P, H, 16))
                        si = sin_sb[:, t, :].unsqueeze(1).broadcast_to((P, H, 16))
                        pool.tensor_tensor(rt[:, 0], x1, si, ALU.mult)
                        pool.tensor_tensor(rt[:, 1], x2, si, ALU.mult)
                        pool.tensor_tensor(x1, x1, co, ALU.mult)
                        link(pool, "pool", pool.tensor_tensor(x2, x2, co, ALU.mult))
                        pool.tensor_tensor(x1, x1, rt[:, 1], ALU.subtract)
                        link(pool, done, pool.tensor_tensor(x2, x2, rt[:, 0], ALU.add))

            @block.scalar
            def _(act):
                act.dma_start(cos_sb, rope_cos.rearrange("(t p) r -> p t r", p=P)).then_inc(s["tables_loaded"], 16)
                act.dma_start(sin_sb, rope_sin.rearrange("(t p) r -> p t r", p=P)).then_inc(s["tables_loaded"], 16)
                act.dma_start(gq_b, row_bcast(g_qh)).then_inc(s["tables_loaded"], 16)
                act.dma_start(gk_b, row_bcast(g_kh)).then_inc(s["tables_loaded"], 16)
                act.dma_start(sgv[:, 0:SG], row_bcast(sg_ln_g)).then_inc(s["tables_loaded"], 16)
                act.dma_start(sgv[:, SG:], row_bcast(sg_ln_b)).then_inc(s["tables_loaded"], 16)
                act.dma_start(wuq, w_uq.rearrange("(k p) n -> p k n", p=P)).then_inc(s["wu_loaded"], 16)
                act.dma_start(wukv, w_ukv.rearrange("(k p) n -> p k n", p=P)).then_inc(s["wu_loaded"], 16)

                def rms(dst, src, n, done):
                    act.activation(dst, src, ACT.Sqrt, bias=eps[:, :], scale=1.0 / n).then_inc(s[done], 1)

                def x_square(t):
                    act.wait_ge(s["x_loaded%d" % (t % 2)], 16 * (t // 2 + 1))
                    link(act, "x_square", act.activation(sq.bitcast(bf16)[:, 0:1024], xt[t % 2], ACT.Square,
                                                         accum_out=stat[:, t:t + 1]))
                    rms(stat[:, 8 + t:9 + t], stat[:, t:t + 1], D, "x_rms")

                def z_out(t, c):
                    act.wait_ge(s["z_psum"], 3 * t + c + 1)
                    act.wait_ge(s["x_rstd"], t + 1)
                    if t >= 2 and c == 0:
                        act.wait_ge(s["zg"], t - 1)
                        act.wait_ge(s["k_scaled"], t - 1)
                        act.wait_ge(s["zs_stored%d" % (t % 2)], 16 * (t // 2))
                    act.activation(z[t % 2][:, c * ZC:(c + 1) * ZC], zp[c], ACT.Copy,
                                   scale=stat[:, 8 + t:9 + t]).then_inc(s["z"], 1)

                def heads(t):
                    zt = z[t % 2]
                    act.wait_ge(s["q_psum"], t + 1)
                    act.activation(sq.rearrange("p (b n) -> p b n", b=2), qp, ACT.Square).then_inc(s["q_square"], 1)
                    act.wait_ge(s["kv_psum"], t + 1)
                    for b, bank in ((0, 7), (1, 0)):
                        kv = PS[:, bank, :].rearrange("p (h c) -> p h c", c=NOPE + VD)
                        act.activation(V[:, t, :].rearrange("p (h c) -> p h c", h=H)[:, 4 * b:4 * b + 4, :],
                                       kv[:, :, NOPE:], ACT.Copy).then_inc(s["v"], 1)
                    act.wait_ge(s["q_stat"], t + 1)
                    rms(stat[:, 56:64], stat[:, 48:56], QK, "q_rms")
                    for b, bank in ((0, 7), (1, 0)):
                        kv = PS[:, bank, :].rearrange("p (h c) -> p h c", c=NOPE + VD)
                        act.activation(sq[:, 0:512].rearrange("p (h c) -> p h c", h=H)[:, 4 * b:4 * b + 4, :],
                                       kv[:, :, 0:NOPE], ACT.Square)
                    act.activation(sq[:, 512:512 + ROPE], zt[:, O_KR:O_SG], ACT.Square).then_inc(s["k_square"], 1)
                    act.wait_ge(s["k_stat"], t + 1)
                    rms(stat[:, 72:80], stat[:, 64:72], QK, "k_rms")

                def t_out(t, psum, ready, dst, done):
                    act.wait_ge(s[ready], t + 1)
                    act.activation(dst[0:QK, :, t * P:(t + 1) * P], tA[0:QK, :].rearrange("p (h c) -> p h c", h=H),
                                   ACT.Copy).then_inc(s[done], 1)

                act.wait_ge(s["pool"], 1)
                x_square(0)
                for c in range(3):
                    z_out(0, c)
                x_square(1)
                for t in range(NT):
                    zt = z[t % 2]
                    if t >= 1:
                        act.wait_ge(s["k_stat"], t)
                    act.activation(sq[:, 0:RQ], zt[:, 0:RQ], ACT.Square, accum_out=stat[:, 16 + t:17 + t])
                    link(act, "c_square", act.activation(sq[:, RQ:O_KR], zt[:, RQ:O_KR], ACT.Square,
                                                         accum_out=stat[:, 24 + t:25 + t]))
                    act.activation(stat[:, 32:33], stat[:, 16 + t:17 + t], ACT.Sqrt, bias=eps[:, :], scale=1.0 / RQ)
                    rms(stat[:, 33:34], stat[:, 24 + t:25 + t], RKV, "c_rms")
                    if t + 2 < NT:
                        x_square(t + 2)
                    if t >= 1:
                        t_out(t - 1, tA, "kT_psum", KT, "kT")
                    if t + 1 < NT:
                        z_out(t + 1, 0)
                        z_out(t + 1, 1)
                    heads(t)
                    if t + 1 < NT:
                        z_out(t + 1, 2)
                    t_out(t, tA, "qT_psum", QT, "qT")
                t_out(NT - 1, tA, "kT_psum", KT, "kT")

            @block.vector
            def _(dve):
                dve.wait_ge(s["rows_psum"], 1)
                link(dve, "vecs", dve.tensor_copy(vecs[:, :], PS[:, 7, 0:NROWS]))

                def x_out(t):
                    dve.wait_ge(s["x_rms"], t + 1)
                    dve.reciprocal(stat[:, 8 + t:9 + t], stat[:, 8 + t:9 + t]).then_inc(s["x_rstd"], 1)
                    dve.wait_ge(s["x_psum"], t + 1)
                    if t >= 2:
                        dve.wait_ge(s["z_psum"], 3 * (t - 1))
                    dve.tensor_tensor(xT[t % 2].rearrange("p (k c) -> p k c", k=KD), tA.rearrange("p (k c) -> p k c", k=KD),
                                      vec("ln1").unsqueeze(2).broadcast_to((P, KD, P)), ALU.mult).then_inc(s["xT"], 1)

                x_out(0)
                x_out(1)
                for t in range(NT):
                    zt = z[t % 2]
                    dve.wait_ge(s["c_rms"], t + 1)
                    link(dve, "dve", dve.reciprocal(stat[:, 34:36], stat[:, 32:34]))
                    dve.tensor_scalar(zt[:, 0:RQ], zt[:, 0:RQ], stat[:, 34:35], None, ALU.mult)
                    dve.tensor_scalar(zt[:, RQ:O_KR], zt[:, RQ:O_KR], stat[:, 35:36], None, ALU.mult).then_inc(s["c"], 1)
                    dve.wait_ge(s["c_psum"], t + 1)
                    gains = vecs[:, ROWS["g_cq"][0]:ROWS["g_cq"][0] + 5].unsqueeze(2).broadcast_to((P, 5, P))
                    dve.tensor_tensor(cT.rearrange("p (k c) -> p k c", k=5), tB[:, 0:640].rearrange("p (k c) -> p k c", k=5),
                                      gains, ALU.mult).then_inc(s["cT"], 1)
                    if t + 2 < NT:
                        x_out(t + 2)
                    dve.wait_ge(s["q_square"], t + 1)
                    ssq, rq = stat[:, 48:56], stat[:, 56:64]
                    dve.tensor_reduce(ssq, sq.rearrange("p (h c) -> p h c", h=H), AX.X, ALU.add).then_inc(s["q_stat"], 1)
                    dve.wait_ge(s["q_rms"], t + 1)
                    link(dve, "dve", dve.reciprocal(rq, rq))
                    if t >= 1:
                        dve.wait_ge(s["qT_psum"], t)
                    dve.tensor_tensor(qn.rearrange("p (b h) c -> p b h c", b=2), qp.rearrange("p b (h c) -> p b h c", c=QK),
                                      rq.rearrange("p (b h) -> p b h", b=2).unsqueeze(3).broadcast_to((P, 2, 4, QK)), ALU.mult).then_inc(s["q_scaled"], 1)
                    dve.wait_ge(s["k_square"], t + 1)
                    ssk, rk, sskr = stat[:, 64:72], stat[:, 72:80], stat[:, 80:81]
                    dve.tensor_reduce(ssk, sq[:, 0:512].rearrange("p (h c) -> p h c", h=H), AX.X, ALU.add)
                    link(dve, "dve", dve.tensor_reduce(sskr, sq[:, 512:512 + ROPE], AX.X, ALU.add))
                    dve.tensor_scalar(ssk, ssk, sskr, None, ALU.add).then_inc(s["k_stat"], 1)
                    dve.wait_ge(s["k_rms"], t + 1)
                    link(dve, "dve", dve.reciprocal(rk, rk))
                    if t >= 1:
                        dve.wait_ge(s["kT_psum"], t)
                    for b, bank in ((0, 7), (1, 0)):
                        dve.tensor_tensor(kn[:, 4 * b:4 * b + 4, 0:NOPE], PS[:, bank, :].rearrange("p (h c) -> p h c", h=4)[:, :, 0:NOPE],
                                          rk[:, 4 * b:4 * b + 4].unsqueeze(2).broadcast_to((P, 4, NOPE)), ALU.mult)
                    dve.tensor_tensor(kn[:, :, NOPE:], zt[:, O_KR:O_SG].unsqueeze(1).broadcast_to((P, H, ROPE)),
                                      rk.unsqueeze(2).broadcast_to((P, H, ROPE)), ALU.mult).then_inc(s["k_scaled"], 1)

            @block.tensor
            def _(pe):
                pe.wait_ge(s["ident"], 1)
                pe.wait_ge(s["rows_loaded"], 16 * 7)
                pe.transpose(PS[:, 7, 0:NROWS], rows_sb[0:NROWS, :], ident[0:NROWS, 0:NROWS]).then_inc(s["rows_psum"], 1)

                def x_in(t):
                    pe.wait_ge(s["x_loaded%d" % (t % 2)], 16 * (t // 2 + 1))
                    if t == 1:
                        pe.wait_ge(s["xT"], 1)
                    if t >= 3:
                        pe.wait_ge(s["kT"], t - 2)
                    if t == 2:
                        pe.wait_ge(s["xT"], 2)
                    for k in range(KD):
                        last = pe.transpose(tA[:, k * P:(k + 1) * P], xt[t % 2][:, k * P:(k + 1) * P], ident[:, :])
                    last.then_inc(s["x_psum"], 1)

                def z_mm(t, c):
                    if c == 0:
                        pe.wait_ge(s["xT"], t + 1)
                        if t >= 2:
                            pe.wait_ge(s["v"], 2 * (t - 1))
                            pe.wait_ge(s["k_scaled"], t - 1)
                    if t >= 1:
                        pe.wait_ge(s["z"], 3 * (t - 1) + c + 1)
                    for k in range(KD):
                        if t == 0 and c == 0:
                            pe.wait_ge(s["win_loaded"], 16 * KD) if k == 0 else None
                        last = pe.matmul(zp[c], xT[t % 2][:, k * P:(k + 1) * P], win[:, k, c * ZC:(c + 1) * ZC],
                                         start=k == 0, stop=k == KD - 1)
                    last.then_inc(s["z_psum"], 1)

                def head_T(t, src, ready, psum):
                    pe.wait_ge(s[ready], t + 1)
                    for h in range(H):
                        last = pe.transpose(tA[0:QK, h * P:(h + 1) * P], src[:, h, :], ident[:, :])
                    last.then_inc(s[psum], 1)

                x_in(0)
                x_in(1)
                for c in range(3):
                    z_mm(0, c)
                for t in range(NT):
                    zt = z[t % 2]
                    if t + 1 < NT:
                        z_mm(t + 1, 0)
                    if t >= 1:
                        pe.wait_ge(s["qT"], t)
                        head_T(t - 1, kn, "kn", "kT_psum")
                    pe.wait_ge(s["c"], t + 1)
                    if t >= 1:
                        pe.wait_ge(s["q_scaled"], t)
                    for k in range(5):
                        last = pe.transpose(tB[:, k * P:(k + 1) * P], zt[:, k * P:(k + 1) * P], ident[:, :])
                    last.then_inc(s["c_psum"], 1)
                    if t + 1 < NT:
                        z_mm(t + 1, 1)
                    if t + 2 < NT:
                        x_in(t + 2)
                    pe.wait_ge(s["cT"], t + 1)
                    if t == 0:
                        pe.wait_ge(s["wu_loaded"], 32)
                    for c in range(2):
                        for k in range(3):
                            last = pe.matmul(PS[:, 5 + c, 0:384], cT[:, k * P:(k + 1) * P], wuq[:, k, c * 384:(c + 1) * 384],
                                             start=k == 0, stop=k == 2)
                    last.then_inc(s["q_psum"], 1)
                    if t == 0:
                        pe.wait_ge(s["vecs"], 1)
                    if t >= 1:
                        pe.wait_ge(s["v"], 2 * t)
                        pe.wait_ge(s["k_scaled"], t)
                    pe.wait_ge(s["z"], 3 * (t + 1) + 1 if t + 1 < NT else 3 * NT)
                    for b, bank in ((0, 7), (1, 0)):
                        for k in range(2):
                            last = pe.matmul(PS[:, bank, :], cT[:, (3 + k) * P:(4 + k) * P], wukv[:, k, b * 512:(b + 1) * 512],
                                             start=k == 0, stop=k == 1)
                    last.then_inc(s["kv_psum"], 1)
                    if t + 1 < NT:
                        z_mm(t + 1, 2)
                    pe.wait_ge(s["xT"], min(t + 3, NT))
                    head_T(t, qn, "qn", "qT_psum")
                pe.wait_ge(s["qT"], NT)
                head_T(NT - 1, kn, "kn", "kT_psum")

        O = R3[:, 0:4096].rearrange("p (t c) -> p t c", t=NT)
        Pb = [R2[:, 0:1024], R2[:, 1024:2048]]
        PTb = [R2[:, 2048:3072], R2[:, 3072:4096]]
        SBn = R2[:, 4096:6144].rearrange("p (g q c) -> p g q c", g=G, q=LC)
        prod = [R2[:, 6144:8192], R2[:, 8192:10176]]
        r1 = [0]

        def in1(n):
            r1[0] += n
            return R1[:, r1[0] - n:r1[0]]
        Ec = in1(G * NC).rearrange("p (g k) -> p g k", g=G)
        Es = in1(G * NC).rearrange("p (g k) -> p g k", g=G)
        LL1 = in1(G * 9 * C).rearrange("p (g j c) -> p g j c", g=G, j=9)
        LL2 = in1(G * 9 * C).rearrange("p (g j c) -> p g j c", g=G, j=9)
        Bb = in1(G * C).rearrange("p (g c) -> p g c", g=G)
        BY = in1(G * C).rearrange("p (g c) -> p g c", g=G)
        Xb = in1(G * C).rearrange("p (g c) -> p g c", g=G)
        Yb = in1(G * C).rearrange("p (g c) -> p g c", g=G)
        CX = in1(G * C).rearrange("p (g c) -> p g c", g=G)
        CY = in1(G * C).rearrange("p (g c) -> p g c", g=G)
        Pr = in1(9 * G).rearrange("p (j g) -> p j g", j=9)
        Pi = in1(9 * G).rearrange("p (j g) -> p j g", j=9)
        lam = in1(3 * G).rearrange("p (a g) -> p a g", a=3)
        sgn = in1(2)
        rows3 = in1(P)
        cnat = prod[1][:, 0:512].rearrange("p (a f n) -> p a f n", a=2, f=2)
        v16 = [0]

        def tiny():
            v16[0] += G
            return R1[:, r1[0] + v16[0] - G:r1[0] + v16[0]]
        t1, t2, t3, t4, dt, lr, li, mag = [tiny() for _ in range(8)]
        th, co, si, den, fr, fi, kk, rr = [tiny() for _ in range(8)]
        R8 = tiny()

        signals("b", ("s_psum", "nmax", "exp", "pt_psum", "ptd", "pta", "o_psum", "o", "par_loaded", "par_psum", "par",
                  "den", "rden", "tables", "pdve", "ppool", "sgn"))
        steps = [(h, i) for h in range(H) for i in range(NT)]

        def wide(n):
            return sum(1 for _, i in steps[:n] if i >= 4)

        with nc.Block() as block:
            @block.sync
            def _(sp):
                for a, v in enumerate((lam_re, lam_im, log_dt)):
                    for half in range(2):
                        sp.dma_start(rows3[a * G:(a + 1) * G, half * NS:(half + 1) * NS], v).then_inc(s["par_loaded"], 16)
                for a, (v, w) in enumerate(((ssm_c_re, ssm_c_im), (ssm_c_im, ssm_c_re))):
                    for half, c in ((0, v), (1, w)):
                        sp.dma_start(cnat[:, a, :, half * NS:(half + 1) * NS],
                                     c.rearrange("(f g) c n -> (g c) f n", f=2)).then_inc(s["par_loaded"], 16)
                for dst, v, w in ((Xb, ssm_b_re, ssm_b_im), (Yb, ssm_b_im, ssm_b_re)):
                    for half, c in ((0, v), (1, w)):
                        sp.dma_start(dst[half * NS:(half + 1) * NS, :, :], c.rearrange("g n c -> n g c")).then_inc(s["par_loaded"], 16)
                sp.wait_ge(s["par_loaded"], 16 * 14)

            @block.gpsimd
            def _(pool):
                def put(ins):
                    link(pool, "ppool", ins)

                def cmul(dr, di, ar, ai, br, bi, t1, t2, t3, t4):
                    pool.tensor_tensor(t1, ar, br, ALU.mult)
                    pool.tensor_tensor(t2, ai, bi, ALU.mult)
                    pool.tensor_tensor(t3, ar, bi, ALU.mult)
                    put(pool.tensor_tensor(t4, ai, br, ALU.mult))
                    pool.tensor_tensor(dr, t1, t2, ALU.subtract)
                    put(pool.tensor_tensor(di, t3, t4, ALU.add))

                def nearest(dst, src, factor):
                    put(pool.tensor_scalar(dst, src, factor, 12582912.0, ALU.mult, ALU.add))
                    put(pool.tensor_scalar(dst, dst, -12582912.0, None, ALU.add))

                def less(dst, src, k, parts, t):
                    for n, c in enumerate(parts):
                        put(pool.tensor_scalar(t, k, -c, None, ALU.mult))
                        put(pool.tensor_tensor(dst, src if n == 0 else dst, t, ALU.add))

                def poly(dst, v, coefs):
                    put(pool.tensor_scalar(dst, v, coefs[-1], coefs[-2], ALU.mult, ALU.add))
                    for c in coefs[-3::-1]:
                        put(pool.tensor_tensor(dst, dst, v, ALU.mult))
                        put(pool.tensor_scalar(dst, dst, c, None, ALU.add))

                def exp(dst, src, k, t, r):
                    put(pool.tensor_scalar(dst, src, -87.0, 88.0, ALU.max, ALU.min))
                    nearest(k, dst, 1 / math.log(2))
                    less(r, dst, k, (0.693359375, math.log(2) - 0.693359375), t)
                    poly(dst, r, [1 / math.factorial(n) for n in range(9)])
                    put(pool.tensor_scalar(t.bitcast(i32), k, 127.0, float(1 << 23), ALU.add, ALU.mult))
                    put(pool.tensor_tensor(dst, dst, t, ALU.mult))

                pool.wait_ge(s["par_loaded"], 16 * 14)
                put(pool.memset(sgn[0:NS, 0:1], 1.0))
                put(pool.memset(sgn[NS:P, 0:1], -1.0))
                put(pool.memset(sgn[0:NS, 1:2], -1.0))
                pool.memset(Pr[:, 0, :], 1.0)
                pool.memset(Pi[:, 0, :], 0.0)
                pool.memset(Ec[:, :, 0:1], 1.0)
                put(pool.memset(Es[:, :, 0:1], 0.0))
                link(pool, "sgn", pool.memset(sgn[NS:P, 1:2], 1.0))
                pool.wait_ge(s["par"], 1)
                exp(dt, lam[:, 2, :], kk, t1, rr)
                put(pool.tensor_scalar(lr, lam[:, 0, :], -1e-4, None, ALU.min))
                put(pool.tensor_copy(li, lam[:, 1, :]))
                put(pool.tensor_tensor(t2, lr, dt, ALU.mult))
                exp(mag, t2, kk, t1, rr)
                put(pool.tensor_tensor(th, li, dt, ALU.mult))
                nearest(kk, th, 1 / (2 * math.pi))
                c1 = 6.28125
                c2 = float(np.float32(round((2 * math.pi - c1) * 2 ** 20) / 2 ** 20))
                less(rr, th, kk, (c1, c2, 2 * math.pi - c1 - c2), t1)
                put(pool.tensor_scalar(rr, rr, 0.25, None, ALU.mult))
                put(pool.tensor_tensor(t2, rr, rr, ALU.mult))
                poly(co, t2, [(-1) ** n / math.factorial(2 * n) for n in range(7)])
                poly(si, t2, [(-1) ** n / math.factorial(2 * n + 1) for n in range(7)])
                put(pool.tensor_tensor(si, si, rr, ALU.mult))

                def double():
                    put(pool.tensor_tensor(t1, si, co, ALU.mult))
                    put(pool.tensor_tensor(t2, si, si, ALU.mult))
                    pool.tensor_scalar(si, t1, 2.0, None, ALU.mult)
                    put(pool.tensor_scalar(co, t2, -2.0, 1.0, ALU.mult, ALU.add))
                double()
                double()
                pool.tensor_tensor(Pr[:, 1, :], mag, co, ALU.mult)
                put(pool.tensor_tensor(Pi[:, 1, :], mag, si, ALU.mult))
                for m in (1, 2, 4):
                    q4 = [prod[0][:, n * 64:n * 64 + m * G].rearrange("p (j g) -> p j g", j=m) for n in range(4)]
                    br, bi = [v[:, m:m + 1, :].broadcast_to((P, m, G)) for v in (Pr, Pi)]
                    cmul(Pr[:, m + 1:2 * m + 1, :], Pi[:, m + 1:2 * m + 1, :], Pr[:, 1:m + 1, :], Pi[:, 1:m + 1, :], br, bi, *q4)
                pool.tensor_tensor(t1, lr, lr, ALU.mult)
                put(pool.tensor_tensor(t2, li, li, ALU.mult))
                pool.tensor_tensor(den, t1, t2, ALU.add).then_inc(s["den"], 1)
                pool.wait_ge(s["rden"], 1)
                put(pool.tensor_scalar(t3, Pr[:, 1, :], -1.0, None, ALU.add))
                put(pool.tensor_scalar(t4, li, -1.0, None, ALU.mult))
                cmul(fr, fi, t3, Pi[:, 1, :], lr, t4, t1, t2, dt, rr)
                pool.tensor_tensor(fr, fr, den, ALU.mult)
                put(pool.tensor_tensor(fi, fi, den, ALU.mult))
                put(pool.tensor_tensor(Yb, Yb, sgn[:, 1:2].unsqueeze(2).broadcast_to((P, G, C)), ALU.mult))
                frb, fib = [v.unsqueeze(2).broadcast_to((P, G, C)) for v in (fr, fi)]
                q4 = [prod[0][:, n * 256:(n + 1) * 256].rearrange("p (g c) -> p g c", g=G) for n in range(4)]
                pool.tensor_tensor(q4[0], frb, Xb, ALU.mult)
                pool.tensor_tensor(q4[1], fib, Yb, ALU.mult)
                pool.tensor_tensor(q4[2], frb, Yb, ALU.mult)
                put(pool.tensor_tensor(q4[3], fib, Xb, ALU.mult))
                pool.tensor_tensor(Bb, q4[0], q4[1], ALU.add)
                put(pool.tensor_tensor(BY, q4[2], q4[3], ALU.subtract))

                def over(v, n, lo=0):
                    return v[:, lo:lo + n, :].rearrange("p j g -> p g j").unsqueeze(3).broadcast_to((P, G, n, C))

                def along(v, n):
                    return v.unsqueeze(2).broadcast_to((P, G, n, C))

                def mix(dst, v, w, op, lo, n, half):
                    g0, g1 = half * G // 2, (half + 1) * G // 2
                    q = [prod[0][:, a * 1024:a * 1024 + (G // 2) * n * C].rearrange("p (g j c) -> p g j c", g=G // 2, j=n) for a in range(2)]
                    pool.tensor_tensor(q[0], over(Pr, n, lo)[:, g0:g1], along(v, n)[:, g0:g1], ALU.mult)
                    put(pool.tensor_tensor(q[1], over(Pi, n, lo)[:, g0:g1], along(w, n)[:, g0:g1], ALU.mult))
                    put(pool.tensor_tensor(dst[:, g0:g1, lo:lo + n, :], q[0], q[1], op))
                for half in range(2):
                    mix(SBn, Bb, BY, ALU.add, 0, LC, half)
                    for lo, n in ((0, 8), (8, 1)):
                        mix(LL1, CX, CY, ALU.add, lo, n, half)
                        mix(LL2, CY, CX, ALU.subtract, lo, n, half)
                for _ in range(3):
                    double()
                put(pool.tensor_tensor(R8, mag, mag, ALU.mult))
                put(pool.tensor_tensor(R8, R8, R8, ALU.mult))
                put(pool.tensor_tensor(R8, R8, R8, ALU.mult))
                for m in (1, 2, 4, 8, 16, 32, 64):
                    n = min(m, 16)
                    for at in range(0, m, n):
                        q4 = [prod[0][:, a * 256:a * 256 + n * G].rearrange("p (g k) -> p g k", g=G) for a in range(4)]
                        br, bi = [v.unsqueeze(2).broadcast_to((P, G, n)) for v in (co, si)]
                        cmul(Ec[:, :, m + at:m + at + n], Es[:, :, m + at:m + at + n], Ec[:, :, at:at + n], Es[:, :, at:at + n], br, bi, *q4)
                    if m < 64:
                        double()

            @block.scalar
            def _(act):
                for n, (h, i) in enumerate(steps + [(0, 0)]):
                    if n < len(steps):
                        w = (i + 1) * P
                        act.wait_ge(s["nmax"], n + 1)
                        if n >= 2:
                            act.wait_ge(s["pt_psum"], n - 1)
                        act.activation(Pb[n % 2][:, 0:w], PS[:, 2 * (n % 2):2 * (n % 2) + 2, :].rearrange("p b n -> p (b n)")[:, 0:w],
                                       ACT.Exp, bias=stat[:, n % 4:n % 4 + 1], accum_out=stat[:, 4 + n % 4:5 + n % 4]).then_inc(s["exp"], 1)
                    if n >= 1:
                        i = steps[n - 1][1]
                        act.wait_ge(s["pt_psum"], n)
                        if n >= 3:
                            act.wait_ge(s["o_psum"], n - 2)
                        if i >= 4:
                            act.activation(PTb[(n - 1) % 2][:, 512:(i + 1) * P], PS[:, 5, 0:(i - 3) * P], ACT.Copy).then_inc(s["pta"], 1)

            @block.vector
            def _(dve):
                dve.wait_ge(s["par_psum"], 1)
                dve.wait_ge(s["sgn"], 1)
                dve.tensor_copy(lam.rearrange("p a g -> p (a g)"), PS[:, 6, 0:3 * G])
                dve.tensor_scalar(CX.rearrange("p g c -> p (g c)"), PS[:, 6, 128:384], sgn[:, 0:1], None, ALU.mult)
                dve.tensor_scalar(CY.rearrange("p g c -> p (g c)"), PS[:, 7, 0:256], -1.0, None, ALU.mult).then_inc(s["par"], 1)
                for n in range(len(steps) + 2):
                    if n < len(steps):
                        h, i = steps[n]
                        sc = PS[:, 2 * (n % 2):2 * (n % 2) + 2, :].rearrange("p b n -> p (b n)")
                        dve.wait_ge(s["s_psum"], n + 1)
                        link(dve, "pdve", dve.tensor_tensor(sc[:, i * P:(i + 1) * P], sc[:, i * P:(i + 1) * P], tril, ALU.add))
                        dve.tensor_reduce(stat[:, n % 4:n % 4 + 1], sc[:, 0:(i + 1) * P], AX.X, ALU.max, negate=True).then_inc(s["nmax"], 1)
                    if 1 <= n <= len(steps):
                        i = steps[n - 1][1]
                        dve.wait_ge(s["pt_psum"], n)
                        if n >= 3:
                            dve.wait_ge(s["o_psum"], n - 2)
                        w = min(i + 1, 4) * P
                        dve.tensor_copy(PTb[(n - 1) % 2][:, 0:w], PS[:, 4, 0:w]).then_inc(s["ptd"], 1)
                    if n >= 2:
                        m = n - 2
                        h, i = steps[m]
                        rs = stat[:, 8 + m % 2:9 + m % 2]
                        link(dve, "pdve", dve.reciprocal(rs, stat[:, 4 + m % 4:5 + m % 4]))
                        dve.wait_ge(s["o_psum"], m + 1)
                        dve.tensor_scalar(O[:, i, h * VD:(h + 1) * VD], PS[:, 6 + m % 2, (h % 2) * VD:(h % 2 + 1) * VD],
                                          rs, None, ALU.mult).then_inc(s["o"], 1)
                    if n == 24:
                        dve.wait_ge(s["den"], 1)
                        dve.reciprocal(den, den).then_inc(s["rden"], 1)

            @block.tensor
            def _(pe):
                pe.wait_ge(s["par_loaded"], 16 * 14)
                pe.transpose(PS[:, 6, 0:3 * G], rows3[0:3 * G, :], ident[0:3 * G, 0:3 * G])
                for a in range(2):
                    for f in range(2):
                        last = pe.transpose(PS[:, 6 + a, (1 - a) * P + f * P:(2 - a) * P + f * P], cnat[:, a, f, :], ident[:, :])
                last.then_inc(s["par_psum"], 1)

                def scores(n):
                    h, i = steps[n]
                    sc = PS[:, 2 * (n % 2):2 * (n % 2) + 2, :].rearrange("p b n -> p (b n)")
                    if n >= 2:
                        pe.wait_ge(s["exp"], n - 1)
                    for at in range(0, (i + 1) * P, 512):
                        to = min(at + 512, (i + 1) * P)
                        last = pe.matmul(sc[:, at:to], QT[0:QK, h, i * P:(i + 1) * P], KT[0:QK, h, at:to], start=True, stop=True)
                    last.then_inc(s["s_psum"], 1)

                def flip(n):
                    h, i = steps[n]
                    pe.wait_ge(s["exp"], n + 1)
                    if n >= 1:
                        pe.wait_ge(s["ptd"], n)
                        if n >= 5:
                            pe.wait_ge(s["pta"], wide(n))
                    for j in range(i + 1):
                        last = pe.transpose(PS[:, 4 + j // 4, (j % 4) * P:(j % 4 + 1) * P], Pb[n % 2][:, j * P:(j + 1) * P], ident[:, :])
                    last.then_inc(s["pt_psum"], 1)

                def values(n):
                    h, i = steps[n]
                    pe.wait_ge(s["ptd"], n + 1)
                    if i >= 4:
                        pe.wait_ge(s["pta"], wide(n + 1))
                    if n == 0:
                        pe.wait_ge(s["par"], 1)
                    if n >= 2:
                        pe.wait_ge(s["o"], n - 1)
                    a = h // 2 * 2 * VD
                    for j in range(i + 1):
                        last = pe.matmul(PS[:, 6 + n % 2, 0:2 * VD], PTb[n % 2][:, j * P:(j + 1) * P], V[:, j, a:a + 2 * VD],
                                         start=j == 0, stop=j == i)
                    last.then_inc(s["o_psum"], 1)

                scores(0)
                for n in range(len(steps) + 1):
                    if n + 1 < len(steps):
                        scores(n + 1)
                    if n < len(steps):
                        flip(n)
                    if n >= 1:
                        values(n - 1)

        slot = [RQKV[:, n * 2048:(n + 1) * 2048] for n in range(10)]
        ZS = slot[0].rearrange("p (t c) -> p t c", t=NT)
        XT = slot[1].rearrange("p (f n) -> p f n", f=2)
        X = slot[2].rearrange("p (g k) -> p g k", g=G)
        TT = slot[3].rearrange("p (g n) -> p g n", g=G)
        ST = slot[4].rearrange("p (g n) -> p g n", g=G)
        SX = slot[5].rearrange("p (g n) -> p g n", g=G)
        M = slot[6].rearrange("p (g k) -> p g k", g=G)
        X1 = slot[7].rearrange("p (g k) -> p g k", g=G)
        X2 = slot[8].rearrange("p (g k) -> p g k", g=G)
        Kt = slot[9][0:C, :].rearrange("p (g n) -> p g n", g=G)
        Y = slot[0].rearrange("p (g k) -> p g k", g=G)
        GT = slot[1].rearrange("p (f n) -> p f n", f=2)
        SIG = slot[3].rearrange("p (f n) -> p f n", f=2)
        sT = slot[7].rearrange("p (f n) -> p f n", f=2)
        wsn = R2[:, 0:512].rearrange("p (g n) -> p g n", g=SGG)
        wsT = R2[:, 512:1024].rearrange("p (g n) -> p g n", g=SGG)
        wglu = R2[:, 1024:1536].rearrange("p (f n) -> p f n", f=2)
        keep = R2[:, 1536:1664]
        dT = R2[0:C, 1664:1680]
        dg = R2[0:C, 1680:1936].rearrange("p (g c) -> p g c", g=G)
        vst = R2[:, 1936:2000]
        tmp = R2[:, 6144:8192]
        vsq = R2[:, 8192:10176]
        u_ = ZG[:, :, 0:SG]
        signals("s", ("zs_loaded", "ws_loaded", "xt_psum", "xt0", "xt1", "sb_psum", "st_v", "st_a", "ws_psum", "wsT", "kt_psum",
                  "kt", "xs_stored", "x_loaded", "tt_loaded", "tt_zero", "gelu", "vvar", "vrms", "vn", "mix_psum", "mixed",
                  "s_psum", "m", "scan", "x1", "x2", "y_psum", "y", "ys_stored", "yt_loaded", "gt", "glu_psum", "sig", "st",
                  "dve", "pool", "keep", "vcent", "vgain"), "s")

        with nc.Block() as block:
            @block.sync
            def _(sp):
                sp.dma_start(ZS, zs_d.rearrange("(t p) c -> p t c", p=P)).then_inc(s["szs_loaded"], 16)
                sp.dma_start(wsn, sg_w.rearrange("g t s -> t g s")).then_inc(s["sws_loaded"], 16)
                sp.dma_start(wglu, w_glu.rearrange("(f p) n -> p f n", p=P)).then_inc(s["sws_loaded"], 16)
                sp.dma_start(dT, ssm_d.rearrange("g c -> c g"), allow_slow_non_contiguous=True).then_inc(s["sws_loaded"], 16)
                for f in range(2):
                    sp.wait_ge(s["sxt%d" % f], 1)
                    sp.dma_start(xs_d[f * P:(f + 1) * P].rearrange("c j k -> c (j k)"), XT[:, f, :]).then_inc(s["sxs_stored"], 16)
                sp.wait_ge(s["sxs_stored"], 32)
                xs_v = xs_d.rearrange("(g c) j k -> j c g k", c=C)
                for j in range(LC):
                    q = LC - 1 - j
                    sp.dma_start(X[q * C:(q + 1) * C, :, :], xs_v[j]).then_inc(s["sx_loaded"], 16)
                ys_v = ys_d.rearrange("(g c) j k -> j c g k", c=C)
                sp.wait_ge(s["sy"], 2)
                for j in range(LC):
                    sp.dma_start(ys_v[j], Y[j * C:(j + 1) * C, :, :]).then_inc(s["sys_stored"], 16)
                sp.wait_ge(s["sys_stored"], 16 * LC)
                sp.dma_start(GT, ys_d.rearrange("(f c) j k -> c f (j k)", f=2)).then_inc(s["syt_loaded"], 16)
                sp.wait_ge(s["syt_loaded"], 16)

            @block.gpsimd
            def _(pool):
                pool.memset(TT, 0.0).then_inc(s["stt_zero"], 1)
                link(pool, "spool", pool.memset(keep, 1.0))
                pool.affine_select(out=keep, in_=keep, compare_op=ALU.is_ge, fill=0.0, base=0,
                                   pattern=[[1, P]], channel_multiplier=-1).then_inc(s["skeep"], 1)
                v3 = ZG[:, :, SG:]
                pool.wait_ge(s["svcent"], 1)
                gb, bb = [sgv[:, a:a + SG].unsqueeze(1).broadcast_to((P, NT, SG)) for a in (0, SG)]
                link(pool, "spool", pool.tensor_tensor(v3, v3, gb, ALU.mult))
                pool.tensor_tensor(v3, v3, bb, ALU.add).then_inc(s["svn"], 1)
                pool.wait_ge(s["sscan"], G)
                pool.tensor_tensor(X2[:, 0:10, :], M[:, 0:10, :], Es[:, 0:10, :], ALU.mult).then_inc(s["sx2"], 1)

            @block.scalar
            def _(act):
                act.activation(ZG.rearrange("p t c -> p (t c)"), ZG.rearrange("p t c -> p (t c)"), ACT.Gelu_apprx_tanh).then_inc(s["sgelu"], 1)
                act.wait_ge(s["stt_zero"], 1)
                act.wait_ge(s["sxt_psum"], 2)
                act.activation(XT[:, 1, :].rearrange("p (j k) -> p k j", j=LC),
                               PS[:, 2:4, :].rearrange("p b (k j) -> p (b k) j", j=LC), ACT.Copy).then_inc(s["sxt1"], 1)
                for h in range(2):
                    act.wait_ge(s["ssb_psum"], h + 1)
                    act.activation(ST[:, h * 8:(h + 1) * 8, :], PS[:, 4 + 2 * h:6 + 2 * h, :].rearrange("p b (g n) -> p (b g) n", n=P),
                                   ACT.Copy).then_inc(s["sst_a"], 1)
                act.wait_ge(s["svvar"], 1)
                act.activation(vst[:, 32:64], vst[:, 0:32], ACT.Sqrt, bias=eps[:, :], scale=1.0 / 64).then_inc(s["svrms"], 1)
                act.wait_ge(s["skt"], 1)
                for j in range(LC):
                    r = (LC - 1 - j) * C
                    act.dma_start(TT[r:r + C, :, j * C:], Kt[:, :, 0:(LC - j) * C]).then_inc(s["stt_loaded"], 16)
                act.wait_ge(s["syt_loaded"], 16)
                act.activation(GT, GT, ACT.Gelu_apprx_tanh).then_inc(s["sgt"], 1)
                bg = vec("b_glu")
                for m in range(2):
                    act.wait_ge(s["sglu_psum"], m + 1)
                    act.activation(SIG[:, m, :].rearrange("p (b n) -> p b n", b=2), PS[:, 2 * m:2 * m + 2, :], ACT.Sigmoid,
                                   bias=bg[:, m:m + 1]).then_inc(s["ssig"], 1)
                act.wait_ge(s["stt_loaded"], 16 * LC)

            @block.vector
            def _(dve):
                dve.wait_ge(s["sxt_psum"], 1)
                dve.tensor_copy(XT[:, 0, :].rearrange("p (j k) -> p k j", j=LC),
                                PS[:, 0:2, :].rearrange("p b (k j) -> p (b k) j", j=LC)).then_inc(s["sxt0"], 1)
                for h in range(2):
                    dve.wait_ge(s["ssb_psum"], h + 1)
                    dve.wait_ge(s["sst_a"], h + 1)
                    t3 = PS[:, 4 + 2 * h:6 + 2 * h, :].rearrange("p b (g n) -> p (b g) n", n=P)
                    dve.tensor_copy(SX[:, h * 8:(h + 1) * 8, 0:NS], t3[:, :, NS:])
                    dve.tensor_scalar(SX[:, h * 8:(h + 1) * 8, NS:], t3[:, :, 0:NS], -1.0, None, ALU.mult).then_inc(s["sst_v"], 1)
                dve.wait_ge(s["sws_psum"], 1)
                dve.wait_ge(s["skeep"], 1)
                dve.tensor_tensor(wsT, PS[:, 0, :].rearrange("p (g n) -> p g n", g=SGG), keep.unsqueeze(1).broadcast_to((P, SGG, P)),
                                  ALU.mult).then_inc(s["swsT"], 1)
                dve.wait_ge(s["skt_psum"], 1)
                dve.tensor_copy(Kt.rearrange("p (b g) n -> p b (g n)", b=4), PS[0:C, 4:8, :])
                link(dve, "sdve", dve.tensor_tensor(dg, ident[0:C, 0:C].unsqueeze(1).broadcast_to((C, G, C)),
                                                    dT.unsqueeze(2).broadcast_to((C, G, C)), ALU.mult))
                dve.tensor_tensor(Kt[:, :, 0:C], Kt[:, :, 0:C], dg, ALU.add).then_inc(s["skt"], 1)
                v4 = ZG[:, :, SG:].rearrange("p t (g c) -> p t g c", g=SGG)
                mean, ss = vst[:, 32:64], vst[:, 0:32]

                def b4(v):
                    return v.rearrange("p (t g) -> p t g", t=NT).unsqueeze(3).broadcast_to((P, NT, SGG, 64))
                dve.wait_ge(s["sgelu"], 1)
                link(dve, "sdve", dve.tensor_reduce(mean.rearrange("p (t g) -> p t g", t=NT), v4, AX.X, ALU.add))
                link(dve, "sdve", dve.tensor_scalar(mean, mean, 1.0 / 64, None, ALU.mult))
                link(dve, "sdve", dve.tensor_tensor(v4, v4, b4(mean), ALU.subtract))
                for h in range(2):
                    sq4 = tmp[:, h * 1024:(h + 1) * 1024].rearrange("p (t g c) -> p t g c", t=4, g=SGG)
                    link(dve, "sdve", dve.tensor_tensor(sq4, v4[:, 4 * h:4 * h + 4], v4[:, 4 * h:4 * h + 4], ALU.mult))
                    link(dve, "sdve", dve.tensor_reduce(ss[:, 16 * h:16 * h + 16].rearrange("p (t g) -> p t g", t=4), sq4, AX.X, ALU.add))
                dve.tensor_scalar(ss, ss, 1.0, None, ALU.mult).then_inc(s["svvar"], 1)
                dve.wait_ge(s["svrms"], 1)
                link(dve, "sdve", dve.reciprocal(mean, mean))
                dve.tensor_tensor(v4, v4, b4(mean), ALU.mult).then_inc(s["svcent"], 1)
                t8 = tmp[:, 0:1024].rearrange("p (g k) -> p g k", g=8)
                for h in range(2):
                    b = (4, 0)[h]
                    dve.wait_ge(s["ss_psum"], h + 1)
                    dve.tensor_tensor(t8, PS[:, b + 2:b + 4, :].rearrange("p b (g k) -> p (b g) k", k=NC), Es[:, 8 * h:8 * h + 8, :], ALU.mult)
                    link(dve, "sdve", dve.tensor_tensor(M[:, 8 * h:8 * h + 8, :], PS[:, b:b + 2, :].rearrange("p b (g k) -> p (b g) k", k=NC),
                                                        Ec[:, 8 * h:8 * h + 8, :], ALU.mult))
                    link(dve, "sm", dve.tensor_tensor(M[:, 8 * h:8 * h + 8, :], M[:, 8 * h:8 * h + 8, :], t8, ALU.add))
                    for g in range(8 * h, 8 * h + 8):
                        ins = dve.tensor_tensor_scan(M[:, g, :], R8[:, g:g + 1].broadcast_to((P, NC)), M[:, g, :], 0.0, ALU.mult, ALU.add)
                        ins.then_inc(s["sscan"], 1)
                dve.wait_ge(s["sscan"], G)
                dve.tensor_tensor(X1, M, Ec, ALU.mult).then_inc(s["sx1"], 1)
                dve.tensor_tensor(X2[:, 10:, :], M[:, 10:, :], Es[:, 10:, :], ALU.mult).then_inc(s["sx1"], 1)
                for g in range(SGG):
                    dve.wait_ge(s["smix_psum"], g + 1)
                    ug = u_[:, :, g * 64:(g + 1) * 64]
                    dve.scalar_tensor_tensor(ug, PS[:, g, :].rearrange("p (t c) -> p t c", t=NT), vec("sg_b")[:, g:g + 1], ug,
                                             ALU.add, ALU.mult).then_inc(s["smixed"], 1)
                for h in range(2):
                    dve.wait_ge(s["sy_psum"], h + 1)
                    dve.tensor_copy(Y[:, 8 * h:8 * h + 8, :], PS[:, 4 + 2 * h:6 + 2 * h, :].rearrange("p b (g k) -> p (b g) k", k=NC)).then_inc(s["sy"], 1)
                for m in range(2):
                    dve.wait_ge(s["ssig"], m + 1)
                    dve.tensor_tensor(sT[:, m, :].rearrange("p (k j) -> p j k", j=LC), GT[:, m, :].rearrange("p (j k) -> p j k", j=LC),
                                      SIG[:, m, :].rearrange("p (j k) -> p j k", j=LC), ALU.mult).then_inc(s["sst"], 1)

            @block.tensor
            def _(pe):
                pe.wait_ge(s["szs_loaded"], 16)
                for f in range(2):
                    for t in range(NT):
                        last = pe.transpose(PS[:, 2 * f + t // 4, (t % 4) * P:(t % 4 + 1) * P], ZS[:, t, f * P:(f + 1) * P], ident[:, :])
                    last.then_inc(s["sxt_psum"], 1)
                for h in range(2):
                    for g in range(8 * h, 8 * h + 8):
                        last = pe.transpose(PS[:, 4 + g // 4, (g % 4) * P:(g % 4 + 1) * P], SBn[:, g].rearrange("p q c -> p (q c)"), ident[:, :])
                    last.then_inc(s["ssb_psum"], 1)
                pe.wait_ge(s["sws_loaded"], 48)
                pe.wait_ge(s["sxt0"], 1)
                for g in range(SGG):
                    last = pe.transpose(PS[:, 0, g * P:(g + 1) * P], wsn[:, g, :], ident[:, :])
                last.then_inc(s["sws_psum"], 1)
                pe.wait_ge(s["sst_v"], 2)
                pe.wait_ge(s["sst_a"], 2)
                for g in range(G):
                    last = pe.matmul(PS[0:C, 4 + g // 4, (g % 4) * P:(g % 4 + 1) * P], Bb[:, g, :], LL1[:, g, 0:LC, :].rearrange("p j c -> p (j c)"),
                                     start=True, stop=True)
                last.then_inc(s["skt_psum"], 1)
                pe.wait_ge(s["sx_loaded"], 16 * LC)
                pe.wait_ge(s["skt"], 1)

                def states(h):
                    b = (4, 0)[h]
                    for w, at in ((ST, b), (SX, b + 2)):
                        for g in range(8 * h, 8 * h + 8):
                            last = pe.matmul(PS[:, at + g % 8 // 4, (g % 4) * P:(g % 4 + 1) * P], w[:, g, :], X[:, g, :], start=True, stop=True)
                    last.then_inc(s["ss_psum"], 1)
                states(0)
                pe.wait_ge(s["swsT"], 1)
                pe.wait_ge(s["sxt1"], 1)
                states(1)
                pe.wait_ge(s["svn"], 1)
                pe.wait_ge(s["sm"], 2)
                for g in range(SGG):
                    last = pe.matmul(PS[:, g, :].rearrange("p (t c) -> p t c", t=NT), wsT[:, g, :], ZG[:, :, SG + g * 64:SG + (g + 1) * 64],
                                     start=True, stop=True)
                    last.then_inc(s["smix_psum"], 1)
                pe.wait_ge(s["stt_loaded"], 16 * LC)
                pe.wait_ge(s["sx1"], 2)
                pe.wait_ge(s["sx2"], 1)
                for g in range(G):
                    o_ = PS[:, 4 + g // 4, (g % 4) * P:(g % 4 + 1) * P]
                    pe.matmul(o_, TT[:, g, :], X[:, g, :], start=True, stop=False)
                    pe.matmul(o_[:, 1:], LL1[:, g, 1:, :].rearrange("p j c -> p (j c)"), X1[:, g, 0:NC - 1], start=False, stop=False)
                    last = pe.matmul(o_[:, 1:], LL2[:, g, 1:, :].rearrange("p j c -> p (j c)"), X2[:, g, 0:NC - 1], start=False, stop=True)
                    if g % 8 == 7:
                        last.then_inc(s["sy_psum"], 1)
                pe.wait_ge(s["sgt"], 1)
                pe.wait_ge(s["smixed"], SGG)
                for m in range(2):
                    for b in range(2):
                        for f in range(2):
                            last = pe.matmul(PS[:, 2 * m + b, :], wglu[:, f, m * P:(m + 1) * P], GT[:, f, b * 512:(b + 1) * 512],
                                             start=f == 0, stop=f == 1)
                    last.then_inc(s["sglu_psum"], 1)

        h = R2[:, 0:8192].rearrange("p (t c) -> p t c", t=NT)
        wout = R1[:, 0:8192].rearrange("p (k n) -> p k n", k=KD)
        hn = [R1[:, 8192:9216], R1[:, 9216:10240]]
        junk = R1[:, 10240:10752].bitcast(bf16)
        wr = R1[:, 10752:11040].rearrange("p (k n) -> p k n", k=KD)
        upper = R1[:, 11040:11168]
        ones = R1[:, 11168:11296]
        mixn = [slot[6][:, 0:1024], slot[6][:, 1024:2048]]
        mixT = [slot[8][:, 0:1024], slot[8][:, 1024:2048]]
        hnT = [slot[9][:, 0:1024], slot[9][:, 1024:2048]]
        ring = [RQKV[:, u * 6144:(u + 1) * 6144] for u in range(2)]
        w13r = [r[:, 0:4096].rearrange("p (k a n) -> p k a n", k=KD, a=2) for r in ring]
        w2r = [r[:, 4096:].rearrange("p (k n) -> p k n", k=2) for r in ring]
        sm2 = sb("sm2", [P, 740])
        c2_ = [0]

        def t2(n):
            c2_[0] += n
            return sm2[:, c2_[0] - n:c2_[0]]
        e_id, e_grp, e_base = t2(E), t2(E), t2(E)
        tokid = t2(2 * NT).rearrange("p (c t) -> p c t", c=2)
        rbias = t2(EG + E)
        lg = t2(8 + E)
        g8, v8 = t2(8), t2(8)
        gi, vi = t2(8).bitcast(u32), t2(8).bitcast(u32)
        gs, i12 = t2(1), t2(2)
        gm, em, o1, o2, mm, rk_, pr1, msum = [t2(E) for _ in range(8)]
        gdiff = t2(NT * EG).rearrange("p (t g) -> p t g", t=NT)
        vdiff = t2(NT)
        slots_f = t2(2 * NT).rearrange("p (t c) -> p t c", t=NT)
        gsum, wsum = t2(NT), t2(NT)
        from_, to_ = t2(E).bitcast(u32), t2(E).bitcast(u32)
        idf, idg = small[:, 1040:1072], t2(E)
        tokrow = small[:, 1072:1200]
        tab = small[:, 1200:1232].bitcast(i32)
        cnt, nov, cum = [small[:, a:a + E] for a in (1232, 1264, 1296)]
        ej, bj, jj = [small[:, a:a + OVER] for a in (1328, 1344, 1360)]
        signals("d", ("x_loaded", "w_loaded", "wr_loaded", "const", "tok_zero", "s_tr", "mix_ss", "mix_rms", "mixn", "mix_tr", "mixT", "h_psum",
                  "h", "h_ss", "h_rms", "h_rstd", "hn", "xf_stored0", "xf_stored1", "hn_tr", "hnT", "lg_psum", "lg", "mask", "rank_psum", "dest",
                  "tok_stored", "tok_loaded", "tok_tr", "idx", "gexp", "pool", "dve", "count", "scan_done", "tab", "msum", "w_ready", "zero"), "d")
        wa_loaded = [sem("w13_loaded%d" % u) for u in range(2)]
        wb_loaded = [sem("w2_loaded%d" % u) for u in range(2)]

        def load_w13(eng, e, u, expert=None):
            v1, v3 = (w1[e], w3[e]) if expert is None else expert[0:2]
            eng.dma_start(w13r[u][:, :, 0, :], v1.rearrange("(k p) n -> p k n", p=P)).then_inc(wa_loaded[u], 16)
            eng.dma_start(w13r[u][:, :, 1, :], v3.rearrange("(k p) n -> p k n", p=P)).then_inc(wa_loaded[u], 16)

        def load_w2(eng, e, u, expert=None):
            v2 = w2[e] if expert is None else expert[2]
            eng.dma_start(w2r[u], v2.rearrange("(k p) n -> p k n", p=P)).then_inc(wb_loaded[u], 16)

        with nc.Block() as block:
            @block.sync
            def _(sp):
                for t in range(NT):
                    sp.dma_start(h[:, t, :], x[t * P:(t + 1) * P, :]).then_inc(s["dx_loaded"], 16)
                for t in range(NT):
                    sp.wait_ge(s["dhn"], t + 1)
                    sp.dma_start(xf_d[t * P:(t + 1) * P, :], hn[t % 2]).then_inc(s["dxf_stored%d" % (t % 2)], 16)
                sp.wait_ge(s["dtok_zero"], 16)
                for u in range(2):
                    load_w13(sp, u, u)
                    load_w2(sp, u, u)
                sp.wait_ge(s["dtok_stored"], 16 * 2 * NT)
                sp.dma_start(tokrow[0:E, :], tok_d.rearrange("(e s) o -> e (s o)", e=E)[:, 0:P]).then_inc(s["dtok_loaded"], 16)
                sp.wait_ge(s["dtok_loaded"], 16)
                for u in range(2):
                    sp.wait_ge(s["dxf_stored%d" % u], 16 * (NT // 2))

            @block.gpsimd
            def _(pool):
                link(pool, "dzero", pool.iota(slot[0][:, 0:256], pattern=[[0, 2], [1, P]], base=2 * S, channel_multiplier=0,
                                              allow_small_or_imprecise_dtypes=True))
                pool.dma_start(tok_d.rearrange("(p n) o -> p (n o)", p=P), slot[0][:, 0:256]).then_inc(s["dtok_zero"], 16)
                pool.iota(e_id, pattern=[[1, E]], base=0, channel_multiplier=0, allow_small_or_imprecise_dtypes=True)
                pool.iota(e_grp, pattern=[[1, EG], [0, EPG]], base=0, channel_multiplier=0, allow_small_or_imprecise_dtypes=True)
                pool.iota(e_base, pattern=[[S, E]], base=0, channel_multiplier=0, allow_small_or_imprecise_dtypes=True)
                pool.iota(tokid, pattern=[[S, 2], [P, NT]], base=0, channel_multiplier=1, allow_small_or_imprecise_dtypes=True)
                pool.iota(jj, pattern=[[1, OVER]], base=0, channel_multiplier=0, allow_small_or_imprecise_dtypes=True)
                pool.memset(lg, NEG)
                pool.memset(msum, 0.0)
                link(pool, "dpool", pool.memset(upper, 1.0))
                pool.affine_select(out=upper, in_=upper, compare_op=ALU.is_gt, fill=0.0, base=0, pattern=[[1, P]], channel_multiplier=-1)
                pool.memset(ones, 1.0).then_inc(s["dconst"], 1)
                pool.wait_ge(s["dtok_zero"], 16)
                for t in range(NT):
                    for c in range(2):
                        pool.wait_ge(s["ddest"], t + 1)
                        pool.indirect_dma_start(tok_d, bass.IndirectOffsetOnAxis(ap=dest[:, t, c:c + 1], axis=0),
                                                tokid[:, c, t:t + 1], None).then_inc(s["dtok_stored"], 16)
                pool.wait_ge(s["dtok_stored"], 16 * 2 * NT)

            @block.scalar
            def _(act):
                for k in range(KD):
                    act.dma_start(wout[:, k, :], w_out[k * P:(k + 1) * P, :]).then_inc(s["dw_loaded"], 16)
                act.dma_start(wr[:, :, 0:EG], w_rg.rearrange("(k p) n -> p k n", p=P)).then_inc(s["dwr_loaded"], 16)
                act.dma_start(wr[:, :, EG:], w_rexp.rearrange("(k p) n -> p k n", p=P)).then_inc(s["dwr_loaded"], 16)
                act.dma_start(rbias[:, 0:EG], row_bcast(b_rg)).then_inc(s["dwr_loaded"], 16)
                act.dma_start(rbias[:, EG:], row_bcast(b_rexp)).then_inc(s["dwr_loaded"], 16)

                def mix_squares(t):
                    a = 3 * (t % 2)
                    act.activation(junk[:, 0:512], O[:, t, :], ACT.Square, accum_out=stat[:, a:a + 1])
                    act.activation(junk[:, 512:768], ZG[:, t, 0:SG], ACT.Square, accum_out=stat[:, a + 1:a + 2])
                    act.wait_ge(s["ds_tr"], t + 1)
                    link(act, "dmix_ss", act.activation(junk[:, 768:1024], PS[:, 2, 0:256], ACT.Square, accum_out=stat[:, a + 2:a + 3]))
                    act.activation(stat[:, 6 + a:7 + a], stat[:, a:a + 1], ACT.Sqrt, bias=eps, scale=1.0 / 512)
                    act.activation(stat[:, 7 + a:9 + a], stat[:, a + 1:a + 3], ACT.Sqrt, bias=eps, scale=1.0 / 256).then_inc(s["dmix_rms"], 1)

                mix_squares(0)
                for t in range(NT):
                    if t + 1 < NT:
                        act.wait_ge(s["dmixn"], t + 1)
                        mix_squares(t + 1)
                    act.wait_ge(s["dh"], t + 1)
                    link(act, "dh_ss", act.activation(junk, h[:, t, :], ACT.Square, accum_out=stat[:, 16:17]))
                    act.activation(stat[:, 17:18], stat[:, 16:17], ACT.Sqrt, bias=eps, scale=1.0 / D).then_inc(s["dh_rms"], 1)
                    act.wait_ge(s["dh_rstd"], t + 1)
                    if t >= 2:
                        act.wait_ge(s["dxf_stored%d" % (t % 2)], 16 * (t // 2))
                        act.wait_ge(s["dhn_tr"], t - 1)
                    act.activation(hn[t % 2], h[:, t, :], ACT.Copy, scale=stat[:, 18:19]).then_inc(s["dhn"], 1)
                act.wait_ge(s["dlg"], NT)
                act.activation(gdiff, gdiff, ACT.Exp)
                act.activation(vdiff, vdiff, ACT.Exp).then_inc(s["dgexp"], 1)

            @block.vector
            def _(dve):
                def lk(ins):
                    link(dve, "ddve", ins)

                def mix_norm(t):
                    a = 3 * (t % 2)
                    dve.wait_ge(s["dmix_rms"], t + 1)
                    lk(dve.reciprocal(stat[:, 20:23], stat[:, 6 + a:9 + a]))
                    if t >= 2:
                        dve.wait_ge(s["dmix_tr"], t - 1)
                    dve.tensor_scalar(mixn[t % 2][:, 0:512], O[:, t, :], stat[:, 20:21], None, ALU.mult)
                    dve.tensor_scalar(mixn[t % 2][:, 512:768], ZG[:, t, 0:SG], stat[:, 21:22], None, ALU.mult)
                    dve.tensor_scalar(mixn[t % 2][:, 768:1024], PS[:, 2, 0:256], stat[:, 22:23], None, ALU.mult).then_inc(s["dmixn"], 1)

                def mix_out(t):
                    dve.wait_ge(s["dmix_tr"], t + 1)
                    if t >= 2:
                        dve.wait_ge(s["dh_psum"], t - 1)
                    dve.tensor_tensor(mixT[t % 2].rearrange("p (k c) -> p k c", k=KD), PS[:, 0:2, :].rearrange("p b (k c) -> p (b k) c", c=P),
                                      vec("g_mix").unsqueeze(2).broadcast_to((P, KD, P)), ALU.mult).then_inc(s["dmixT"], 1)

                def route(t):
                    dve.wait_ge(s["dlg_psum"], t + 1)
                    if t == 0:
                        dve.wait_ge(s["dwr_loaded"], 64)
                        dve.wait_ge(s["dconst"], 1)
                    dve.tensor_tensor(lg[:, 0:EG], PS[:, 7, 0:EG], rbias[:, 0:EG], ALU.add)
                    lk(dve.tensor_tensor(lg[:, 8:], PS[:, 7, EG:EG + E], rbias[:, EG:], ALU.add))
                    lk(dve.max(g8, lg[:, 0:8]))
                    dve.tensor_scalar(gdiff[:, t, :], lg[:, 0:EG], g8[:, 0:1], None, ALU.subtract)
                    lk(dve.max_index(gi, g8, lg[:, 0:8]))
                    lk(dve.tensor_copy(gs, gi[:, 0:1]))
                    lk(dve.tensor_scalar(gm, e_grp, gs, None, ALU.is_equal))
                    dve.tensor_tensor(em, lg[:, 8:], gm, ALU.mult)
                    lk(dve.tensor_scalar(pr1, gm, -1.0, -NEG, ALU.add, ALU.mult))
                    lk(dve.tensor_tensor(em, em, pr1, ALU.add))
                    lk(dve.max(v8, em))
                    dve.tensor_tensor(vdiff[:, t:t + 1], v8[:, 1:2], v8[:, 0:1], ALU.subtract).then_inc(s["dlg"], 1)
                    lk(dve.max_index(vi, v8, em))
                    lk(dve.tensor_copy(i12, vi[:, 0:2]))
                    dve.tensor_scalar(o1, e_id, i12[:, 0:1], None, ALU.is_equal)
                    lk(dve.tensor_scalar(o2, e_id, i12[:, 1:2], None, ALU.is_equal))
                    if t >= 1:
                        dve.wait_ge(s["drank_psum"], t)
                    link(dve, "dmask", dve.tensor_tensor(mm, o1, o2, ALU.add))

                def place(t):
                    dve.wait_ge(s["drank_psum"], t + 1)
                    lk(dve.tensor_tensor(rk_, PS[:, 2, 256:256 + E], e_base, ALU.add))
                    dve.tensor_tensor(o1, o1, rk_, ALU.mult)
                    lk(dve.tensor_tensor(o2, o2, rk_, ALU.mult))
                    dve.tensor_reduce(slots_f[:, t, 0:1], o1, AX.X, ALU.add)
                    lk(dve.tensor_reduce(slots_f[:, t, 1:2], o2, AX.X, ALU.add))
                    dve.tensor_copy(dest[:, t, :], slots_f[:, t, :]).then_inc(s["ddest"], 1)
                    link(dve, "dmsum", dve.tensor_tensor(msum, msum, mm, ALU.add))

                mix_norm(0)
                mix_out(0)
                dve.wait_ge(s["dx_loaded"], 16 * NT)
                for t in range(NT + 2):
                    if t + 1 < NT:
                        mix_norm(t + 1)
                    if t >= 2:
                        place(t - 2)
                    if t >= NT:
                        if t == NT:
                            route(NT - 1)
                        continue
                    dve.wait_ge(s["dh_psum"], t + 1)
                    dve.tensor_tensor(h[:, t, :].rearrange("p (b n) -> p b n", b=2), h[:, t, :].rearrange("p (b n) -> p b n", b=2),
                                      PS[:, 3:5, :], ALU.add).then_inc(s["dh"], 1)
                    dve.wait_ge(s["dh_rms"], t + 1)
                    if t >= 1:
                        dve.wait_ge(s["dhn"], t)
                    dve.reciprocal(stat[:, 18:19], stat[:, 17:18]).then_inc(s["dh_rstd"], 1)
                    if t + 1 < NT:
                        mix_out(t + 1)
                    dve.wait_ge(s["dhn_tr"], t + 1)
                    dve.tensor_tensor(hnT[t % 2].rearrange("p (k c) -> p k c", k=KD), PS[:, 5:7, :].rearrange("p b (k c) -> p (b k) c", c=P),
                                      vec("ln2").unsqueeze(2).broadcast_to((P, KD, P)), ALU.mult).then_inc(s["dhnT"], 1)
                    if t >= 1:
                        route(t - 1)
                dve.wait_ge(s["dgexp"], 1)
                lk(dve.tensor_reduce(gsum, gdiff, AX.X, ALU.add))
                lk(dve.tensor_scalar(wsum, vdiff, 1.0, None, ALU.add))
                lk(dve.tensor_tensor(gsum, gsum, wsum, ALU.mult))
                lk(dve.reciprocal(wts[:, :, 0], gsum))
                lk(dve.tensor_tensor(wts[:, :, 1], wts[:, :, 0], vdiff, ALU.mult))
                dve.wait_ge(s["dcount"], 1)
                lk(dve.tensor_copy(cnt, PS[:, 7, 128:128 + E]))
                lk(dve.tensor_scalar(nov, cnt, float(P), None, ALU.is_gt))
                for b in range(2, S // P):
                    lk(dve.scalar_tensor_tensor(nov, cnt, float(P * b), nov, ALU.is_gt, ALU.add))
                lk(dve.tensor_tensor_scan(cum, ones[:, 0:E], nov, 0.0, ALU.mult, ALU.add))
                big = junk.bitcast(fp32)[:, 0:OVER * E].rearrange("p (j e) -> p j e", e=E)
                cb = cum.unsqueeze(1).broadcast_to((P, OVER, E))
                lk(dve.tensor_tensor(big, cb, jj.unsqueeze(2).broadcast_to((P, OVER, E)), ALU.is_le))
                lk(dve.tensor_reduce(ej, big, AX.X, ALU.add))
                lk(dve.tensor_tensor(big, big, nov.unsqueeze(1).broadcast_to((P, OVER, E)), ALU.mult))
                lk(dve.tensor_reduce(bj, big, AX.X, ALU.add))
                lk(dve.tensor_tensor(bj, jj, bj, ALU.subtract))
                lk(dve.tensor_scalar(bj, bj, float(P), float(P), ALU.mult, ALU.add))
                lk(dve.tensor_scalar(ej, ej, float(E - 1), None, ALU.min))
                lk(dve.scalar_tensor_tensor(bj, ej, float(S), bj, ALU.mult, ALU.add))
                lk(dve.tensor_scalar(bj, bj, float(E * S - P), None, ALU.min))
                dve.tensor_copy(tab[:, 0:1], cum[:, E - 1:E])
                dve.tensor_copy(tab[:, 1:1 + OVER], ej)
                dve.tensor_copy(tab[:, 1 + OVER:1 + 2 * OVER], bj).then_inc(s["dtab"], 1)
                dve.wait_ge(s["dtok_tr"], 1)
                lk(dve.tensor_copy(idf, PS[:, 6, 0:E]))
                lk(dve.tensor_scalar(idg, idf, float(S), -float(S), ALU.is_ge, ALU.mult))
                lk(dve.tensor_tensor(idg, idg, idf, ALU.add))
                lk(dve.tensor_scalar(idg, idg, float(S - 1), None, ALU.min))
                dve.tensor_copy(from_, idg)
                dve.tensor_copy(to_, idf).then_inc(s["didx"], 1)

            @block.tensor
            def _(pe):
                sTv = sT

                def flip_s(t):
                    if t >= 1:
                        pe.wait_ge(s["dmixn"], t)
                    if t >= 4:
                        pe.wait_ge(s["ddest"], t - 3)
                    for f in range(2):
                        last = pe.transpose(PS[:, 2, f * P:(f + 1) * P], sTv[:, f, t * P:(t + 1) * P], ident[:, :])
                    last.then_inc(s["ds_tr"], 1)

                def flip_mix(t):
                    pe.wait_ge(s["dmixn"], t + 1)
                    if t >= 1:
                        pe.wait_ge(s["dmixT"], t)
                    for k in range(KD):
                        last = pe.transpose(PS[:, k // 4, (k % 4) * P:(k % 4 + 1) * P], mixn[t % 2][:, k * P:(k + 1) * P], ident[:, :])
                    last.then_inc(s["dmix_tr"], 1)

                def router(t):
                    pe.wait_ge(s["dhn"], t + 1)
                    if t >= 1:
                        pe.wait_ge(s["dhnT"], t)
                    for k in range(KD):
                        last = pe.transpose(PS[:, 5 + k // 4, (k % 4) * P:(k % 4 + 1) * P], hn[t % 2][:, k * P:(k + 1) * P], ident[:, :])
                    last.then_inc(s["dhn_tr"], 1)

                def logits(t):
                    pe.wait_ge(s["dhnT"], t + 1)
                    if t >= 1:
                        pe.wait_ge(s["dmask"], t)
                    for k in range(KD):
                        last = pe.matmul(PS[:, 7, 0:EG + E], hnT[t % 2][:, k * P:(k + 1) * P], wr[:, k, :], start=k == 0, stop=k == KD - 1)
                    last.then_inc(s["dlg_psum"], 1)

                def ranks(t):
                    pe.wait_ge(s["dmask"], t + 1)
                    if t >= 1:
                        pe.wait_ge(s["dmsum"], t)
                    pe.wait_ge(s["dmixn"], min(t + 4, NT))
                    pe.matmul(PS[:, 2, 256:256 + E], upper, mm, start=True, stop=False)
                    pe.matmul(PS[:, 2, 256:256 + E], ones, msum, start=False, stop=True).then_inc(s["drank_psum"], 1)

                flip_s(0)
                flip_mix(0)
                pe.wait_ge(s["dw_loaded"], 16 * KD)
                pe.wait_ge(s["dconst"], 1)
                pe.wait_ge(s["dwr_loaded"], 64)
                for t in range(NT + 2):
                    if t + 1 < NT:
                        flip_s(t + 1)
                    if t < NT:
                        pe.wait_ge(s["dmixT"], t + 1)
                        if t >= 1:
                            pe.wait_ge(s["dh"], t)
                        for b in range(2):
                            for k in range(KD):
                                last = pe.matmul(PS[:, 3 + b, :], mixT[t % 2][:, k * P:(k + 1) * P], wout[:, k, b * 512:(b + 1) * 512],
                                                 start=k == 0, stop=k == KD - 1)
                        last.then_inc(s["dh_psum"], 1)
                    if t >= 2:
                        ranks(t - 2)
                    if 1 <= t <= NT:
                        logits(t - 1)
                    if t + 1 < NT:
                        flip_mix(t + 1)
                    if t < NT:
                        router(t)
                pe.wait_ge(s["ddest"], NT)
                pe.wait_ge(s["dmsum"], NT)
                pe.matmul(PS[:, 7, 128:128 + E], ones, msum, start=True, stop=True).then_inc(s["dcount"], 1)
                pe.wait_ge(s["dtok_loaded"], 16)
                pe.wait_ge(s["dhnT"], NT)
                pe.transpose(PS[:, 6, 0:E], tokrow[0:E, :], ident[0:E, 0:E]).then_inc(s["dtok_tr"], 1)

        eo = [0]

        def ine(n):
            eo[0] += n
            return R1[:, eo[0] - n:eo[0]]
        xg, xgT, yb = [[ine(1024), ine(1024)] for _ in range(3)]
        act_, actT, sil = [[ine(F), ine(F)] for _ in range(3)]
        bpg = ine(D)
        wple = ine(2 * D).rearrange("p (k n) -> p k n", k=2)
        tokc, tokf = ine(1), ine(1)
        o_from, o_to = ine(1).bitcast(u32), ine(1).bitcast(u32)
        wpg = R3[:, :].rearrange("p (k n) -> p k n", k=KD)
        signals("e", ("xg_loaded0", "xg_loaded1", "xT_psum", "xgT", "up_psum", "silu", "act", "actT_psum", "actT", "y_psum", "yv", "ya",
                  "y_stored", "late_loaded"), "e")

        def ge(e, n):
            return not isinstance(e, int) or e >= n

        def lt(e, n):
            return not isinstance(e, int) or e < n

        def pairs(eng, step):
            for e in (0, 1):
                step(e, e, 0)
            with eng.Fori(1, E // 2 - 1) as i:
                for u in range(2):
                    step(i * 2 + u, u, i)
            for e in (E - 2, E - 1):
                step(e, e % 2, E // 2 - 1)

        with nc.Block() as block:
            @block.sync
            def _(sp):
                sp.dma_start(wpg, w_pg.rearrange("(k p) n -> p k n", p=P)).then_inc(s["elate_loaded"], 16)
                sp.dma_start(bpg, row_bcast(b_pg)).then_inc(s["elate_loaded"], 16)
                sp.dma_start(wple, w_ple.rearrange("(k p) n -> p k n", p=P)).then_inc(s["elate_loaded"], 16)

                def step(e, u, i):
                    if lt(e, E - 2):
                        sp.wait_ge(s["eup_psum"], e + 1)
                        load_w13(sp, e + 2, u)
                    if ge(e, 1) and lt(e, E - 1):
                        sp.wait_ge(s["ey_psum"], e)
                        load_w2(sp, e + 1, 1 - u)
                pairs(sp, step)
                sp.wait_ge(s["elate_loaded"], 48)

            @block.gpsimd
            def _(pool):
                for e in range(E + 2):
                    u = e % 2
                    if e < E:
                        if e >= 2:
                            pool.wait_ge(s["exT_psum"], e - 1)
                        pool.indirect_dma_start(xg[u], None, xf_d, bass.IndirectOffsetOnAxis(ap=from_[:, e:e + 1], axis=0)).then_inc(
                            s["exg_loaded%d" % u], 16)
                    if e >= 2:
                        pool.wait_ge(s["eyv"], e - 1)
                        pool.wait_ge(s["eya"], e - 1)
                        if e >= 3:
                            pool.wait_ge(s["ey_stored"], 16 * (e - 2))
                        pool.indirect_dma_start(y_d, bass.IndirectOffsetOnAxis(ap=to_[:, e - 2:e - 1], axis=0), yb[u], None,
                                                bounds_check=2 * S - 1, oob_is_err=False).then_inc(s["ey_stored"], 16)
                pool.wait_ge(s["ey_stored"], 16 * E)

            @block.scalar
            def _(act):
                def y_out(e, u, i):
                    act.wait_ge(s["ey_psum"], e + 1)
                    if ge(e, 2):
                        act.wait_ge(s["ey_stored"], e * 16 - 16)
                    act.activation(yb[u][:, 512:1024], PS[:, 6, :], ACT.Copy).then_inc(s["eya"], 1)

                def step(e, u, i):
                    act.wait_ge(s["eup_psum"], e + 1)
                    if ge(e, 2):
                        act.wait_ge(s["eact"], e - 1)
                    act.activation(sil[u], PS[:, 2 + u, 0:F], ACT.Silu).then_inc(s["esilu"], 1)
                    if ge(e, 1):
                        y_out(e - 1, 1 - u, i if u else i - 1)
                    act.wait_ge(s["eactT_psum"], e + 1)
                    act.activation(actT[u], PS[:, 4, 0:F], ACT.Copy).then_inc(s["eactT"], 1)
                pairs(act, step)
                y_out(E - 1, 1, E // 2 - 1)

            @block.vector
            def _(dve):
                def x_out(e, u, i):
                    dve.wait_ge(s["exT_psum"], e + 1)
                    if ge(e, 2):
                        dve.wait_ge(s["eup_psum"], e - 1)
                    dve.tensor_tensor(xgT[u].rearrange("p (k c) -> p k c", k=KD), PS[:, 0:2, :].rearrange("p b (k c) -> p (b k) c", c=P),
                                      vec("ln2").unsqueeze(2).broadcast_to((P, KD, P)), ALU.mult).then_inc(s["exgT"], 1)

                def y_out(e, u, i):
                    dve.wait_ge(s["ey_psum"], e + 1)
                    if ge(e, 2):
                        dve.wait_ge(s["ey_stored"], e * 16 - 16)
                    dve.tensor_copy(yb[u][:, 0:512], PS[:, 5, :]).then_inc(s["eyv"], 1)

                def step(e, u, i):
                    dve.wait_ge(s["esilu"], e + 1)
                    if ge(e, 2):
                        dve.wait_ge(s["eactT_psum"], e - 1)
                    dve.tensor_tensor(act_[u], sil[u], PS[:, 2 + u, F:2 * F], ALU.mult).then_inc(s["eact"], 1)
                    if lt(e, E - 1):
                        x_out(e + 1, 1 - u, i)
                    if ge(e, 1):
                        y_out(e - 1, 1 - u, i if u else i - 1)
                x_out(0, 0, 0)
                pairs(dve, step)
                y_out(E - 1, 1, E // 2 - 1)

            @block.tensor
            def _(pe):
                def flip_x(e, u, i):
                    pe.wait_ge(s["exg_loaded%d" % u], i * 16 + 16)
                    if ge(e, 1):
                        pe.wait_ge(s["exgT"], e)
                    for k in range(KD):
                        last = pe.transpose(PS[:, k // 4, (k % 4) * P:(k % 4 + 1) * P], xg[u][:, k * P:(k + 1) * P], ident[:, :])
                    last.then_inc(s["exT_psum"], 1)

                def down(e, u, i):
                    pe.wait_ge(s["eactT"], e + 1)
                    pe.wait_ge(wb_loaded[u], i * 16 + 16)
                    if ge(e, 1):
                        pe.wait_ge(s["eyv"], e)
                        pe.wait_ge(s["eya"], e)
                    for b in range(2):
                        for k in range(2):
                            last = pe.matmul(PS[:, 5 + b, :], actT[u][:, k * P:(k + 1) * P], w2r[u][:, k, b * 512:(b + 1) * 512],
                                             start=k == 0, stop=k == 1)
                    last.then_inc(s["ey_psum"], 1)

                def step(e, u, i):
                    pe.wait_ge(s["exgT"], e + 1)
                    pe.wait_ge(wa_loaded[u], i * 32 + 32)
                    if ge(e, 2):
                        pe.wait_ge(s["eact"], e - 1)
                    for k in range(KD):
                        last = pe.matmul(PS[:, 2 + u, :], xgT[u][:, k * P:(k + 1) * P], w13r[u][:, k, :, :].rearrange("p a n -> p (a n)"),
                                         start=k == 0, stop=k == KD - 1)
                    last.then_inc(s["eup_psum"], 1)
                    if lt(e, E - 1):
                        flip_x(e + 1, 1 - u, i + u)
                    if ge(e, 1):
                        down(e - 1, 1 - u, i if u else i - 1)
                    pe.wait_ge(s["eact"], e + 1)
                    if ge(e, 1):
                        pe.wait_ge(s["eactT"], e)
                    for k in range(2):
                        last = pe.transpose(PS[:, 4, k * P:(k + 1) * P], act_[u][:, k * P:(k + 1) * P], ident[:, :])
                    last.then_inc(s["eactT_psum"], 1)
                flip_x(0, 0, 0)
                pairs(pe, step)
                down(E - 1, 1, E // 2 - 1)

        signals("o", ("w_loaded", "tok_loaded", "idx", "x_loaded", "xT_psum", "xT", "up_psum", "silu", "act", "actT_psum", "actT", "y_psum", "y", "y_stored"), "o")
        ou = 0

        def few(eng, step):
            number = eng.value_load(tab[0:1, 0:1], min_val=0, max_val=OVER)
            for j in range(OVER):
                with eng.If(number > j):
                    step(j)

        def overflow(eng, step):
            number = eng.value_load(tab[0:1, 0:1], min_val=0, max_val=OVER)
            with eng.Fori(0, OVER) as j:
                with eng.If(number > j):
                    step(j)

        with nc.Block() as block:
            @block.sync
            def _(sp):
                w1v, w3v, w2v = [v.rearrange("e (k p) n -> e p k n", p=P) for v in (w1, w3, w2)]

                def step(j):
                    expert = sp.value_load(tab[0:1, j + 1:j + 2], min_val=0, max_val=E - 1)
                    base = sp.value_load(tab[0:1, j + 1 + OVER:j + 2 + OVER], min_val=0, max_val=E * S - P)
                    sp.dma_start(tokc, tok_d[bass.ds(base, P), :]).then_inc(s["otok_loaded"], 16)
                    for a, v in ((0, w1v), (1, w3v)):
                        sp.dma_start(w13r[ou][:, :, a, :], v[bass.ds(expert, 1)].rearrange("e p k n -> (e p) k n")).then_inc(s["ow_loaded"], 16)
                    sp.dma_start(w2r[ou], w2v[bass.ds(expert, 1)].rearrange("e p k n -> (e p) k n")).then_inc(s["ow_loaded"], 16)
                    sp.wait_ge(s["oy_stored"], j * 16 + 16)
                few(sp, step)

            @block.gpsimd
            def _(pool):
                def step(j):
                    pool.wait_ge(s["otok_loaded"], j * 16 + 16)
                    n = 5 * j
                    pool.tensor_scalar(tokf, tokc, float(S), -float(S), ALU.is_ge, ALU.mult).then_inc(s["oidx"], 1)
                    pool.wait_ge(s["oidx"], n + 1)
                    pool.tensor_tensor(tokf, tokf, tokc, ALU.add).then_inc(s["oidx"], 1)
                    pool.wait_ge(s["oidx"], n + 2)
                    pool.tensor_scalar(tokf, tokf, float(S - 1), None, ALU.min).then_inc(s["oidx"], 1)
                    pool.wait_ge(s["oidx"], n + 3)
                    pool.tensor_copy(o_from, tokf).then_inc(s["oidx"], 1)
                    pool.tensor_copy(o_to, tokc).then_inc(s["oidx"], 1)
                    pool.wait_ge(s["oidx"], n + 5)
                    pool.indirect_dma_start(xg[ou], None, xf_d, bass.IndirectOffsetOnAxis(ap=o_from, axis=0)).then_inc(s["ox_loaded"], 16)
                    pool.wait_ge(s["oy"], j + 1)
                    pool.indirect_dma_start(y_d, bass.IndirectOffsetOnAxis(ap=o_to, axis=0), yb[ou], None,
                                            bounds_check=2 * S - 1, oob_is_err=False).then_inc(s["oy_stored"], 16)
                    pool.wait_ge(s["oy_stored"], 16 * j + 16)
                few(pool, step)

            @block.scalar
            def _(act):
                def step(j):
                    act.wait_ge(s["oup_psum"], j + 1)
                    act.activation(sil[ou], PS[:, 2, 0:F], ACT.Silu).then_inc(s["osilu"], 1)
                    act.wait_ge(s["oactT_psum"], j + 1)
                    act.activation(actT[ou], PS[:, 4, 0:F], ACT.Copy).then_inc(s["oactT"], 1)
                overflow(act, step)

            @block.vector
            def _(dve):
                def step(j):
                    dve.wait_ge(s["oxT_psum"], j + 1)
                    dve.tensor_tensor(xgT[ou].rearrange("p (k c) -> p k c", k=KD), PS[:, 0:2, :].rearrange("p b (k c) -> p (b k) c", c=P),
                                      vec("ln2").unsqueeze(2).broadcast_to((P, KD, P)), ALU.mult).then_inc(s["oxT"], 1)
                    dve.wait_ge(s["osilu"], j + 1)
                    dve.tensor_tensor(act_[ou], sil[ou], PS[:, 2, F:2 * F], ALU.mult).then_inc(s["oact"], 1)
                    dve.wait_ge(s["oy_psum"], j + 1)
                    dve.tensor_copy(yb[ou].rearrange("p (b n) -> p b n", b=2), PS[:, 5:7, :]).then_inc(s["oy"], 1)
                overflow(dve, step)

            @block.tensor
            def _(pe):
                def step(j):
                    pe.wait_ge(s["ox_loaded"], j * 16 + 16)
                    for k in range(KD):
                        last = pe.transpose(PS[:, k // 4, (k % 4) * P:(k % 4 + 1) * P], xg[ou][:, k * P:(k + 1) * P], ident[:, :])
                    last.then_inc(s["oxT_psum"], 1)
                    pe.wait_ge(s["ow_loaded"], j * 48 + 48)
                    pe.wait_ge(s["oxT"], j + 1)
                    for k in range(KD):
                        last = pe.matmul(PS[:, 2, :], xgT[ou][:, k * P:(k + 1) * P], w13r[ou][:, k, :, :].rearrange("p a n -> p (a n)"),
                                         start=k == 0, stop=k == KD - 1)
                    last.then_inc(s["oup_psum"], 1)
                    pe.wait_ge(s["oact"], j + 1)
                    for k in range(2):
                        last = pe.transpose(PS[:, 4, k * P:(k + 1) * P], act_[ou][:, k * P:(k + 1) * P], ident[:, :])
                    last.then_inc(s["oactT_psum"], 1)
                    pe.wait_ge(s["oactT"], j + 1)
                    for b in range(2):
                        for k in range(2):
                            last = pe.matmul(PS[:, 5 + b, :], actT[ou][:, k * P:(k + 1) * P], w2r[ou][:, k, b * 512:(b + 1) * 512],
                                             start=k == 0, stop=k == 1)
                    last.then_inc(s["oy_psum"], 1)
                overflow(pe, step)

        fo = [0]

        def inf(n):
            fo[0] += n
            return RQKV[:, fo[0] - n:fo[0]]
        y1, y2, h2T, gate, prodf, outb = [[inf(D), inf(D)] for _ in range(6)]
        pt, pT = [[inf(PLE), inf(PLE)] for _ in range(2)]
        signals("f", ("p_loaded0", "p_loaded1", "y_loaded0", "y_loaded1", "h1", "h", "hT_psum", "hT", "pT_psum", "pT", "gate_psum", "gate", "sig",
                  "ple_psum", "prod", "out", "stored0", "stored1"), "f")
        with nc.Block() as block:
            @block.sync
            def _(sp):
                def load_y(t):
                    if t >= 2:
                        sp.wait_ge(s["fh"], t - 1)
                    for c, y_ in ((0, y1[t % 2]), (1, y2[t % 2])):
                        sp.dma_start(y_, y_d[c * S + t * P:c * S + (t + 1) * P, :]).then_inc(s["fy_loaded%d" % (t % 2)], 16)
                load_y(0)
                for t in range(NT + 1):
                    if t + 1 < NT:
                        load_y(t + 1)
                    if t < NT:
                        if t >= 2:
                            sp.wait_ge(s["fpT_psum"], t - 1)
                        sp.dma_start(pt[t % 2], p[t * P:(t + 1) * P, :]).then_inc(s["fp_loaded%d" % (t % 2)], 16)
                    if t >= 1:
                        sp.wait_ge(s["fout"], t)
                        sp.dma_start(out[(t - 1) * P:t * P, :], outb[(t - 1) % 2]).then_inc(s["fstored%d" % ((t - 1) % 2)], 16)
                for u in range(2):
                    sp.wait_ge(s["fstored%d" % u], 16 * (NT // 2))

            @block.scalar
            def _(act):
                def turned(t):
                    act.wait_ge(s["fhT_psum"], t + 1)
                    if t >= 2:
                        act.wait_ge(s["fgate_psum"], t - 1)
                    act.activation(h2T[t % 2].rearrange("p (b n) -> p b n", b=2), PS[:, 0:2, :], ACT.Copy).then_inc(s["fhT"], 1)
                    act.wait_ge(s["fpT_psum"], t + 1)
                    if t >= 2:
                        act.wait_ge(s["fple_psum"], t - 1)
                    act.activation(pT[t % 2], PS[:, 6, 0:PLE], ACT.Copy).then_inc(s["fpT"], 1)
                turned(0)
                for t in range(NT):
                    if t + 1 < NT:
                        turned(t + 1)
                    act.wait_ge(s["fgate"], t + 1)
                    act.activation(gate[t % 2], gate[t % 2], ACT.Sigmoid).then_inc(s["fsig"], 1)

            @block.vector
            def _(dve):
                def add_y(t):
                    u = t % 2
                    dve.wait_ge(s["fy_loaded%d" % u], 32 * (t // 2 + 1))
                    link(dve, "fh1", dve.scalar_tensor_tensor(h[:, t, :], y1[u], wts[:, t, 0:1], h[:, t, :], ALU.mult, ALU.add))
                    dve.scalar_tensor_tensor(h[:, t, :], y2[u], wts[:, t, 1:2], h[:, t, :], ALU.mult, ALU.add).then_inc(s["fh"], 1)
                add_y(0)
                for t in range(NT + 1):
                    if t < NT:
                        if t + 1 < NT:
                            add_y(t + 1)
                        u = t % 2
                        dve.wait_ge(s["fgate_psum"], t + 1)
                        if t >= 2:
                            dve.wait_ge(s["fprod"], t - 1)
                        dve.tensor_tensor(gate[u].rearrange("p (b n) -> p b n", b=2), PS[:, 2:4, :], bpg.rearrange("p (b n) -> p b n", b=2),
                                          ALU.add).then_inc(s["fgate"], 1)
                        dve.wait_ge(s["fsig"], t + 1)
                        dve.wait_ge(s["fple_psum"], t + 1)
                        link(dve, "fprod", dve.tensor_tensor(prodf[u].rearrange("p (b n) -> p b n", b=2), gate[u].rearrange("p (b n) -> p b n", b=2),
                                                             PS[:, 4:6, :], ALU.mult))
                        if t >= 2:
                            dve.wait_ge(s["fstored%d" % u], 16 * (t // 2))
                        dve.tensor_tensor(outb[u], prodf[u], h[:, t, :], ALU.add).then_inc(s["fout"], 1)

            @block.tensor
            def _(pe):
                def turn(t):
                    pe.wait_ge(s["fh"], t + 1)
                    if t >= 1:
                        pe.wait_ge(s["fhT"], t)
                    for k in range(KD):
                        last = pe.transpose(PS[:, k // 4, (k % 4) * P:(k % 4 + 1) * P], h[:, t, k * P:(k + 1) * P], ident[:, :])
                    last.then_inc(s["fhT_psum"], 1)
                    pe.wait_ge(s["fp_loaded%d" % (t % 2)], 16 * (t // 2 + 1))
                    if t >= 1:
                        pe.wait_ge(s["fpT"], t)
                    for k in range(2):
                        last = pe.transpose(PS[:, 6, k * P:(k + 1) * P], pt[t % 2][:, k * P:(k + 1) * P], ident[:, :])
                    last.then_inc(s["fpT_psum"], 1)
                turn(0)
                for t in range(NT):
                    pe.wait_ge(s["fhT"], t + 1)
                    if t >= 1:
                        pe.wait_ge(s["fgate"], t)
                    for b in range(2):
                        for k in range(KD):
                            last = pe.matmul(PS[:, 2 + b, :], h2T[t % 2][:, k * P:(k + 1) * P], wpg[:, k, b * 512:(b + 1) * 512],
                                             start=k == 0, stop=k == KD - 1)
                    last.then_inc(s["fgate_psum"], 1)
                    if t + 1 < NT:
                        turn(t + 1)
                    pe.wait_ge(s["fpT"], t + 1)
                    if t >= 1:
                        pe.wait_ge(s["fprod"], t)
                    for b in range(2):
                        for k in range(2):
                            last = pe.matmul(PS[:, 4 + b, :], pT[t % 2][:, k * P:(k + 1) * P], wple[:, k, b * 512:(b + 1) * 512],
                                             start=k == 0, stop=k == 1)
                    last.then_inc(s["fple_psum"], 1)


_INS = ['x', 'p', 'ln1', 'w_in', 'g_cq', 'g_ckv', 'w_uq', 'w_ukv', 'g_qh', 'g_kh', 'sg_ln_g', 'sg_ln_b',
        'sg_w', 'sg_b', 'lam_re', 'lam_im', 'log_dt', 'ssm_b_re', 'ssm_b_im', 'ssm_c_re', 'ssm_c_im',
        'ssm_d', 'w_glu', 'b_glu', 'g_mix', 'w_out', 'ln2', 'w_rg', 'b_rg', 'w_rexp', 'b_rexp', 'w1',
        'w3', 'w2', 'w_pg', 'b_pg', 'w_ple']
_OUTS = [((1, S, D), 'float32')]


def kernel(**inputs):
    import numpy as _np
    import concourse.bacc as _bacc
    from concourse import mybir as _mybir
    from concourse.bass_utils import run_bass_kernel_spmd as _run

    inv = (1.0 / (_np.float32(10000.0) ** (_np.arange(0, ROPE, 2, dtype=_np.float32) / _np.float32(ROPE)))).astype(_np.float32)
    ang = _np.arange(S, dtype=_np.float32)[:, None] * inv[None, :]
    laid = {name: inputs[name] for name in _INS}
    laid["rope_cos"], laid["rope_sin"] = _np.cos(ang), _np.sin(ang)

    nc = _bacc.Bacc("TRN2", target_bir_lowering=False, num_devices=1)
    arrays, args = {}, []
    for name, a in laid.items():
        a = _np.ascontiguousarray(a)
        arrays[f"in_{name}_dram"] = a
        args.append(nc.dram_tensor(f"in_{name}_dram", a.shape, _mybir.dt.from_np(a.dtype), kind="ExternalInput").ap())
    for i, (shape, dtype) in enumerate(_OUTS):
        dt = _mybir.dt.from_np(_np.dtype(dtype))
        args.append(nc.dram_tensor(f"out_{i}_dram", shape, dt, kind="ExternalOutput").ap())
    trunk_kernel(nc, *args)
    r = _run(nc, [arrays], core_ids=[0])
    return r.results[0]["out_0_dram"]
```

```python
import concourse.bass as bass
from concourse import mybir
from contextlib import ExitStack
import math
import numpy as np

P = 128
S, D = 1024, 1024
NT, KD = S // P, D // P
H, NOPE, ROPE, VD = 8, 64, 32, 64
QK = NOPE + ROPE
RQ, RKV = 384, 256
SG, SGG = 256, 4
SSM, G, C, NS = 256, 16, 16, 64
COLS = RQ + RKV + ROPE + 2 * SG + SSM
ZC = COLS // 3
O_KR = RQ + RKV
O_SG = O_KR + ROPE
O_SSM = O_SG + 2 * SG
LC, NC = 8, S // 8
E, EG, EPG, F = 32, 4, 8, 256
PLE = 256
EPS = 1e-6
SCALE = QK ** -0.5
NEG = -1e30
OVER = (2 * S) // P - 1

fp32 = mybir.dt.float32
fp32r = mybir.dt.float32r
bf16 = mybir.dt.bfloat16
u32 = mybir.dt.uint32
i32 = mybir.dt.int32
ALU = mybir.AluOpType
ACT = mybir.ActivationFunctionType
AX = mybir.AxisListType

ROWS = {}
_n = 0
for _name, _k in (("ln1", 8), ("g_cq", 3), ("g_ckv", 2), ("g_mix", 8), ("ln2", 8), ("b_glu", 2), ("sg_b", 4)):
    ROWS[_name] = (_n, _k)
    _n += _k
NROWS = _n


def trunk_kernel(nc, x, p, ln1, w_in, g_cq, g_ckv, w_uq, w_ukv, g_qh, g_kh, sg_ln_g, sg_ln_b, sg_w,
                 sg_b, lam_re, lam_im, log_dt, ssm_b_re, ssm_b_im, ssm_c_re, ssm_c_im, ssm_d, w_glu,
                 b_glu, g_mix, w_out, ln2, w_rg, b_rg, w_rexp, b_rexp, w1, w3, w2, w_pg, b_pg,
                 w_ple, rope_cos, rope_sin, out):
    x, p, out = x[0], p[0, 0], out[0]
    (ln1, w_in, g_cq, g_ckv, w_uq, w_ukv, g_qh, g_kh, sg_ln_g, sg_ln_b, sg_w, sg_b, lam_re, lam_im,
     log_dt, ssm_b_re, ssm_b_im, ssm_c_re, ssm_c_im, ssm_d, w_glu, b_glu, g_mix, w_out, ln2, w_rg,
     b_rg, w_rexp, b_rexp, w1, w3, w2, w_pg, b_pg, w_ple) = [a[0] for a in (
         ln1, w_in, g_cq, g_ckv, w_uq, w_ukv, g_qh, g_kh, sg_ln_g, sg_ln_b, sg_w, sg_b, lam_re,
         lam_im, log_dt, ssm_b_re, ssm_b_im, ssm_c_re, ssm_c_im, ssm_d, w_glu, b_glu, g_mix, w_out,
         ln2, w_rg, b_rg, w_rexp, b_rexp, w1, w3, w2, w_pg, b_pg, w_ple)]
    ctx = ExitStack()
    with ctx:
        def sb(name, shape, dt=fp32):
            return ctx.enter_context(nc.sbuf_tensor(name, shape, dt))

        def sem(name):
            return ctx.enter_context(nc.semaphore(name))

        phase = []
        s, L = {}, {}

        def signals(letter, names, prefix=""):
            if phase:
                nc.clear_and_free_semaphores(phase)
                phase.clear()
                nc.all_engine_barrier()
            for n in names:
                s[prefix + n] = nc.alloc_semaphore(name=letter + "_" + n)
                phase.append(s[prefix + n])

        def dram(name, shape, dt=fp32):
            return nc.dram_tensor(name, shape, dt).ap()

        zs_d = dram("zs_scratch", [S, SSM])
        ys_d = dram("ys_scratch", [SSM, LC, NC])
        xs_d = dram("xs_scratch", [SSM, LC, NC])
        xf_d = dram("xf_scratch", [S, D])
        tok_d = dram("tok_scratch", [E * S, 1])
        y_d = dram("y_scratch", [2 * S, D])

        R1 = sb("R1", [P, KD * COLS])
        with nc.sbuf_tensor("RQKV_r", [P, 20480], fp32r) as RQKV_r:
            pass
        RQKV = sb("RQKV", [P, 20480])
        R3 = sb("R3", [P, 8192])
        with nc.sbuf_tensor("R2_r", [P, 10176], fp32r) as R2_r:
            pass
        R2 = sb("R2", [P, 10176])
        ident = sb("ident", [P, P])
        vecs = sb("vecs", [P, NROWS])
        small = sb("small", [P, 1400])
        PS = ctx.enter_context(nc.psum_tensor("PS", [P, 8, 512], fp32))

        def vec(name):
            a, k = ROWS[name]
            return vecs[:, a:a + k]

        def row_bcast(a):
            return a.unsqueeze(0).broadcast_to((P, a.shape[0]))

        o = [0]

        def take(n):
            o[0] += n
            return small[:, o[0] - n:o[0]]
        cos_sb = take(NT * 16).rearrange("p (t r) -> p t r", t=NT)
        sin_sb = take(NT * 16).rearrange("p (t r) -> p t r", t=NT)
        gq_b, gk_b = take(QK), take(QK)
        stat = take(96)
        eps = take(1)
        tril = take(P)
        rows_sb = take(P)
        wts = take(2 * NT).rearrange("p (t c) -> p t c", t=NT)
        dest = take(2 * NT).bitcast(u32).rearrange("p (t c) -> p t c", t=NT)

        QT = RQKV[:, 0:8192].rearrange("p (h t) -> p h t", h=H)
        KT = RQKV[:, 8192:16384].rearrange("p (h t) -> p h t", h=H)
        V = RQKV[:, 16384:20480].rearrange("p (t c) -> p t c", t=NT)
        ZG = R3[:, 4096:8192].rearrange("p (t c) -> p t c", t=NT)
        xt = [R3[:, 0:1024], R3[:, 1024:2048]]
        xT = [R3[:, 2048:3072], R3[:, 3072:4096]]
        win = R1[:, :].rearrange("p (k n) -> p k n", k=KD)
        a2 = [0]

        def in2(n):
            a2[0] += n
            return R2[:, a2[0] - n:a2[0]]
        wuq = in2(3 * 768).rearrange("p (k n) -> p k n", k=3)
        wukv = in2(2 * 1024).rearrange("p (k n) -> p k n", k=2)
        z = [in2(COLS), in2(COLS)]
        cT = in2(640)
        sq = in2(768)
        qn = in2(768).rearrange("p (h c) -> p h c", h=H)
        kn = in2(768).rearrange("p (h c) -> p h c", h=H)
        rt = small[:, 1040:1040 + 256].rearrange("p (a h c) -> p a h c", a=2, h=H)
        assert o[0] <= 1040
        sgv = sb("sgv", [P, 512])

        zp = [PS[:, c, 0:ZC] for c in range(3)]
        tA = PS[:, 3:5, :].rearrange("p b n -> p (b n)")
        tB = PS[:, 5:7, :].rearrange("p b n -> p (b n)")
        qp = PS[:, 5:7, 0:384]

        signals("a", (
            "ident", "x_loaded0", "x_loaded1", "ln1_loaded", "ln1_psum", "rows_loaded", "rows_psum", "vecs", "tables_loaded", "wu_loaded",
            "x_psum", "xT", "x_square", "x_rstd", "z_psum", "z", "c_square", "c", "c_psum", "cT",
            "q_psum", "kv_psum", "q_square", "q_scaled", "k_square", "k_scaled", "v", "qn", "kn", "qT_psum", "kT_psum", "qT", "kT",
            "zg", "gelu", "zs_stored0", "zs_stored1", "dve", "pool", "tril", "k_stat", "q_stat", "x_rms", "c_rms", "q_rms", "k_rms") +
                tuple("win_loaded%d" % k for k in range(KD)))

        def link(eng, name, ins, by=1):
            L[name] = L.get(name, 0) + by
            ins.then_inc(s[name], by)
            eng.wait_ge(s[name], L[name])

        def rotate(eng, name, t, n, gain, tmp, done):
            link(eng, name, eng.tensor_tensor(n, n, gain.unsqueeze(1).broadcast_to((P, H, QK)), ALU.mult))
            x1, x2 = n[:, :, NOPE:NOPE + 16], n[:, :, NOPE + 16:QK]
            co = cos_sb[:, t, :].unsqueeze(1).broadcast_to((P, H, 16))
            si = sin_sb[:, t, :].unsqueeze(1).broadcast_to((P, H, 16))
            eng.tensor_tensor(tmp[:, 0], x1, si, ALU.mult)
            eng.tensor_tensor(tmp[:, 1], x2, si, ALU.mult)
            eng.tensor_tensor(x1, x1, co, ALU.mult)
            link(eng, name, eng.tensor_tensor(x2, x2, co, ALU.mult))
            eng.tensor_tensor(x1, x1, tmp[:, 1], ALU.subtract)
            link(eng, done, eng.tensor_tensor(x2, x2, tmp[:, 0], ALU.add))

        with nc.Block() as block:
            @block.sync
            def _(sp):
                at, k = ROWS["ln1"]
                sp.dma_start(rows_sb[at:at + k, :], ln1.rearrange("(k p) -> k p", p=P)).then_inc(s["ln1_loaded"], 16)
                sp.dma_start(xt[0], x[0:P, :]).then_inc(s["x_loaded0"], 16)
                for k in range(KD):
                    sp.dma_start(win[:, k, :], w_in[k * P:(k + 1) * P, :]).then_inc(s["win_loaded%d" % k], 16)
                    if k == 1:
                        sp.dma_start(xt[1], x[P:2 * P, :]).then_inc(s["x_loaded1"], 16)
                sp.dma_start(wuq, w_uq.rearrange("(k p) n -> p k n", p=P)).then_inc(s["wu_loaded"], 16)
                sp.dma_start(wukv, w_ukv.rearrange("(k p) n -> p k n", p=P)).then_inc(s["wu_loaded"], 16)
                for t in range(2, NT + 2):
                    if t < NT:
                        sp.wait_ge(s["x_psum"], t - 1)
                        sp.wait_ge(s["x_square"], t - 1)
                        sp.dma_start(xt[t % 2], x[t * P:(t + 1) * P, :]).then_inc(s["x_loaded%d" % (t % 2)], 16)
                    sp.wait_ge(s["z"], 3 * (t - 1))
                    sp.dma_start(zs_d[(t - 2) * P:(t - 1) * P, :], z[t % 2][:, O_SSM:COLS]).then_inc(s["zs_stored%d" % (t % 2)], 16)
                for u in range(2):
                    sp.wait_ge(s["zs_stored%d" % u], 16 * (NT // 2))

            @block.gpsimd
            def _(pool):
                link(pool, "pool", pool.memset(eps, EPS))
                link(pool, "pool", pool.memset(ident[:], 0.0))
                pool.affine_select(out=ident[:], in_=ident[:], compare_op=ALU.not_equal, fill=1.0, base=0,
                                   pattern=[[-1, P]], channel_multiplier=1).then_inc(s["ident"], 1)
                link(pool, "pool", pool.memset(tril, 0.0))
                pool.affine_select(out=tril, in_=tril, compare_op=ALU.is_ge, fill=NEG, base=0,
                                   pattern=[[-1, P]], channel_multiplier=1).then_inc(s["tril"], 1)
                pool.wait_ge(s["tables_loaded"], 16 * 6)
                link(pool, "pool", pool.tensor_scalar(gq_b, gq_b, SCALE, None, ALU.mult))
                for t in range(NT):
                    pool.wait_ge(s["z"], 3 * (t + 1))
                    pool.tensor_copy(ZG[:, t, :], z[t % 2][:, O_SG:O_SSM]).then_inc(s["zg"], 1)
                    pool.wait_ge(s["q_scaled"], t + 1)
                    rotate(pool, "pool", t, qn, gq_b, rt, "qn")
                    if t + 1 < NT:
                        pool.wait_ge(s["k_scaled"], t + 1)
                        rotate(pool, "pool", t, kn, gk_b, rt, "kn")

            @block.scalar
            def _(act):
                for v, a in ((g_cq, "g_cq"), (g_ckv, "g_ckv"), (g_mix, "g_mix"), (ln2, "ln2"), (b_glu, "b_glu")):
                    at, k = ROWS[a]
                    act.dma_start(rows_sb[at:at + k, :], v.rearrange("(k p) -> k p", p=P)).then_inc(s["rows_loaded"], 16)
                at, k = ROWS["sg_b"]
                act.dma_start(rows_sb[at:at + k, :], sg_b).then_inc(s["rows_loaded"], 16)
                act.dma_start(cos_sb, rope_cos.rearrange("(t p) r -> p t r", p=P)).then_inc(s["tables_loaded"], 16)
                act.dma_start(sin_sb, rope_sin.rearrange("(t p) r -> p t r", p=P)).then_inc(s["tables_loaded"], 16)
                act.dma_start(gq_b, row_bcast(g_qh)).then_inc(s["tables_loaded"], 16)
                act.dma_start(gk_b, row_bcast(g_kh)).then_inc(s["tables_loaded"], 16)
                act.dma_start(sgv[:, 0:SG], row_bcast(sg_ln_g)).then_inc(s["tables_loaded"], 16)
                act.dma_start(sgv[:, SG:], row_bcast(sg_ln_b)).then_inc(s["tables_loaded"], 16)

                def rms(dst, src, n, done):
                    act.activation(dst, src, ACT.Sqrt, bias=eps[:, :], scale=1.0 / n).then_inc(s[done], 1)

                def x_square(t):
                    act.wait_ge(s["x_loaded%d" % (t % 2)], 16 * (t // 2 + 1))
                    link(act, "x_square", act.activation(sq.bitcast(bf16)[:, 0:1024], xt[t % 2], ACT.Square,
                                                         accum_out=stat[:, t:t + 1]))
                    rms(stat[:, 8 + t:9 + t], stat[:, t:t + 1], D, "x_rms")

                def z_out(t, c):
                    act.wait_ge(s["z_psum"], 3 * t + c + 1)
                    act.wait_ge(s["x_rstd"], t + 1)
                    if t >= 2 and c == 0:
                        act.wait_ge(s["zg"], t - 1)
                        act.wait_ge(s["k_scaled"], t - 1)
                        act.wait_ge(s["zs_stored%d" % (t % 2)], 16 * (t // 2))
                    act.activation(z[t % 2][:, c * ZC:(c + 1) * ZC], zp[c], ACT.Copy,
                                   scale=stat[:, 8 + t:9 + t]).then_inc(s["z"], 1)

                def heads(t):
                    zt = z[t % 2]
                    act.wait_ge(s["q_psum"], t + 1)
                    act.activation(sq.rearrange("p (b n) -> p b n", b=2), qp, ACT.Square).then_inc(s["q_square"], 1)
                    act.wait_ge(s["kv_psum"], t + 1)
                    for b, bank in ((0, 7), (1, 0)):
                        kv = PS[:, bank, :].rearrange("p (h c) -> p h c", c=NOPE + VD)
                        act.activation(V[:, t, :].rearrange("p (h c) -> p h c", h=H)[:, 4 * b:4 * b + 4, :],
                                       kv[:, :, NOPE:], ACT.Copy).then_inc(s["v"], 1)
                    act.wait_ge(s["q_stat"], t + 1)
                    rms(stat[:, 56:64], stat[:, 48:56], QK, "q_rms")
                    for b, bank in ((0, 7), (1, 0)):
                        kv = PS[:, bank, :].rearrange("p (h c) -> p h c", c=NOPE + VD)
                        act.activation(sq[:, 0:512].rearrange("p (h c) -> p h c", h=H)[:, 4 * b:4 * b + 4, :],
                                       kv[:, :, 0:NOPE], ACT.Square)
                    act.activation(sq[:, 512:512 + ROPE], zt[:, O_KR:O_SG], ACT.Square).then_inc(s["k_square"], 1)
                    act.wait_ge(s["k_stat"], t + 1)
                    rms(stat[:, 72:80], stat[:, 64:72], QK, "k_rms")

                def t_out(t, psum, ready, dst, done):
                    act.wait_ge(s[ready], t + 1)
                    act.activation(dst[0:QK, :, t * P:(t + 1) * P], tA[0:QK, :].rearrange("p (h c) -> p h c", h=H),
                                   ACT.Copy).then_inc(s[done], 1)

                act.wait_ge(s["pool"], 1)
                x_square(0)
                for c in range(3):
                    z_out(0, c)
                x_square(1)
                for t in range(NT):
                    zt = z[t % 2]
                    if t >= 1:
                        act.wait_ge(s["k_stat"], t)
                    act.activation(sq[:, 0:RQ], zt[:, 0:RQ], ACT.Square, accum_out=stat[:, 16 + t:17 + t])
                    link(act, "c_square", act.activation(sq[:, RQ:O_KR], zt[:, RQ:O_KR], ACT.Square,
                                                         accum_out=stat[:, 24 + t:25 + t]))
                    act.activation(stat[:, 32:33], stat[:, 16 + t:17 + t], ACT.Sqrt, bias=eps[:, :], scale=1.0 / RQ)
                    rms(stat[:, 33:34], stat[:, 24 + t:25 + t], RKV, "c_rms")
                    if t + 2 < NT:
                        x_square(t + 2)
                    if t >= 1:
                        t_out(t - 1, tA, "kT_psum", KT, "kT")
                    if t + 1 < NT:
                        z_out(t + 1, 0)
                        z_out(t + 1, 1)
                    heads(t)
                    if t + 1 < NT:
                        z_out(t + 1, 2)
                    else:
                        act.wait_ge(s["zg"], NT)
                        act.activation(R3[:, 4096:8192], R3[:, 4096:8192], ACT.Gelu_apprx_tanh).then_inc(s["gelu"], 1)
                    t_out(t, tA, "qT_psum", QT, "qT")
                act.activation(stat[:, 90:91], eps[:, :], ACT.Exp)
                t_out(NT - 1, tA, "kT_psum", KT, "kT")

            @block.vector
            def _(dve):
                dve.wait_ge(s["ln1_psum"], 1)
                link(dve, "vecs", dve.tensor_copy(vecs[:, 0:KD], PS[:, 7, 0:KD]))

                def x_out(t):
                    dve.wait_ge(s["x_psum"], t + 1)
                    if t >= 2:
                        dve.wait_ge(s["z_psum"], 3 * (t - 1))
                    dve.tensor_tensor(xT[t % 2].rearrange("p (k c) -> p k c", k=KD), tA.rearrange("p (k c) -> p k c", k=KD),
                                      vec("ln1").unsqueeze(2).broadcast_to((P, KD, P)), ALU.mult).then_inc(s["xT"], 1)
                    dve.wait_ge(s["x_rms"], t + 1)
                    dve.reciprocal(stat[:, 8 + t:9 + t], stat[:, 8 + t:9 + t]).then_inc(s["x_rstd"], 1)

                x_out(0)
                x_out(1)
                dve.wait_ge(s["rows_psum"], 1)
                link(dve, "vecs", dve.tensor_copy(vecs[:, KD:], PS[:, 7, KD:NROWS]))
                for t in range(NT):
                    zt = z[t % 2]
                    dve.wait_ge(s["c_rms"], t + 1)
                    link(dve, "dve", dve.reciprocal(stat[:, 34:36], stat[:, 32:34]))
                    dve.tensor_scalar(zt[:, 0:RQ], zt[:, 0:RQ], stat[:, 34:35], None, ALU.mult)
                    dve.tensor_scalar(zt[:, RQ:O_KR], zt[:, RQ:O_KR], stat[:, 35:36], None, ALU.mult).then_inc(s["c"], 1)
                    dve.wait_ge(s["c_psum"], t + 1)
                    gains = vecs[:, ROWS["g_cq"][0]:ROWS["g_cq"][0] + 5].unsqueeze(2).broadcast_to((P, 5, P))
                    dve.tensor_tensor(cT.rearrange("p (k c) -> p k c", k=5), tB[:, 0:640].rearrange("p (k c) -> p k c", k=5),
                                      gains, ALU.mult).then_inc(s["cT"], 1)
                    if t + 2 < NT:
                        x_out(t + 2)
                    dve.wait_ge(s["q_square"], t + 1)
                    ssq, rq = stat[:, 48:56], stat[:, 56:64]
                    dve.tensor_reduce(ssq, sq.rearrange("p (h c) -> p h c", h=H), AX.X, ALU.add).then_inc(s["q_stat"], 1)
                    dve.wait_ge(s["q_rms"], t + 1)
                    link(dve, "dve", dve.reciprocal(rq, rq))
                    if t >= 1:
                        dve.wait_ge(s["qT_psum"], t)
                    dve.tensor_tensor(qn.rearrange("p (b h) c -> p b h c", b=2), qp.rearrange("p b (h c) -> p b h c", c=QK),
                                      rq.rearrange("p (b h) -> p b h", b=2).unsqueeze(3).broadcast_to((P, 2, 4, QK)), ALU.mult).then_inc(s["q_scaled"], 1)
                    dve.wait_ge(s["k_square"], t + 1)
                    ssk, rk, sskr = stat[:, 64:72], stat[:, 72:80], stat[:, 80:81]
                    dve.tensor_reduce(ssk, sq[:, 0:512].rearrange("p (h c) -> p h c", h=H), AX.X, ALU.add)
                    link(dve, "dve", dve.tensor_reduce(sskr, sq[:, 512:512 + ROPE], AX.X, ALU.add))
                    dve.tensor_scalar(ssk, ssk, sskr, None, ALU.add).then_inc(s["k_stat"], 1)
                    dve.wait_ge(s["k_rms"], t + 1)
                    link(dve, "dve", dve.reciprocal(rk, rk))
                    if t >= 1:
                        dve.wait_ge(s["kT_psum"], t)
                    for b, bank in ((0, 7), (1, 0)):
                        dve.tensor_tensor(kn[:, 4 * b:4 * b + 4, 0:NOPE], PS[:, bank, :].rearrange("p (h c) -> p h c", h=4)[:, :, 0:NOPE],
                                          rk[:, 4 * b:4 * b + 4].unsqueeze(2).broadcast_to((P, 4, NOPE)), ALU.mult)
                    dve.tensor_tensor(kn[:, :, NOPE:], zt[:, O_KR:O_SG].unsqueeze(1).broadcast_to((P, H, ROPE)),
                                      rk.unsqueeze(2).broadcast_to((P, H, ROPE)), ALU.mult).then_inc(s["k_scaled"], 1)
                dve.wait_ge(s["k_scaled"], NT)
                dve.wait_ge(s["tables_loaded"], 16 * 6)
                rotate(dve, "dve", NT - 1, kn, gk_b, sq[:, 0:256].rearrange("p (a h r) -> p a h r", a=2, h=H), "kn")

            @block.tensor
            def _(pe):
                pe.wait_ge(s["ident"], 1)
                pe.wait_ge(s["ln1_loaded"], 16)
                pe.transpose(PS[:, 7, 0:KD], rows_sb[0:KD, :], ident[0:KD, 0:KD]).then_inc(s["ln1_psum"], 1)

                def x_in(t):
                    pe.wait_ge(s["x_loaded%d" % (t % 2)], 16 * (t // 2 + 1))
                    if t == 1:
                        pe.wait_ge(s["xT"], 1)
                    if t >= 3:
                        pe.wait_ge(s["kT"], t - 2)
                    if t == 2:
                        pe.wait_ge(s["xT"], 2)
                    for k in range(KD):
                        last = pe.transpose(tA[:, k * P:(k + 1) * P], xt[t % 2][:, k * P:(k + 1) * P], ident[:, :])
                    last.then_inc(s["x_psum"], 1)

                def z_mm(t, c):
                    if c == 0:
                        pe.wait_ge(s["xT"], t + 1)
                        if t >= 2:
                            pe.wait_ge(s["v"], 2 * (t - 1))
                            pe.wait_ge(s["k_scaled"], t - 1)
                    if t >= 1:
                        pe.wait_ge(s["z"], 3 * (t - 1) + c + 1)
                    for k in range(KD):
                        last = pe.matmul(zp[c], xT[t % 2][:, k * P:(k + 1) * P], win[:, k, c * ZC:(c + 1) * ZC],
                                         start=k == 0, stop=k == KD - 1)
                    last.then_inc(s["z_psum"], 1)

                def head_T(t, src, ready, psum):
                    pe.wait_ge(s[ready], t + 1)
                    for h in range(H):
                        last = pe.transpose(tA[0:QK, h * P:(h + 1) * P], src[:, h, :], ident[:, :])
                    last.then_inc(s[psum], 1)

                x_in(0)
                pe.wait_ge(s["xT"], 1)
                for k in range(KD):
                    pe.wait_ge(s["win_loaded%d" % k], 16)
                    for c in range(3):
                        last = pe.matmul(zp[c], xT[0][:, k * P:(k + 1) * P], win[:, k, c * ZC:(c + 1) * ZC],
                                         start=k == 0, stop=k == KD - 1)
                        if k == KD - 1:
                            last.then_inc(s["z_psum"], 1)
                    if k == KD // 2:
                        x_in(1)
                        pe.wait_ge(s["vecs"], 1)
                        pe.wait_ge(s["rows_loaded"], 16 * 6)
                        pe.transpose(PS[:, 7, 0:NROWS], rows_sb[0:NROWS, :], ident[0:NROWS, 0:NROWS]).then_inc(s["rows_psum"], 1)
                for t in range(NT):
                    zt = z[t % 2]
                    if t + 1 < NT:
                        z_mm(t + 1, 0)
                    if t >= 1:
                        pe.wait_ge(s["qT"], t)
                        head_T(t - 1, kn, "kn", "kT_psum")
                    pe.wait_ge(s["c"], t + 1)
                    if t >= 1:
                        pe.wait_ge(s["q_scaled"], t)
                    for k in range(5):
                        last = pe.transpose(tB[:, k * P:(k + 1) * P], zt[:, k * P:(k + 1) * P], ident[:, :])
                    last.then_inc(s["c_psum"], 1)
                    if t + 1 < NT:
                        z_mm(t + 1, 1)
                    if t + 2 < NT:
                        x_in(t + 2)
                    pe.wait_ge(s["cT"], t + 1)
                    if t == 0:
                        pe.wait_ge(s["wu_loaded"], 32)
                    for c in range(2):
                        for k in range(3):
                            last = pe.matmul(PS[:, 5 + c, 0:384], cT[:, k * P:(k + 1) * P], wuq[:, k, c * 384:(c + 1) * 384],
                                             start=k == 0, stop=k == 2)
                    last.then_inc(s["q_psum"], 1)
                    if t == 0:
                        pe.wait_ge(s["vecs"], 2)
                    if t >= 1:
                        pe.wait_ge(s["v"], 2 * t)
                        pe.wait_ge(s["k_scaled"], t)
                    pe.wait_ge(s["z"], 3 * (t + 1) + 1 if t + 1 < NT else 3 * NT)
                    for b, bank in ((0, 7), (1, 0)):
                        for k in range(2):
                            last = pe.matmul(PS[:, bank, :], cT[:, (3 + k) * P:(4 + k) * P], wukv[:, k, b * 512:(b + 1) * 512],
                                             start=k == 0, stop=k == 1)
                    last.then_inc(s["kv_psum"], 1)
                    if t + 1 < NT:
                        z_mm(t + 1, 2)
                    pe.wait_ge(s["xT"], min(t + 3, NT))
                    head_T(t, qn, "qn", "qT_psum")
                pe.wait_ge(s["qT"], NT)
                head_T(NT - 1, kn, "kn", "kT_psum")

        O = R3[:, 0:4096].rearrange("p (t c) -> p t c", t=NT)
        Pb = [R2[:, 0:1024], R2[:, 1024:2048]]
        PTb = [R2[:, 2048:3072], R2[:, 3072:4096]]
        SBn = R2[:, 4096:6144].rearrange("p (g q c) -> p g q c", g=G, q=LC)
        prod = [R2[:, 6144:8192], R2[:, 8192:10176]]
        r1 = [0]

        def in1(n):
            r1[0] += n
            return R1[:, r1[0] - n:r1[0]]
        Ec = in1(G * NC).rearrange("p (g k) -> p g k", g=G)
        Es = in1(G * NC).rearrange("p (g k) -> p g k", g=G)
        LL1 = in1(G * 9 * C).rearrange("p (g j c) -> p g j c", g=G, j=9)
        LL2 = in1(G * 9 * C).rearrange("p (g j c) -> p g j c", g=G, j=9)
        Bb = in1(G * C).rearrange("p (g c) -> p g c", g=G)
        BY = in1(G * C).rearrange("p (g c) -> p g c", g=G)
        Xb = in1(G * C).rearrange("p (g c) -> p g c", g=G)
        Yb = in1(G * C).rearrange("p (g c) -> p g c", g=G)
        CX = in1(G * C).rearrange("p (g c) -> p g c", g=G)
        CY = in1(G * C).rearrange("p (g c) -> p g c", g=G)
        Pr = in1(9 * G).rearrange("p (j g) -> p j g", j=9)
        Pi = in1(9 * G).rearrange("p (j g) -> p j g", j=9)
        lam = in1(3 * G).rearrange("p (a g) -> p a g", a=3)
        sgn = in1(2)
        rows3 = in1(P)
        cnat = prod[1][:, 0:512].rearrange("p (a f n) -> p a f n", a=2, f=2)
        v16 = [0]

        def tiny():
            v16[0] += G
            return R1[:, r1[0] + v16[0] - G:r1[0] + v16[0]]
        t1, t2, t3, t4, dt, lr, li, mag = [tiny() for _ in range(8)]
        th, co, si, den, fr, fi, kk, rr = [tiny() for _ in range(8)]
        R8 = tiny()

        signals("b", ("s_psum", "nmax", "exp", "pt_psum", "ptd", "pta", "o_psum", "o", "par_loaded", "par_psum", "par",
                  "vcent", "vsq", "den", "rden", "pdve", "ppool", "sgn"))
        zs_loaded = sem("zs_loaded")
        vst = stat[:, 16:80]
        steps = [(h, i if h % 2 == 0 else NT - 1 - i) for h in range(H) for i in range(NT)]
        PAR = 5

        def wide(n):
            return sum(1 for _, i in steps[:n] if i >= 4)

        with nc.Block() as block:
            @block.sync
            def _(sp):
                for a, v in enumerate((lam_re, lam_im, log_dt)):
                    for half in range(2):
                        sp.dma_start(rows3[a * G:(a + 1) * G, half * NS:(half + 1) * NS], v).then_inc(s["par_loaded"], 16)
                for a, (v, w) in enumerate(((ssm_c_re, ssm_c_im), (ssm_c_im, ssm_c_re))):
                    for half, c in ((0, v), (1, w)):
                        sp.dma_start(cnat[:, a, :, half * NS:(half + 1) * NS],
                                     c.rearrange("(f g) c n -> (g c) f n", f=2)).then_inc(s["par_loaded"], 16)
                for dst, v, w in ((Xb, ssm_b_re, ssm_b_im), (Yb, ssm_b_im, ssm_b_re)):
                    for half, c in ((0, v), (1, w)):
                        sp.dma_start(dst[half * NS:(half + 1) * NS, :, :], c.rearrange("g n c -> n g c")).then_inc(s["par_loaded"], 16)
                sp.wait_ge(s["par_loaded"], 16 * 14)
                sp.wait_ge(s["s_psum"], 2 * NT)
                sp.dma_start(RQKV[:, 0:2048].rearrange("p (t c) -> p t c", t=NT), zs_d.rearrange("(t p) c -> p t c", p=P)).then_inc(zs_loaded, 16)
                sp.wait_ge(zs_loaded, 16)

            @block.gpsimd
            def _(pool):
                def put(ins):
                    link(pool, "ppool", ins)

                def cmul(dr, di, ar, ai, br, bi, t1, t2, t3, t4):
                    pool.tensor_tensor(t1, ar, br, ALU.mult)
                    pool.tensor_tensor(t2, ai, bi, ALU.mult)
                    pool.tensor_tensor(t3, ar, bi, ALU.mult)
                    put(pool.tensor_tensor(t4, ai, br, ALU.mult))
                    pool.tensor_tensor(dr, t1, t2, ALU.subtract)
                    put(pool.tensor_tensor(di, t3, t4, ALU.add))

                def nearest(dst, src, factor):
                    put(pool.tensor_scalar(dst, src, factor, 12582912.0, ALU.mult, ALU.add))
                    put(pool.tensor_scalar(dst, dst, -12582912.0, None, ALU.add))

                def less(dst, src, k, parts, t):
                    for n, c in enumerate(parts):
                        put(pool.tensor_scalar(t, k, -c, None, ALU.mult))
                        put(pool.tensor_tensor(dst, src if n == 0 else dst, t, ALU.add))

                def poly(dst, v, coefs):
                    put(pool.tensor_scalar(dst, v, coefs[-1], coefs[-2], ALU.mult, ALU.add))
                    for c in coefs[-3::-1]:
                        put(pool.tensor_tensor(dst, dst, v, ALU.mult))
                        put(pool.tensor_scalar(dst, dst, c, None, ALU.add))

                def exp(dst, src, k, t, r):
                    put(pool.tensor_scalar(dst, src, -87.0, 88.0, ALU.max, ALU.min))
                    nearest(k, dst, 1 / math.log(2))
                    less(r, dst, k, (0.693359375, math.log(2) - 0.693359375), t)
                    poly(dst, r, [1 / math.factorial(n) for n in range(9)])
                    put(pool.tensor_scalar(t.bitcast(i32), k, 127.0, float(1 << 23), ALU.add, ALU.mult))
                    put(pool.tensor_tensor(dst, dst, t, ALU.mult))

                pool.wait_ge(s["par_loaded"], 16 * 14)
                put(pool.memset(sgn[0:NS, 0:1], 1.0))
                put(pool.memset(sgn[NS:P, 0:1], -1.0))
                put(pool.memset(sgn[0:NS, 1:2], -1.0))
                pool.memset(Pr[:, 0, :], 1.0)
                pool.memset(Pi[:, 0, :], 0.0)
                pool.memset(Ec[:, :, 0:1], 1.0)
                put(pool.memset(Es[:, :, 0:1], 0.0))
                link(pool, "sgn", pool.memset(sgn[NS:P, 1:2], 1.0))
                pool.wait_ge(s["par"], 1)
                exp(dt, lam[:, 2, :], kk, t1, rr)
                put(pool.tensor_scalar(lr, lam[:, 0, :], -1e-4, None, ALU.min))
                put(pool.tensor_copy(li, lam[:, 1, :]))
                put(pool.tensor_tensor(t2, lr, dt, ALU.mult))
                exp(mag, t2, kk, t1, rr)
                put(pool.tensor_tensor(th, li, dt, ALU.mult))
                nearest(kk, th, 1 / (2 * math.pi))
                c1 = 6.28125
                c2 = float(np.float32(round((2 * math.pi - c1) * 2 ** 20) / 2 ** 20))
                less(rr, th, kk, (c1, c2, 2 * math.pi - c1 - c2), t1)
                put(pool.tensor_scalar(rr, rr, 0.25, None, ALU.mult))
                put(pool.tensor_tensor(t2, rr, rr, ALU.mult))
                poly(co, t2, [(-1) ** n / math.factorial(2 * n) for n in range(7)])
                poly(si, t2, [(-1) ** n / math.factorial(2 * n + 1) for n in range(7)])
                put(pool.tensor_tensor(si, si, rr, ALU.mult))

                def double():
                    put(pool.tensor_tensor(t1, si, co, ALU.mult))
                    put(pool.tensor_tensor(t2, si, si, ALU.mult))
                    pool.tensor_scalar(si, t1, 2.0, None, ALU.mult)
                    put(pool.tensor_scalar(co, t2, -2.0, 1.0, ALU.mult, ALU.add))
                double()
                double()
                pool.tensor_tensor(Pr[:, 1, :], mag, co, ALU.mult)
                put(pool.tensor_tensor(Pi[:, 1, :], mag, si, ALU.mult))
                for m in (1, 2, 4):
                    q4 = [prod[0][:, n * 64:n * 64 + m * G].rearrange("p (j g) -> p j g", j=m) for n in range(4)]
                    br, bi = [v[:, m:m + 1, :].broadcast_to((P, m, G)) for v in (Pr, Pi)]
                    cmul(Pr[:, m + 1:2 * m + 1, :], Pi[:, m + 1:2 * m + 1, :], Pr[:, 1:m + 1, :], Pi[:, 1:m + 1, :], br, bi, *q4)
                pool.tensor_tensor(t1, lr, lr, ALU.mult)
                put(pool.tensor_tensor(t2, li, li, ALU.mult))
                pool.tensor_tensor(den, t1, t2, ALU.add).then_inc(s["den"], 1)
                pool.wait_ge(s["rden"], 1)
                put(pool.tensor_scalar(t3, Pr[:, 1, :], -1.0, None, ALU.add))
                put(pool.tensor_scalar(t4, li, -1.0, None, ALU.mult))
                cmul(fr, fi, t3, Pi[:, 1, :], lr, t4, t1, t2, dt, rr)
                pool.tensor_tensor(fr, fr, den, ALU.mult)
                put(pool.tensor_tensor(fi, fi, den, ALU.mult))
                put(pool.tensor_tensor(Yb, Yb, sgn[:, 1:2].unsqueeze(2).broadcast_to((P, G, C)), ALU.mult))
                frb, fib = [v.unsqueeze(2).broadcast_to((P, G, C)) for v in (fr, fi)]
                q4 = [prod[0][:, n * 256:(n + 1) * 256].rearrange("p (g c) -> p g c", g=G) for n in range(4)]
                pool.tensor_tensor(q4[0], frb, Xb, ALU.mult)
                pool.tensor_tensor(q4[1], fib, Yb, ALU.mult)
                pool.tensor_tensor(q4[2], frb, Yb, ALU.mult)
                put(pool.tensor_tensor(q4[3], fib, Xb, ALU.mult))
                pool.tensor_tensor(Bb, q4[0], q4[1], ALU.add)
                put(pool.tensor_tensor(BY, q4[2], q4[3], ALU.subtract))

                def over(v, n, lo=0):
                    return v[:, lo:lo + n, :].rearrange("p j g -> p g j").unsqueeze(3).broadcast_to((P, G, n, C))

                def along(v, n):
                    return v.unsqueeze(2).broadcast_to((P, G, n, C))

                def mix(dst, v, w, op, lo, n, half):
                    g0, g1 = half * G // 2, (half + 1) * G // 2
                    q = [prod[0][:, a * 1024:a * 1024 + (G // 2) * n * C].rearrange("p (g j c) -> p g j c", g=G // 2, j=n) for a in range(2)]
                    pool.tensor_tensor(q[0], over(Pr, n, lo)[:, g0:g1], along(v, n)[:, g0:g1], ALU.mult)
                    put(pool.tensor_tensor(q[1], over(Pi, n, lo)[:, g0:g1], along(w, n)[:, g0:g1], ALU.mult))
                    put(pool.tensor_tensor(dst[:, g0:g1, lo:lo + n, :], q[0], q[1], op))
                for half in range(2):
                    mix(SBn, Bb, BY, ALU.add, 0, LC, half)
                    for lo, n in ((0, 8), (8, 1)):
                        mix(LL1, CX, CY, ALU.add, lo, n, half)
                        mix(LL2, CY, CX, ALU.subtract, lo, n, half)
                for _ in range(3):
                    double()
                put(pool.tensor_tensor(R8, mag, mag, ALU.mult))
                put(pool.tensor_tensor(R8, R8, R8, ALU.mult))
                put(pool.tensor_tensor(R8, R8, R8, ALU.mult))
                for m in (1, 2, 4, 8, 16, 32, 64):
                    n = min(m, 16)
                    for at in range(0, m, n):
                        q4 = [prod[0][:, a * 256:a * 256 + n * G].rearrange("p (g k) -> p g k", g=G) for a in range(4)]
                        br, bi = [v.unsqueeze(2).broadcast_to((P, G, n)) for v in (co, si)]
                        cmul(Ec[:, :, m + at:m + at + n], Es[:, :, m + at:m + at + n], Ec[:, :, at:at + n], Es[:, :, at:at + n], br, bi, *q4)
                    if m < 64:
                        double()
                pool.wait_ge(s["vcent"], NT)
                pool.tensor_tensor(prod[0].rearrange("p (t c) -> p t c", t=NT), ZG[:, :, SG:], ZG[:, :, SG:], ALU.mult).then_inc(s["vsq"], 1)

            @block.scalar
            def _(act):
                for n, (h, i) in enumerate(steps + [(0, 0)]):
                    if n < len(steps):
                        w = (i + 1) * P
                        act.wait_ge(s["nmax"], n + 1)
                        if n >= 2:
                            act.wait_ge(s["pt_psum"], n - 1)
                        act.activation(Pb[n % 2][:, 0:w], PS[:, 2 * (n % 2):2 * (n % 2) + 2, :].rearrange("p b n -> p (b n)")[:, 0:w],
                                       ACT.Exp, bias=stat[:, n % 4:n % 4 + 1], accum_out=stat[:, 4 + n % 4:5 + n % 4]).then_inc(s["exp"], 1)
                    if n >= 1:
                        i = steps[n - 1][1]
                        act.wait_ge(s["pt_psum"], n)
                        if n >= 3:
                            act.wait_ge(s["o_psum"], n - 2)
                        if i >= 4:
                            act.activation(PTb[(n - 1) % 2][:, 512:(i + 1) * P], PS[:, 5, 0:(i - 3) * P], ACT.Copy).then_inc(s["pta"], 1)

            @block.vector
            def _(dve):
                for n in range(len(steps) + 2):
                    if n < len(steps):
                        h, i = steps[n]
                        sc = PS[:, 2 * (n % 2):2 * (n % 2) + 2, :].rearrange("p b n -> p (b n)")
                        dve.wait_ge(s["s_psum"], n + 1)
                        link(dve, "pdve", dve.tensor_tensor(sc[:, i * P:(i + 1) * P], sc[:, i * P:(i + 1) * P], tril, ALU.add))
                        dve.tensor_reduce(stat[:, n % 4:n % 4 + 1], sc[:, 0:(i + 1) * P], AX.X, ALU.max, negate=True).then_inc(s["nmax"], 1)
                    if 1 <= n <= len(steps):
                        i = steps[n - 1][1]
                        dve.wait_ge(s["pt_psum"], n)
                        if n >= 3:
                            dve.wait_ge(s["o_psum"], n - 2)
                        w = min(i + 1, 4) * P
                        dve.tensor_copy(PTb[(n - 1) % 2][:, 0:w], PS[:, 4, 0:w]).then_inc(s["ptd"], 1)
                    if n >= 2:
                        m = n - 2
                        h, i = steps[m]
                        rs = stat[:, 8 + m % 2:9 + m % 2]
                        link(dve, "pdve", dve.reciprocal(rs, stat[:, 4 + m % 4:5 + m % 4]))
                        dve.wait_ge(s["o_psum"], m + 1)
                        dve.tensor_scalar(O[:, i, h * VD:(h + 1) * VD], PS[:, 6 + m % 2, (h % 2) * VD:(h % 2 + 1) * VD],
                                          rs, None, ALU.mult).then_inc(s["o"], 1)
                    if n % 6 == 3 and n // 6 >= 1 and n // 6 <= NT:
                        v4 = ZG[:, n // 6 - 1, SG:].rearrange("p (g c) -> p g c", g=SGG)
                        mean = vst[:, (n // 6 - 1) * SGG:(n // 6) * SGG]
                        link(dve, "pdve", dve.tensor_reduce(mean, v4, AX.X, ALU.add))
                        link(dve, "pdve", dve.tensor_scalar(mean, mean, 1.0 / 64, None, ALU.mult))
                        dve.tensor_tensor(v4, v4, mean.unsqueeze(2).broadcast_to((P, SGG, 64)), ALU.subtract).then_inc(s["vcent"], 1)
                    if n == PAR:
                        dve.wait_ge(s["par_psum"], 1)
                        dve.wait_ge(s["sgn"], 1)
                        dve.tensor_copy(lam.rearrange("p a g -> p (a g)"), PS[:, 6, 0:3 * G])
                        dve.tensor_scalar(CX.rearrange("p g c -> p (g c)"), PS[:, 6, 128:384], sgn[:, 0:1], None, ALU.mult)
                        dve.tensor_scalar(CY.rearrange("p g c -> p (g c)"), PS[:, 7, 0:256], -1.0, None, ALU.mult).then_inc(s["par"], 1)
                    if n == 24:
                        dve.wait_ge(s["den"], 1)
                        dve.reciprocal(den, den).then_inc(s["rden"], 1)

            @block.tensor
            def _(pe):
                def parameters():
                    pe.wait_ge(s["o"], PAR - 1)
                    pe.wait_ge(s["par_loaded"], 16 * 14)
                    pe.transpose(PS[:, 6, 0:3 * G], rows3[0:3 * G, :], ident[0:3 * G, 0:3 * G])
                    for a in range(2):
                        for f in range(2):
                            last = pe.transpose(PS[:, 6 + a, (1 - a) * P + f * P:(2 - a) * P + f * P], cnat[:, a, f, :], ident[:, :])
                    last.then_inc(s["par_psum"], 1)

                def scores(n):
                    h, i = steps[n]
                    sc = PS[:, 2 * (n % 2):2 * (n % 2) + 2, :].rearrange("p b n -> p (b n)")
                    if n >= 2:
                        pe.wait_ge(s["exp"], n - 1)
                    for at in range(0, (i + 1) * P, 512):
                        to = min(at + 512, (i + 1) * P)
                        last = pe.matmul(sc[:, at:to], QT[0:QK, h, i * P:(i + 1) * P], KT[0:QK, h, at:to], start=True, stop=True)
                    last.then_inc(s["s_psum"], 1)

                def flip(n):
                    h, i = steps[n]
                    pe.wait_ge(s["exp"], n + 1)
                    if n >= 1:
                        pe.wait_ge(s["ptd"], n)
                        if n >= 5:
                            pe.wait_ge(s["pta"], wide(n))
                    for j in range(i + 1):
                        last = pe.transpose(PS[:, 4 + j // 4, (j % 4) * P:(j % 4 + 1) * P], Pb[n % 2][:, j * P:(j + 1) * P], ident[:, :])
                    last.then_inc(s["pt_psum"], 1)

                def values(n):
                    h, i = steps[n]
                    pe.wait_ge(s["ptd"], n + 1)
                    if i >= 4:
                        pe.wait_ge(s["pta"], wide(n + 1))
                    if n == PAR - 1:
                        pe.wait_ge(s["par"], 1)
                    if n >= 2:
                        pe.wait_ge(s["o"], n - 1)
                    a = h // 2 * 2 * VD
                    for j in range(i + 1):
                        last = pe.matmul(PS[:, 6 + n % 2, 0:2 * VD], PTb[n % 2][:, j * P:(j + 1) * P], V[:, j, a:a + 2 * VD],
                                         start=j == 0, stop=j == i)
                    last.then_inc(s["o_psum"], 1)

                scores(0)
                for n in range(len(steps) + 1):
                    if n + 1 < len(steps):
                        scores(n + 1)
                    if n < len(steps):
                        flip(n)
                    if n == PAR:
                        parameters()
                    if n >= 1:
                        values(n - 1)

        slot = [RQKV[:, n * 2048:(n + 1) * 2048] for n in range(10)]
        ZS = slot[0].rearrange("p (t c) -> p t c", t=NT)
        XT = slot[1].rearrange("p (f n) -> p f n", f=2)
        X = slot[2].rearrange("p (g k) -> p g k", g=G)
        TT = slot[3].rearrange("p (g n) -> p g n", g=G)
        ST = slot[4].rearrange("p (g n) -> p g n", g=G)
        SX = slot[5].rearrange("p (g n) -> p g n", g=G)
        M = slot[6].rearrange("p (g k) -> p g k", g=G)
        X1 = slot[7].rearrange("p (g k) -> p g k", g=G)
        X2 = slot[8].rearrange("p (g k) -> p g k", g=G)
        Kt = slot[9][0:C, :].rearrange("p (g n) -> p g n", g=G)
        Y = slot[0].rearrange("p (g k) -> p g k", g=G)
        GT = slot[1].rearrange("p (f n) -> p f n", f=2)
        SIG = slot[6].rearrange("p (f n) -> p f n", f=2)
        sT = slot[7].rearrange("p (f n) -> p f n", f=2)
        wsn = R2[:, 0:512].rearrange("p (g n) -> p g n", g=SGG)
        wsT = R2[:, 512:1024].rearrange("p (g n) -> p g n", g=SGG)
        wglu = R2[:, 1024:1536].rearrange("p (f n) -> p f n", f=2)
        keep = R2[:, 1536:1664]
        dT = R2[0:C, 1664:1680]
        dg = R2[0:C, 1680:1936].rearrange("p (g c) -> p g c", g=G)
        tmp = R2[:, 6144:8192]
        t8 = R2[:, 8192:9216].rearrange("p (g k) -> p g k", g=8)
        u_ = ZG[:, :, 0:SG]
        wout = R2[:, 0:8192].rearrange("p (k n) -> p k n", k=KD)
        wout_lo = R2_r[:, 0:8192].rearrange("p (k n) -> p k n", k=KD)
        wout_loaded = [sem("wout_loaded%d" % k) for k in range(0, KD, 2)]
        wout_hi = RQKV_r[:, 4096:12288].rearrange("p (k n) -> p k n", k=KD)

        def load_wout(eng, k):
            eng.dma_start(wout[:, k:k + 2, :], w_out[k * P:(k + 2) * P].rearrange("(k p) n -> p k n", p=P)).then_inc(wout_loaded[k // 2], 16)

        def high_wout(act, k):
            act.wait_ge(wout_loaded[k // 2], 16)
            return act.activation(wout_hi[:, k, :], wout[:, k, :], ACT.Copy, scale=vec("g_mix")[:, k:k + 1])

        def low_wout(dve, k):
            return dve.scalar_tensor_tensor(wout_lo[:, k, :], wout[:, k, :], vec("g_mix")[:, k:k + 1],
                                            wout_hi[:, k, :].bitcast(fp32), ALU.mult, ALU.subtract)
        signals("s", ("kt_a", "w_hi", "w_lo", "ws_loaded", "xt_psum", "xt0", "xt1", "sb_psum", "st_v", "st_a", "ws_psum", "wsT", "kt_psum",
                  "kt", "xs_stored", "x_loaded", "tt_loaded", "tt_zero", "vvar", "vrms", "vn", "mix_psum", "mixed",
                  "s_psum", "m", "scan", "x1", "x2", "y_psum", "y", "ys_stored", "yt_loaded", "gt", "glu_psum", "sig", "st",
                  "dve", "pool", "keep"), "s")

        xs_v = xs_d.rearrange("(g c) j k -> j c g k", c=C)
        ys_v = ys_d.rearrange("(g c) j k -> j c g k", c=C)

        def load_x(eng, a):
            for j in range(a, LC, 2):
                q = LC - 1 - j
                eng.dma_start(X[q * C:(q + 1) * C, :, :], xs_v[j]).then_inc(s["sx_loaded"], 16)

        with nc.Block() as block:
            @block.sync
            def _(sp):
                sp.dma_start(wsn, sg_w.rearrange("g t s -> t g s")).then_inc(s["sws_loaded"], 16)
                sp.dma_start(wglu, w_glu.rearrange("(f p) n -> p f n", p=P)).then_inc(s["sws_loaded"], 16)
                sp.dma_start(dT, ssm_d.rearrange("g c -> c g"), allow_slow_non_contiguous=True).then_inc(s["sws_loaded"], 16)
                for f in range(2):
                    sp.wait_ge(s["sxt%d" % f], 1)
                    sp.dma_start(xs_d[f * P:(f + 1) * P].rearrange("c j k -> c (j k)"), XT[:, f, :]).then_inc(s["sxs_stored"], 16)
                sp.wait_ge(s["sxs_stored"], 32)
                load_x(sp, 0)
                load_wout(sp, 2)
                sp.wait_ge(s["ssb_psum"], 2)
                load_wout(sp, 4)
                sp.wait_ge(s["svvar"], 1)
                load_wout(sp, 6)
                sp.wait_ge(s["sy"], 2)
                for j in range(0, LC, 2):
                    sp.dma_start(ys_v[j], Y[j * C:(j + 1) * C, :, :]).then_inc(s["sys_stored"], 16)
                sp.wait_ge(s["sys_stored"], 16 * LC)
                sp.dma_start(GT, ys_d.rearrange("(f c) j k -> c f (j k)", f=2)).then_inc(s["syt_loaded"], 16)
                sp.wait_ge(s["syt_loaded"], 16)

            @block.gpsimd
            def _(pool):
                pool.memset(TT, 0.0).then_inc(s["stt_zero"], 1)
                link(pool, "spool", pool.memset(keep, 1.0))
                pool.affine_select(out=keep, in_=keep, compare_op=ALU.is_ge, fill=0.0, base=0,
                                   pattern=[[1, P]], channel_multiplier=-1).then_inc(s["skeep"], 1)
                pool.wait_ge(s["sscan"], G // 2)
                pool.tensor_tensor(X2[:, 0:8, :], M[:, 0:8, :], Es[:, 0:8, :], ALU.mult).then_inc(s["sx2"], 1)

            @block.scalar
            def _(act):
                act.wait_ge(s["stt_zero"], 1)
                act.wait_ge(s["sxt_psum"], 2)
                act.activation(XT[:, 1, :].rearrange("p (j k) -> p k j", j=LC),
                               PS[:, 2:4, :].rearrange("p b (k j) -> p (b k) j", j=LC), ACT.Copy).then_inc(s["sxt1"], 1)
                for h in range(2):
                    act.wait_ge(s["ssb_psum"], h + 1)
                    act.activation(ST[:, h * 8:(h + 1) * 8, :], PS[:, 4 + 2 * h:6 + 2 * h, :].rearrange("p b (g n) -> p (b g) n", n=P),
                                   ACT.Copy).then_inc(s["sst_a"], 1)
                act.wait_ge(s["svvar"], 1)
                act.activation(vst[:, 32:64], vst[:, 0:32], ACT.Sqrt, bias=eps[:, :], scale=1.0 / 64).then_inc(s["svrms"], 1)
                act.wait_ge(s["sxs_stored"], 32)
                load_x(act, 1)
                act.wait_ge(s["skt_psum"], 1)
                act.activation(Kt.rearrange("p (b g) n -> p b (g n)", b=4), PS[0:C, 4:8, :], ACT.Copy).then_inc(s["skt_a"], 1)
                act.wait_ge(s["skt"], 1)
                for j in range(LC):
                    r = (LC - 1 - j) * C
                    act.dma_start(TT[r:r + C, :, j * C:], Kt[:, :, 0:(LC - j) * C]).then_inc(s["stt_loaded"], 16)
                act.wait_ge(s["sy"], 2)
                for j in range(1, LC, 2):
                    act.dma_start(ys_v[j], Y[j * C:(j + 1) * C, :, :]).then_inc(s["sys_stored"], 16)
                for k in range(2, KD):
                    high_wout(act, k).then_inc(s["sw_hi"], 1)
                act.wait_ge(s["syt_loaded"], 16)
                act.activation(GT, GT, ACT.Gelu_apprx_tanh).then_inc(s["sgt"], 1)
                bg = vec("b_glu")
                for m in range(2):
                    act.wait_ge(s["sglu_psum"], m + 1)
                    act.activation(SIG[:, m, :].rearrange("p (b n) -> p b n", b=2), PS[:, 4 + 2 * m:6 + 2 * m, :], ACT.Sigmoid,
                                   bias=bg[:, m:m + 1]).then_inc(s["ssig"], 1)
                act.activation(stat[:, 90:91], eps[:, :], ACT.Sqrt)
                act.wait_ge(s["stt_loaded"], 16 * LC)

            @block.vector
            def _(dve):
                dve.wait_ge(s["sxt_psum"], 1)
                dve.tensor_copy(XT[:, 0, :].rearrange("p (j k) -> p k j", j=LC),
                                PS[:, 0:2, :].rearrange("p b (k j) -> p (b k) j", j=LC)).then_inc(s["sxt0"], 1)
                v4 = ZG[:, :, SG:].rearrange("p t (g c) -> p t g c", g=SGG)
                mean, ss = vst[:, 32:64], vst[:, 0:32]

                def b4(v):
                    return v.rearrange("p (t g) -> p t g", t=NT).unsqueeze(3).broadcast_to((P, NT, SGG, 64))
                dve.tensor_reduce(ss.rearrange("p (t g) -> p t g", t=NT), tmp.rearrange("p (t g c) -> p t g c", t=NT, g=SGG),
                                  AX.X, ALU.add).then_inc(s["svvar"], 1)
                for h in range(2):
                    dve.wait_ge(s["ssb_psum"], h + 1)
                    dve.wait_ge(s["sst_a"], h + 1)
                    t3 = PS[:, 4 + 2 * h:6 + 2 * h, :].rearrange("p b (g n) -> p (b g) n", n=P)
                    dve.tensor_copy(SX[:, h * 8:(h + 1) * 8, 0:NS], t3[:, :, NS:])
                    dve.tensor_scalar(SX[:, h * 8:(h + 1) * 8, NS:], t3[:, :, 0:NS], -1.0, None, ALU.mult).then_inc(s["sst_v"], 1)
                dve.wait_ge(s["svrms"], 1)
                link(dve, "sdve", dve.reciprocal(mean, mean))
                link(dve, "sdve", dve.tensor_tensor(v4, v4, b4(mean), ALU.mult))
                v3 = ZG[:, :, SG:]
                gb, bb = [sgv[:, a:a + SG].unsqueeze(1).broadcast_to((P, NT, SG)) for a in (0, SG)]
                link(dve, "sdve", dve.tensor_tensor(v3, v3, gb, ALU.mult))
                dve.tensor_tensor(v3, v3, bb, ALU.add).then_inc(s["svn"], 1)
                dve.wait_ge(s["sws_loaded"], 48)
                link(dve, "sdve", dve.tensor_tensor(dg, ident[0:C, 0:C].unsqueeze(1).broadcast_to((C, G, C)),
                                                    dT.unsqueeze(2).broadcast_to((C, G, C)), ALU.mult))
                dve.wait_ge(s["skt_a"], 1)
                dve.tensor_tensor(Kt[:, :, 0:C], Kt[:, :, 0:C], dg, ALU.add).then_inc(s["skt"], 1)
                dve.wait_ge(s["sws_psum"], 1)
                dve.wait_ge(s["skeep"], 1)
                dve.tensor_tensor(wsT, PS[:, 0, :].rearrange("p (g n) -> p g n", g=SGG), keep.unsqueeze(1).broadcast_to((P, SGG, P)),
                                  ALU.mult).then_inc(s["swsT"], 1)
                for h in range(2):
                    b = (4, 0)[h]
                    dve.wait_ge(s["ss_psum"], h + 1)
                    dve.tensor_tensor(t8, PS[:, b + 2:b + 4, :].rearrange("p b (g k) -> p (b g) k", k=NC), Es[:, 8 * h:8 * h + 8, :], ALU.mult)
                    link(dve, "sdve", dve.tensor_tensor(M[:, 8 * h:8 * h + 8, :], PS[:, b:b + 2, :].rearrange("p b (g k) -> p (b g) k", k=NC),
                                                        Ec[:, 8 * h:8 * h + 8, :], ALU.mult))
                    link(dve, "sm", dve.tensor_tensor(M[:, 8 * h:8 * h + 8, :], M[:, 8 * h:8 * h + 8, :], t8, ALU.add))
                    for g in range(8 * h, 8 * h + 8):
                        ins = dve.tensor_tensor_scan(M[:, g, :], R8[:, g:g + 1].broadcast_to((P, NC)), M[:, g, :], 0.0, ALU.mult, ALU.add)
                        ins.then_inc(s["sscan"], 1)
                    dve.wait_ge(s["sscan"], 8 * h + 8)
                    dve.tensor_tensor(X1[:, 8 * h:8 * h + 8, :], M[:, 8 * h:8 * h + 8, :], Ec[:, 8 * h:8 * h + 8, :], ALU.mult).then_inc(s["sx1"], 1)
                dve.tensor_tensor(X2[:, 8:, :], M[:, 8:, :], Es[:, 8:, :], ALU.mult).then_inc(s["sx1"], 1)
                for h in range(2):
                    dve.wait_ge(s["sy_psum"], h + 1)
                    dve.tensor_copy(Y[:, 8 * h:8 * h + 8, :], PS[:, 4 + 2 * h:6 + 2 * h, :].rearrange("p b (g k) -> p (b g) k", k=NC)).then_inc(s["sy"], 1)
                for k in range(2, 4):
                    dve.wait_ge(s["sw_hi"], k - 1)
                    low_wout(dve, k).then_inc(s["sw_lo"], 1)
                for g in range(SGG):
                    dve.wait_ge(s["smix_psum"], g + 1)
                    ug = u_[:, :, g * 64:(g + 1) * 64]
                    dve.scalar_tensor_tensor(ug, PS[:, g, :].rearrange("p (t c) -> p t c", t=NT), vec("sg_b")[:, g:g + 1], ug,
                                             ALU.add, ALU.mult).then_inc(s["smixed"], 1)
                for k in range(4, KD):
                    dve.wait_ge(s["sw_hi"], k - 1)
                    low_wout(dve, k).then_inc(s["sw_lo"], 1)
                for m in range(2):
                    dve.wait_ge(s["ssig"], m + 1)
                    dve.tensor_tensor(sT[:, m, :].rearrange("p (k j) -> p j k", j=LC), GT[:, m, :].rearrange("p (j k) -> p j k", j=LC),
                                      SIG[:, m, :].rearrange("p (j k) -> p j k", j=LC), ALU.mult).then_inc(s["sst"], 1)

            @block.tensor
            def _(pe):
                pe.wait_ge(zs_loaded, 16)
                for f in range(2):
                    for t in range(NT):
                        last = pe.transpose(PS[:, 2 * f + t // 4, (t % 4) * P:(t % 4 + 1) * P], ZS[:, t, f * P:(f + 1) * P], ident[:, :])
                    last.then_inc(s["sxt_psum"], 1)
                for h in range(2):
                    for g in range(8 * h, 8 * h + 8):
                        last = pe.transpose(PS[:, 4 + g // 4, (g % 4) * P:(g % 4 + 1) * P], SBn[:, g].rearrange("p q c -> p (q c)"), ident[:, :])
                    last.then_inc(s["ssb_psum"], 1)
                pe.wait_ge(s["sst_v"], 2)
                pe.wait_ge(s["sst_a"], 2)
                for g in range(G):
                    last = pe.matmul(PS[0:C, 4 + g // 4, (g % 4) * P:(g % 4 + 1) * P], Bb[:, g, :], LL1[:, g, 0:LC, :].rearrange("p j c -> p (j c)"),
                                     start=True, stop=True)
                last.then_inc(s["skt_psum"], 1)
                pe.wait_ge(s["sws_loaded"], 48)
                pe.wait_ge(s["sxt0"], 1)
                for g in range(SGG):
                    last = pe.transpose(PS[:, 0, g * P:(g + 1) * P], wsn[:, g, :], ident[:, :])
                last.then_inc(s["sws_psum"], 1)
                pe.wait_ge(s["sx_loaded"], 16 * LC)
                pe.wait_ge(s["skt_a"], 1)

                def states(h):
                    b = (4, 0)[h]
                    for w, at in ((ST, b), (SX, b + 2)):
                        for g in range(8 * h, 8 * h + 8):
                            last = pe.matmul(PS[:, at + g % 8 // 4, (g % 4) * P:(g % 4 + 1) * P], w[:, g, :], X[:, g, :], start=True, stop=True)
                    last.then_inc(s["ss_psum"], 1)
                states(0)
                pe.wait_ge(s["swsT"], 1)
                pe.wait_ge(s["sxt1"], 1)
                states(1)
                pe.wait_ge(s["stt_loaded"], 16 * LC)
                pe.wait_ge(s["sx2"], 1)
                for g in range(G):
                    pe.wait_ge(s["sx1"], 1 if g < G // 2 else 3)
                    o_ = PS[:, 4 + g // 4, (g % 4) * P:(g % 4 + 1) * P]
                    pe.matmul(o_, TT[:, g, :], X[:, g, :], start=True, stop=False)
                    pe.matmul(o_[:, 1:], LL1[:, g, 1:, :].rearrange("p j c -> p (j c)"), X1[:, g, 0:NC - 1], start=False, stop=False)
                    last = pe.matmul(o_[:, 1:], LL2[:, g, 1:, :].rearrange("p j c -> p (j c)"), X2[:, g, 0:NC - 1], start=False, stop=True)
                    if g % 8 == 7:
                        last.then_inc(s["sy_psum"], 1)
                pe.wait_ge(s["sys_stored"], 16 * LC)
                pe.wait_ge(s["svn"], 1)
                pe.wait_ge(s["sm"], 2)
                for g in range(SGG):
                    last = pe.matmul(PS[:, g, :].rearrange("p (t c) -> p t c", t=NT), wsT[:, g, :], ZG[:, :, SG + g * 64:SG + (g + 1) * 64],
                                     start=True, stop=True)
                    last.then_inc(s["smix_psum"], 1)
                pe.wait_ge(s["sgt"], 1)
                pe.wait_ge(s["sy"], 2)
                for m in range(2):
                    for b in range(2):
                        for f in range(2):
                            last = pe.matmul(PS[:, 4 + 2 * m + b, :], wglu[:, f, m * P:(m + 1) * P], GT[:, f, b * 512:(b + 1) * 512],
                                             start=f == 0, stop=f == 1)
                    last.then_inc(s["sglu_psum"], 1)

        h = R1[:, 0:8192].rearrange("p (t c) -> p t c", t=NT)
        hn = [R1[:, 8192:9216], R1[:, 9216:10240]]
        junk = R1[:, 10240:10752].bitcast(bf16)
        wr = R1[:, 10752:11040].rearrange("p (k n) -> p k n", k=KD)
        upper = R1[:, 11040:11168]
        ones = R1[:, 11168:11296]
        mixn = [slot[6][:, 0:1024], slot[6][:, 1024:2048]]
        mixT_hi, mixT_lo = [[RQKV_r[:, a:a + D] for a in (2048 * n, 2048 * n + D)] for n in (8, 1)]
        ptile = [R2[:, 8192 + t * PLE:8192 + (t + 1) * PLE] for t in range(7)] + [sgv[:, 0:PLE]]
        pT = slot[8].rearrange("p (t c) -> p t c", t=NT)
        wple = slot[7].rearrange("p (k n) -> p k n", k=2)
        ple = R3[:, :].rearrange("p (t c) -> p t c", t=NT)
        PLE_EARLY, PLE_LATE = 3, 5

        def ple_product(pe, t, bank):
            for b in range(2):
                for k in range(2):
                    last = pe.matmul(PS[:, bank + b, :], pT[:, t, k * P:(k + 1) * P], wple[:, k, b * 512:(b + 1) * 512],
                                     start=k == 0, stop=k == 1)
            return last
        hnT = [slot[9][:, 0:1024], slot[9][:, 1024:2048]]
        ring = [RQKV[:, u * 6144:(u + 1) * 6144] for u in range(2)]
        w13r = [r[:, 0:4096].rearrange("p (k a n) -> p k a n", k=KD, a=2) for r in ring]
        w2r = [r[:, 4096:].rearrange("p (k n) -> p k n", k=2) for r in ring]
        sm2 = sb("sm2", [P, 740])
        c2_ = [0]

        def t2(n):
            c2_[0] += n
            return sm2[:, c2_[0] - n:c2_[0]]
        e_id, e_grp, e_base = t2(E), t2(E), t2(E)
        tokid = t2(2 * NT).rearrange("p (c t) -> p c t", c=2)
        rbias = t2(EG + E)
        lg = t2(8 + E)
        g8, v8 = t2(8), t2(8)
        gi, vi = t2(8).bitcast(u32), t2(8).bitcast(u32)
        gs, i12 = t2(1), t2(2)
        gm, em, o1, o2, mm, rk_, pr1, msum = [t2(E) for _ in range(8)]
        gdiff = t2(NT * EG).rearrange("p (t g) -> p t g", t=NT)
        vdiff = t2(NT)
        slots_f = t2(2 * NT).rearrange("p (t c) -> p t c", t=NT)
        gsum, wsum = t2(NT), t2(NT)
        from_, to_ = t2(E).bitcast(u32), t2(E).bitcast(u32)
        idf, idg = small[:, 1040:1072], t2(E)
        tokrow = small[:, 1072:1200]
        tab = small[:, 1200:1232].bitcast(i32)
        cnt, nov, cum = [small[:, a:a + E] for a in (1232, 1264, 1296)]
        ej, bj, jj = [small[:, a:a + OVER] for a in (1328, 1344, 1360)]
        signals("d", tuple("x_loaded%d" % t for t in range(NT)) + ("w_hi", "w_lo", "mixT_hi", "p_loaded", "wple_loaded", "pT_psum", "pT", "ple_psum", "ple", "wr_loaded", "const", "tok_zero", "s_tr", "mix_ss", "mix_rms", "mixn", "mix_tr", "mixT", "h_psum",
                  "h", "h_ss", "h_rms", "h_rstd", "hn", "xf_stored0", "xf_stored1", "hn_tr", "hnT", "lg_psum", "lg", "mask", "rank_psum", "dest",
                  "tok_stored", "tok_loaded", "tok_tr", "idx", "gexp", "pool", "dve", "msum", "zero"), "d")
        wa_loaded = [sem("w13_loaded%d" % u) for u in range(2)]
        wb_loaded = [sem("w2_loaded%d" % u) for u in range(2)]

        def load_w13(eng, e, u):
            eng.dma_start(w13r[u][:, :, 0, :], w1[e].rearrange("(k p) n -> p k n", p=P)).then_inc(wa_loaded[u], 16)
            eng.dma_start(w13r[u][:, :, 1, :], w3[e].rearrange("(k p) n -> p k n", p=P)).then_inc(wa_loaded[u], 16)

        def load_w2(eng, e, u):
            eng.dma_start(w2r[u], w2[e].rearrange("(k p) n -> p k n", p=P)).then_inc(wb_loaded[u], 16)

        with nc.Block() as block:
            @block.sync
            def _(sp):
                load_wout(sp, 0)
                sp.dma_start(wr[:, :, 0:EG], w_rg.rearrange("(k p) n -> p k n", p=P)).then_inc(s["dwr_loaded"], 16)
                sp.dma_start(wr[:, :, EG:], w_rexp.rearrange("(k p) n -> p k n", p=P)).then_inc(s["dwr_loaded"], 16)
                sp.dma_start(rbias[:, 0:EG], row_bcast(b_rg)).then_inc(s["dwr_loaded"], 16)
                sp.dma_start(rbias[:, EG:], row_bcast(b_rexp)).then_inc(s["dwr_loaded"], 16)
                for t in range(NT):
                    sp.dma_start(h[:, t, :], x[t * P:(t + 1) * P, :]).then_inc(s["dx_loaded%d" % t], 16)
                for t in range(NT):
                    sp.dma_start(ptile[t], p[t * P:(t + 1) * P, :]).then_inc(s["dp_loaded"], 16)
                for t in range(NT):
                    if t == NT - 1:
                        sp.wait_ge(s["ds_tr"], NT)
                        sp.dma_start(wple, w_ple.rearrange("(k p) n -> p k n", p=P)).then_inc(s["dwple_loaded"], 16)
                        sp.wait_ge(s["dh_psum"], NT)
                        sp.wait_ge(s["dtok_zero"], 16)
                        load_w13(sp, 0, 0)
                        load_w2(sp, 0, 0)
                    sp.wait_ge(s["dhn"], t + 1)
                    sp.dma_start(xf_d[t * P:(t + 1) * P, :], hn[t % 2]).then_inc(s["dxf_stored%d" % (t % 2)], 16)
                load_w13(sp, 1, 1)
                load_w2(sp, 1, 1)
                sp.wait_ge(s["dtok_stored"], 16 * 2 * NT)
                sp.dma_start(tokrow[0:E, :], tok_d.rearrange("(e s) o -> e (s o)", e=E)[:, 0:P]).then_inc(s["dtok_loaded"], 16)
                sp.wait_ge(s["dtok_loaded"], 16)
                for u in range(2):
                    sp.wait_ge(s["dxf_stored%d" % u], 16 * (NT // 2))

            @block.gpsimd
            def _(pool):
                link(pool, "dzero", pool.iota(slot[0][:, 0:256], pattern=[[0, 2], [1, P]], base=2 * S, channel_multiplier=0,
                                              allow_small_or_imprecise_dtypes=True))
                pool.dma_start(tok_d.rearrange("(p n) o -> p (n o)", p=P), slot[0][:, 0:256]).then_inc(s["dtok_zero"], 16)
                pool.iota(e_id, pattern=[[1, E]], base=0, channel_multiplier=0, allow_small_or_imprecise_dtypes=True)
                pool.iota(e_grp, pattern=[[1, EG], [0, EPG]], base=0, channel_multiplier=0, allow_small_or_imprecise_dtypes=True)
                pool.iota(e_base, pattern=[[S, E]], base=0, channel_multiplier=0, allow_small_or_imprecise_dtypes=True)
                pool.iota(tokid, pattern=[[S, 2], [P, NT]], base=0, channel_multiplier=1, allow_small_or_imprecise_dtypes=True)
                pool.iota(jj, pattern=[[1, OVER]], base=0, channel_multiplier=0, allow_small_or_imprecise_dtypes=True)
                pool.memset(lg, NEG)
                pool.memset(msum, 0.0)
                link(pool, "dpool", pool.memset(upper, 1.0))
                pool.affine_select(out=upper, in_=upper, compare_op=ALU.is_gt, fill=0.0, base=0, pattern=[[1, P]], channel_multiplier=-1)
                pool.memset(ones, 1.0).then_inc(s["dconst"], 1)
                pool.wait_ge(s["dtok_zero"], 16)
                for t in range(NT):
                    if t == NT - 1:
                        pool.wait_ge(s["dh_psum"], NT)
                        link(pool, "dpool", pool.memset(R2[:, 0:2 * D], 0.0))
                    for c in range(2):
                        pool.wait_ge(s["ddest"], t + 1)
                        pool.indirect_dma_start(tok_d, bass.IndirectOffsetOnAxis(ap=dest[:, t, c:c + 1], axis=0),
                                                tokid[:, c, t:t + 1], None).then_inc(s["dtok_stored"], 16)
                pool.wait_ge(s["dtok_stored"], 16 * 2 * NT)

            @block.scalar
            def _(act):
                def mix_high(t):
                    act.wait_ge(s["dmix_tr"], t + 1)
                    if t >= 2:
                        act.wait_ge(s["dh_psum"], t - 1)
                    act.activation(mixT_hi[t % 2].rearrange("p (b n) -> p b n", b=2), PS[:, 0:2, :], ACT.Copy).then_inc(s["dmixT_hi"], 1)

                def mix_squares(t):
                    a = 3 * (t % 2)
                    act.activation(junk[:, 0:512], O[:, t, :], ACT.Square, accum_out=stat[:, a:a + 1])
                    act.activation(junk[:, 512:768], ZG[:, t, 0:SG], ACT.Square, accum_out=stat[:, a + 1:a + 2])
                    act.wait_ge(s["ds_tr"], t + 1)
                    link(act, "dmix_ss", act.activation(junk[:, 768:1024], PS[:, 2, 0:256], ACT.Square, accum_out=stat[:, a + 2:a + 3]))
                    act.activation(stat[:, 6 + a:7 + a], stat[:, a:a + 1], ACT.Sqrt, bias=eps, scale=1.0 / 512)
                    act.activation(stat[:, 7 + a:9 + a], stat[:, a + 1:a + 3], ACT.Sqrt, bias=eps, scale=1.0 / 256).then_inc(s["dmix_rms"], 1)

                mix_squares(0)
                mix_high(0)
                for k in range(2):
                    high_wout(act, k).then_inc(s["dw_hi"], 1)
                for t in range(NT):
                    if t + 1 < NT:
                        act.wait_ge(s["dmixn"], t + 1)
                        mix_squares(t + 1)
                    if t + 1 < NT:
                        mix_high(t + 1)
                    act.wait_ge(s["dh"], t + 1)
                    link(act, "dh_ss", act.activation(junk, h[:, t, :], ACT.Square, accum_out=stat[:, 16:17]))
                    act.activation(stat[:, 17:18], stat[:, 16:17], ACT.Sqrt, bias=eps, scale=1.0 / D).then_inc(s["dh_rms"], 1)
                    act.wait_ge(s["dh_rstd"], t + 1)
                    if t >= 2:
                        act.wait_ge(s["dxf_stored%d" % (t % 2)], 16 * (t // 2))
                        act.wait_ge(s["dhn_tr"], t - 1)
                    act.activation(hn[t % 2], h[:, t, :], ACT.Copy, scale=stat[:, 18:19]).then_inc(s["dhn"], 1)
                act.wait_ge(s["dpT_psum"], 1)
                act.activation(pT[:, 0:4, :].rearrange("p t c -> p (t c)").rearrange("p (b n) -> p b n", b=2), PS[:, 0:2, :], ACT.Copy).then_inc(s["dpT"], 1)
                act.wait_ge(s["dlg"], NT)
                act.activation(gdiff, gdiff, ACT.Exp)
                act.activation(vdiff, vdiff, ACT.Exp).then_inc(s["dgexp"], 1)
                act.wait_ge(s["dpT_psum"], 2)
                act.activation(pT[:, 4:8, :].rearrange("p t c -> p (t c)").rearrange("p (b n) -> p b n", b=2), PS[:, 5:7, :], ACT.Copy).then_inc(s["dpT"], 1)
                act.wait_ge(s["dmixn"], NT)
                for t in range(PLE_EARLY):
                    act.wait_ge(s["dple_psum"], t + 1)
                    b = (3, 0)[t % 2]
                    act.activation(ple[:, t, :].rearrange("p (b n) -> p b n", b=2), PS[:, b:b + 2, :], ACT.Copy).then_inc(s["dple"], 1)

            @block.vector
            def _(dve):
                def lk(ins):
                    link(dve, "ddve", ins)

                def mix_norm(t):
                    a = 3 * (t % 2)
                    dve.wait_ge(s["dmix_rms"], t + 1)
                    lk(dve.reciprocal(stat[:, 20:23], stat[:, 6 + a:9 + a]))
                    if t >= 2:
                        dve.wait_ge(s["dmix_tr"], t - 1)
                    dve.tensor_scalar(mixn[t % 2][:, 0:512], O[:, t, :], stat[:, 20:21], None, ALU.mult)
                    dve.tensor_scalar(mixn[t % 2][:, 512:768], ZG[:, t, 0:SG], stat[:, 21:22], None, ALU.mult)
                    dve.tensor_scalar(mixn[t % 2][:, 768:1024], PS[:, 2, 0:256], stat[:, 22:23], None, ALU.mult).then_inc(s["dmixn"], 1)

                def mix_out(t):
                    dve.wait_ge(s["dmixT_hi"], t + 1)
                    if t >= 2:
                        dve.wait_ge(s["dh_psum"], t - 1)
                    dve.tensor_tensor(mixT_lo[t % 2].rearrange("p (b n) -> p b n", b=2), PS[:, 0:2, :],
                                      mixT_hi[t % 2].bitcast(fp32).rearrange("p (b n) -> p b n", b=2), ALU.subtract).then_inc(s["dmixT"], 1)

                def route(t):
                    dve.wait_ge(s["dlg_psum"], t + 1)
                    if t == 0:
                        dve.wait_ge(s["dwr_loaded"], 64)
                        dve.wait_ge(s["dconst"], 1)
                    dve.tensor_tensor(lg[:, 0:EG], PS[:, 7, 0:EG], rbias[:, 0:EG], ALU.add)
                    lk(dve.tensor_tensor(lg[:, 8:], PS[:, 7, EG:EG + E], rbias[:, EG:], ALU.add))
                    lk(dve.max(g8, lg[:, 0:8]))
                    dve.tensor_scalar(gdiff[:, t, :], lg[:, 0:EG], g8[:, 0:1], None, ALU.subtract)
                    lk(dve.max_index(gi, g8, lg[:, 0:8]))
                    lk(dve.tensor_copy(gs, gi[:, 0:1]))
                    lk(dve.tensor_scalar(gm, e_grp, gs, None, ALU.is_equal))
                    dve.tensor_tensor(em, lg[:, 8:], gm, ALU.mult)
                    lk(dve.tensor_scalar(pr1, gm, -1.0, -NEG, ALU.add, ALU.mult))
                    lk(dve.tensor_tensor(em, em, pr1, ALU.add))
                    lk(dve.max(v8, em))
                    dve.tensor_tensor(vdiff[:, t:t + 1], v8[:, 1:2], v8[:, 0:1], ALU.subtract).then_inc(s["dlg"], 1)
                    lk(dve.max_index(vi, v8, em))
                    lk(dve.tensor_copy(i12, vi[:, 0:2]))
                    dve.tensor_scalar(o1, e_id, i12[:, 0:1], None, ALU.is_equal)
                    lk(dve.tensor_scalar(o2, e_id, i12[:, 1:2], None, ALU.is_equal))
                    if t >= 1:
                        dve.wait_ge(s["drank_psum"], t)
                    link(dve, "dmask", dve.tensor_tensor(mm, o1, o2, ALU.add))

                def place(t):
                    dve.wait_ge(s["drank_psum"], t + 1)
                    lk(dve.tensor_tensor(rk_, PS[:, 2, 256:256 + E], e_base, ALU.add))
                    dve.tensor_tensor(o1, o1, rk_, ALU.mult)
                    lk(dve.tensor_tensor(o2, o2, rk_, ALU.mult))
                    dve.tensor_reduce(slots_f[:, t, 0:1], o1, AX.X, ALU.add)
                    lk(dve.tensor_reduce(slots_f[:, t, 1:2], o2, AX.X, ALU.add))
                    dve.tensor_copy(dest[:, t, :], slots_f[:, t, :]).then_inc(s["ddest"], 1)
                    link(dve, "dmsum", dve.tensor_tensor(msum, msum, mm, ALU.add))

                mix_norm(0)
                mix_out(0)
                for k in range(2):
                    dve.wait_ge(s["dw_hi"], k + 1)
                    low_wout(dve, k).then_inc(s["dw_lo"], 1)
                for t in range(NT + 2):
                    if t + 1 < NT:
                        mix_norm(t + 1)
                    if t + 1 < NT:
                        mix_out(t + 1)
                    if 1 <= t <= NT:
                        dve.wait_ge(s["dhn_tr"], t)
                        dve.tensor_tensor(hnT[(t - 1) % 2].rearrange("p (k c) -> p k c", k=KD),
                                          PS[:, 5:7, :].rearrange("p b (k c) -> p (b k) c", c=P),
                                          vec("ln2").unsqueeze(2).broadcast_to((P, KD, P)), ALU.mult).then_inc(s["dhnT"], 1)
                    if t < NT:
                        dve.wait_ge(s["dh_psum"], t + 1)
                        dve.wait_ge(s["dx_loaded%d" % t], 16)
                        dve.tensor_tensor(h[:, t, :].rearrange("p (b n) -> p b n", b=2), h[:, t, :].rearrange("p (b n) -> p b n", b=2),
                                          PS[:, 3:5, :], ALU.add).then_inc(s["dh"], 1)
                    if t >= 2:
                        place(t - 2)
                    if t < NT:
                        dve.wait_ge(s["dh_rms"], t + 1)
                        if t >= 1:
                            dve.wait_ge(s["dhn"], t)
                        dve.reciprocal(stat[:, 18:19], stat[:, 17:18]).then_inc(s["dh_rstd"], 1)
                    if 1 <= t <= NT:
                        route(t - 1)
                dve.wait_ge(s["dgexp"], 1)
                lk(dve.tensor_reduce(gsum, gdiff, AX.X, ALU.add))
                lk(dve.tensor_scalar(wsum, vdiff, 1.0, None, ALU.add))
                lk(dve.tensor_tensor(gsum, gsum, wsum, ALU.mult))
                lk(dve.reciprocal(wts[:, :, 0], gsum))
                lk(dve.tensor_tensor(wts[:, :, 1], wts[:, :, 0], vdiff, ALU.mult))
                dve.wait_ge(s["dtok_tr"], 1)
                lk(dve.tensor_copy(idf, PS[:, 6, 0:E]))
                lk(dve.tensor_scalar(idg, idf, float(S), -float(S), ALU.is_ge, ALU.mult))
                lk(dve.tensor_tensor(idg, idg, idf, ALU.add))
                dve.tensor_copy(from_, idg)
                dve.tensor_copy(to_, idf).then_inc(s["didx"], 1)

            @block.tensor
            def _(pe):

                def flip_s(t):
                    if t >= 1:
                        pe.wait_ge(s["dmixn"], t)
                    if t >= 4:
                        pe.wait_ge(s["ddest"], t - 3)
                    for f in range(2):
                        last = pe.transpose(PS[:, 2, f * P:(f + 1) * P], sT[:, f, t * P:(t + 1) * P], ident[:, :])
                    last.then_inc(s["ds_tr"], 1)

                def flip_mix(t):
                    pe.wait_ge(s["dmixn"], t + 1)
                    if t >= 1:
                        pe.wait_ge(s["dmixT"], t)
                    for k in range(KD):
                        last = pe.transpose(PS[:, k // 4, (k % 4) * P:(k % 4 + 1) * P], mixn[t % 2][:, k * P:(k + 1) * P], ident[:, :])
                    last.then_inc(s["dmix_tr"], 1)

                def router(t):
                    pe.wait_ge(s["dhn"], t + 1)
                    if t >= 1:
                        pe.wait_ge(s["dhnT"], t)
                    for k in range(KD):
                        last = pe.transpose(PS[:, 5 + k // 4, (k % 4) * P:(k % 4 + 1) * P], hn[t % 2][:, k * P:(k + 1) * P], ident[:, :])
                    last.then_inc(s["dhn_tr"], 1)

                def logits(t):
                    pe.wait_ge(s["dhnT"], t + 1)
                    if t >= 1:
                        pe.wait_ge(s["dmask"], t)
                    for k in range(KD):
                        last = pe.matmul(PS[:, 7, 0:EG + E], hnT[t % 2][:, k * P:(k + 1) * P], wr[:, k, :], start=k == 0, stop=k == KD - 1)
                    last.then_inc(s["dlg_psum"], 1)

                def ranks(t):
                    pe.wait_ge(s["dmask"], t + 1)
                    if t >= 1:
                        pe.wait_ge(s["dmsum"], t)
                    pe.wait_ge(s["dmixn"], min(t + 4, NT))
                    pe.matmul(PS[:, 2, 256:256 + E], upper, mm, start=True, stop=False)
                    pe.matmul(PS[:, 2, 256:256 + E], ones, msum, start=False, stop=True).then_inc(s["drank_psum"], 1)

                flip_s(0)
                flip_mix(0)

                def out_product(t, half):
                    for n, k in list(enumerate((2, 3, 4, 5, 6, 7, 0, 1)))[4 * half:4 * half + 4]:
                        if t == 0 and k < 2:
                            pe.wait_ge(s["dw_hi"], k + 1)
                            pe.wait_ge(s["dw_lo"], k + 1)
                        hi, lo = [m[t % 2][:, k * P:(k + 1) * P] for m in (mixT_hi, mixT_lo)]
                        for b in range(2):
                            c = slice(b * 512, (b + 1) * 512)
                            pe.matmul(PS[:, 3 + b, :], hi, wout_hi[:, k, c], start=n == 0, stop=False)
                            pe.matmul(PS[:, 3 + b, :], hi, wout_lo[:, k, c], start=False, stop=False)
                            last = pe.matmul(PS[:, 3 + b, :], lo, wout_hi[:, k, c], start=False, stop=n == KD - 1)
                    if half:
                        last.then_inc(s["dh_psum"], 1)

                def flip_p(n):
                    if n == 0:
                        pe.wait_ge(s["dp_loaded"], 16 * NT)
                        pe.wait_ge(s["dmixT"], NT)
                    else:
                        pe.wait_ge(s["dhnT"], NT)
                    for m in range(8):
                        last = pe.transpose(PS[:, (0, 5)[n] + m // 4, (m % 4) * P:(m % 4 + 1) * P], ptile[4 * n + m // 2][:, (m % 2) * P:(m % 2 + 1) * P],
                                            ident[:, :])
                    last.then_inc(s["dpT_psum"], 1)

                def embed(t):
                    pe.wait_ge(s["dpT"], 1)
                    if t == 0:
                        pe.wait_ge(s["dwple_loaded"], 16)
                        pe.wait_ge(s["dh"], NT)
                    if t >= 2:
                        pe.wait_ge(s["dple"], t - 1)
                    ple_product(pe, t, (3, 0)[t % 2]).then_inc(s["dple_psum"], 1)

                pe.wait_ge(s["dconst"], 1)
                for t in range(NT + 2):
                    if t == NT + 1:
                        embed(0)
                    if t + 1 < NT:
                        flip_s(t + 1)
                    if t < NT:
                        pe.wait_ge(s["dmixT"], t + 1)
                        if t >= 1:
                            pe.wait_ge(s["dh"], t)
                        out_product(t, 0)
                    if t + 1 < NT:
                        flip_mix(t + 1)
                    if 1 <= t <= NT:
                        router(t - 1)
                    if t < NT:
                        out_product(t, 1)
                    if t >= 2:
                        ranks(t - 2)
                    if t == NT:
                        flip_p(0)
                    if 1 <= t <= NT:
                        if t == 1:
                            pe.wait_ge(s["dwr_loaded"], 64)
                        logits(t - 1)
                flip_p(1)
                embed(1)
                pe.wait_ge(s["ddest"], NT)
                pe.wait_ge(s["dmsum"], NT)
                pe.matmul(PS[:, 7, 128:128 + E], ones, msum, start=True, stop=True)
                embed(2)
                pe.wait_ge(s["dtok_loaded"], 16)
                pe.wait_ge(s["dpT"], 2)
                pe.transpose(PS[:, 6, 0:E], tokrow[0:E, :], ident[0:E, 0:E]).then_inc(s["dtok_tr"], 1)

        eo = [0]

        def ine(n):
            eo[0] += n
            return R2[:, eo[0] - n:eo[0]]
        xg, xgT, yb = [[ine(1024), ine(1024)] for _ in range(3)]
        act_, actT, sil = [[ine(F), ine(F)] for _ in range(3)]
        tokc, tokf = ine(1), ine(1)
        o_from, o_to = ine(1).bitcast(u32), ine(1).bitcast(u32)
        signals("e", ("dve", "ple_psum", "ple", "xg_loaded0", "xg_loaded1", "xT_psum", "xgT", "up_psum", "silu", "act", "actT_psum", "actT", "y_psum", "yv", "ya",
                  "y_stored"), "e")

        def ge(e, n):
            return not isinstance(e, int) or e >= n

        def lt(e, n):
            return not isinstance(e, int) or e < n

        def pairs(eng, step):
            for e in (0, 1):
                step(e, e, 0)
            with eng.Fori(1, E // 2 - 1) as i:
                for u in range(2):
                    step(i * 2 + u, u, i)
            for e in (E - 2, E - 1):
                step(e, e % 2, E // 2 - 1)

        with nc.Block() as block:
            @block.sync
            def _(sp):
                def step(e, u, i):
                    if lt(e, E - 2):
                        sp.wait_ge(s["eup_psum"], e + 1)
                        load_w13(sp, e + 2, u)
                    if ge(e, 1) and lt(e, E - 1):
                        sp.wait_ge(s["ey_psum"], e)
                        load_w2(sp, e + 1, 1 - u)
                pairs(sp, step)

            @block.gpsimd
            def _(pool):
                def gather(e):
                    if e >= 2:
                        pool.wait_ge(s["exT_psum"], e - 1)
                    pool.indirect_dma_start(xg[e % 2], None, xf_d, bass.IndirectOffsetOnAxis(ap=from_[:, e:e + 1], axis=0),
                                            bounds_check=S - 1, oob_is_err=False).then_inc(s["exg_loaded%d" % (e % 2)], 16)
                gather(0)
                for e in range(E + 2):
                    u = e % 2
                    if e + 1 < E:
                        gather(e + 1)
                    if e >= 2:
                        pool.wait_ge(s["eyv"], e - 1)
                        pool.wait_ge(s["eya"], e - 1)
                        if e >= 3:
                            pool.wait_ge(s["ey_stored"], 16 * (e - 2))
                        pool.indirect_dma_start(y_d, bass.IndirectOffsetOnAxis(ap=to_[:, e - 2:e - 1], axis=0), yb[u], None,
                                                bounds_check=2 * S - 1, oob_is_err=False).then_inc(s["ey_stored"], 16)
                pool.wait_ge(s["ey_stored"], 16 * E)

            @block.scalar
            def _(act):
                def y_out(e, u, i):
                    act.wait_ge(s["ey_psum"], e + 1)
                    if ge(e, 2):
                        act.wait_ge(s["ey_stored"], e * 16 - 16)
                    act.activation(yb[u][:, 512:1024], PS[:, 6, :], ACT.Copy).then_inc(s["eya"], 1)

                def step(e, u, i):
                    act.wait_ge(s["eup_psum"], e + 1)
                    if ge(e, 2):
                        act.wait_ge(s["eact"], e - 1)
                    act.activation(sil[u], PS[:, 2 + u, 0:F], ACT.Silu).then_inc(s["esilu"], 1)
                    if ge(e, 1):
                        y_out(e - 1, 1 - u, i if u else i - 1)
                    act.wait_ge(s["eactT_psum"], e + 1)
                    act.activation(actT[u], PS[:, 4, 0:F], ACT.Copy).then_inc(s["eactT"], 1)
                def ple_out(t):
                    act.wait_ge(s["eple_psum"], t - PLE_EARLY + 1)
                    act.activation(ple[:, t, :].rearrange("p (b n) -> p b n", b=2), PS[:, 2:4, :], ACT.Copy).then_inc(s["eple"], 1)
                for t in range(PLE_EARLY, PLE_LATE - 1):
                    ple_out(t)
                pairs(act, step)
                y_out(E - 1, 1, E // 2 - 1)
                ple_out(PLE_LATE - 1)

            @block.vector
            def _(dve):
                def x_out(e, u, i):
                    dve.wait_ge(s["exT_psum"], e + 1)
                    if ge(e, 2):
                        dve.wait_ge(s["eup_psum"], e - 1)
                    dve.tensor_tensor(xgT[u].rearrange("p (k c) -> p k c", k=KD), PS[:, 0:2, :].rearrange("p b (k c) -> p (b k) c", c=P),
                                      vec("ln2").unsqueeze(2).broadcast_to((P, KD, P)), ALU.mult).then_inc(s["exgT"], 1)

                def y_out(e, u, i):
                    dve.wait_ge(s["ey_psum"], e + 1)
                    if ge(e, 2):
                        dve.wait_ge(s["ey_stored"], e * 16 - 16)
                    dve.tensor_copy(yb[u][:, 0:512], PS[:, 5, :]).then_inc(s["eyv"], 1)

                def step(e, u, i):
                    dve.wait_ge(s["esilu"], e + 1)
                    if ge(e, 2):
                        dve.wait_ge(s["eactT_psum"], e - 1)
                    dve.tensor_tensor(act_[u], sil[u], PS[:, 2 + u, F:2 * F], ALU.mult).then_inc(s["eact"], 1)
                    if lt(e, E - 1):
                        x_out(e + 1, 1 - u, i)
                    if ge(e, 1):
                        y_out(e - 1, 1 - u, i if u else i - 1)

                def lk(ins):
                    link(dve, "edve", ins)
                lk(dve.tensor_copy(cnt, PS[:, 7, 128:128 + E]))
                lk(dve.tensor_scalar(nov, cnt, float(P), None, ALU.is_gt))
                for b in range(2, S // P):
                    lk(dve.scalar_tensor_tensor(nov, cnt, float(P * b), nov, ALU.is_gt, ALU.add))
                lk(dve.tensor_tensor_scan(cum, ones[:, 0:E], nov, 0.0, ALU.mult, ALU.add))
                big = junk.bitcast(fp32)[:, 0:OVER * E].rearrange("p (j e) -> p j e", e=E)
                cb = cum.unsqueeze(1).broadcast_to((P, OVER, E))
                lk(dve.tensor_tensor(big, cb, jj.unsqueeze(2).broadcast_to((P, OVER, E)), ALU.is_le))
                lk(dve.tensor_reduce(ej, big, AX.X, ALU.add))
                lk(dve.tensor_tensor(big, big, nov.unsqueeze(1).broadcast_to((P, OVER, E)), ALU.mult))
                lk(dve.tensor_reduce(bj, big, AX.X, ALU.add))
                lk(dve.tensor_tensor(bj, jj, bj, ALU.subtract))
                lk(dve.tensor_scalar(bj, bj, float(P), float(P), ALU.mult, ALU.add))
                lk(dve.tensor_scalar(ej, ej, float(E - 1), None, ALU.min))
                lk(dve.scalar_tensor_tensor(bj, ej, float(S), bj, ALU.mult, ALU.add))
                lk(dve.tensor_scalar(bj, bj, float(E * S - P), None, ALU.min))
                dve.tensor_copy(tab[:, 0:1], cum[:, E - 1:E])
                dve.tensor_copy(tab[:, 1:1 + OVER], ej)
                dve.tensor_copy(tab[:, 1 + OVER:1 + 2 * OVER], bj)
                x_out(0, 0, 0)
                pairs(dve, step)
                y_out(E - 1, 1, E // 2 - 1)

            @block.tensor
            def _(pe):
                def flip_x(e, u, i):
                    pe.wait_ge(s["exg_loaded%d" % u], i * 16 + 16)
                    if ge(e, 1):
                        pe.wait_ge(s["exgT"], e)
                    for k in range(KD):
                        last = pe.transpose(PS[:, k // 4, (k % 4) * P:(k % 4 + 1) * P], xg[u][:, k * P:(k + 1) * P], ident[:, :])
                    last.then_inc(s["exT_psum"], 1)

                def down(e, u, i):
                    pe.wait_ge(s["eactT"], e + 1)
                    pe.wait_ge(wb_loaded[u], i * 16 + 16)
                    if ge(e, 1):
                        pe.wait_ge(s["eyv"], e)
                        pe.wait_ge(s["eya"], e)
                    for b in range(2):
                        for k in range(2):
                            last = pe.matmul(PS[:, 5 + b, :], actT[u][:, k * P:(k + 1) * P], w2r[u][:, k, b * 512:(b + 1) * 512],
                                             start=k == 0, stop=k == 1)
                    last.then_inc(s["ey_psum"], 1)

                def step(e, u, i):
                    pe.wait_ge(s["exgT"], e + 1)
                    pe.wait_ge(wa_loaded[u], i * 32 + 32)
                    if ge(e, 2):
                        pe.wait_ge(s["eact"], e - 1)
                    for k in range(KD):
                        last = pe.matmul(PS[:, 2 + u, :], xgT[u][:, k * P:(k + 1) * P], w13r[u][:, k, :, :].rearrange("p a n -> p (a n)"),
                                         start=k == 0, stop=k == KD - 1)
                    last.then_inc(s["eup_psum"], 1)
                    if lt(e, E - 1):
                        flip_x(e + 1, 1 - u, i + u)
                    if ge(e, 1):
                        down(e - 1, 1 - u, i if u else i - 1)
                    pe.wait_ge(s["eact"], e + 1)
                    if ge(e, 1):
                        pe.wait_ge(s["eactT"], e)
                    for k in range(2):
                        last = pe.transpose(PS[:, 4, k * P:(k + 1) * P], act_[u][:, k * P:(k + 1) * P], ident[:, :])
                    last.then_inc(s["eactT_psum"], 1)
                for t in range(PLE_EARLY, PLE_LATE - 1):
                    if t > PLE_EARLY:
                        pe.wait_ge(s["eple"], t - PLE_EARLY)
                    ple_product(pe, t, 2).then_inc(s["eple_psum"], 1)
                flip_x(0, 0, 0)
                pe.wait_ge(s["eple"], PLE_LATE - 1 - PLE_EARLY)
                pairs(pe, step)
                down(E - 1, 1, E // 2 - 1)
                pe.wait_ge(s["eact"], E)
                ple_product(pe, PLE_LATE - 1, 2).then_inc(s["eple_psum"], 1)

        signals("o", ("w_loaded", "tok_loaded", "idx", "x_loaded", "xT_psum", "xT", "up_psum", "silu", "act", "actT_psum", "actT", "y_psum", "y", "y_stored"), "o")
        ou = 0

        def few(eng, step):
            number = eng.value_load(tab[0:1, 0:1], min_val=0, max_val=OVER)
            with eng.If(number > 0):
                for j in range(OVER):
                    with eng.If(number > j):
                        step(j)

        def overflow(eng, step):
            number = eng.value_load(tab[0:1, 0:1], min_val=0, max_val=OVER)
            with eng.If(number > 0):
                with eng.Fori(0, OVER) as j:
                    with eng.If(number > j):
                        step(j)

        with nc.Block() as block:
            @block.sync
            def _(sp):
                w1v, w3v, w2v = [v.rearrange("e (k p) n -> e p k n", p=P) for v in (w1, w3, w2)]

                def step(j):
                    expert = sp.value_load(tab[0:1, j + 1:j + 2], min_val=0, max_val=E - 1)
                    base = sp.value_load(tab[0:1, j + 1 + OVER:j + 2 + OVER], min_val=0, max_val=E * S - P)
                    sp.dma_start(tokc, tok_d[bass.ds(base, P), :]).then_inc(s["otok_loaded"], 16)
                    for a, v in ((0, w1v), (1, w3v)):
                        sp.dma_start(w13r[ou][:, :, a, :], v[bass.ds(expert, 1)].rearrange("e p k n -> (e p) k n")).then_inc(s["ow_loaded"], 16)
                    sp.dma_start(w2r[ou], w2v[bass.ds(expert, 1)].rearrange("e p k n -> (e p) k n")).then_inc(s["ow_loaded"], 16)
                    sp.wait_ge(s["oy_stored"], j * 16 + 16)
                few(sp, step)

            @block.gpsimd
            def _(pool):
                def step(j):
                    pool.wait_ge(s["otok_loaded"], j * 16 + 16)
                    n = 5 * j
                    pool.tensor_scalar(tokf, tokc, float(S), -float(S), ALU.is_ge, ALU.mult).then_inc(s["oidx"], 1)
                    pool.wait_ge(s["oidx"], n + 1)
                    pool.tensor_tensor(tokf, tokf, tokc, ALU.add).then_inc(s["oidx"], 1)
                    pool.wait_ge(s["oidx"], n + 2)
                    pool.tensor_scalar(tokf, tokf, float(S - 1), None, ALU.min).then_inc(s["oidx"], 1)
                    pool.wait_ge(s["oidx"], n + 3)
                    pool.tensor_copy(o_from, tokf).then_inc(s["oidx"], 1)
                    pool.tensor_copy(o_to, tokc).then_inc(s["oidx"], 1)
                    pool.wait_ge(s["oidx"], n + 5)
                    pool.indirect_dma_start(xg[ou], None, xf_d, bass.IndirectOffsetOnAxis(ap=o_from, axis=0)).then_inc(s["ox_loaded"], 16)
                    pool.wait_ge(s["oy"], j + 1)
                    pool.indirect_dma_start(y_d, bass.IndirectOffsetOnAxis(ap=o_to, axis=0), yb[ou], None,
                                            bounds_check=2 * S - 1, oob_is_err=False).then_inc(s["oy_stored"], 16)
                    pool.wait_ge(s["oy_stored"], 16 * j + 16)
                few(pool, step)

            @block.scalar
            def _(act):
                def step(j):
                    act.wait_ge(s["oup_psum"], j + 1)
                    act.activation(sil[ou], PS[:, 2, 0:F], ACT.Silu).then_inc(s["osilu"], 1)
                    act.wait_ge(s["oactT_psum"], j + 1)
                    act.activation(actT[ou], PS[:, 4, 0:F], ACT.Copy).then_inc(s["oactT"], 1)
                overflow(act, step)

            @block.vector
            def _(dve):
                def step(j):
                    dve.wait_ge(s["oxT_psum"], j + 1)
                    dve.tensor_tensor(xgT[ou].rearrange("p (k c) -> p k c", k=KD), PS[:, 0:2, :].rearrange("p b (k c) -> p (b k) c", c=P),
                                      vec("ln2").unsqueeze(2).broadcast_to((P, KD, P)), ALU.mult).then_inc(s["oxT"], 1)
                    dve.wait_ge(s["osilu"], j + 1)
                    dve.tensor_tensor(act_[ou], sil[ou], PS[:, 2, F:2 * F], ALU.mult).then_inc(s["oact"], 1)
                    dve.wait_ge(s["oy_psum"], j + 1)
                    dve.tensor_copy(yb[ou].rearrange("p (b n) -> p b n", b=2), PS[:, 5:7, :]).then_inc(s["oy"], 1)
                overflow(dve, step)

            @block.tensor
            def _(pe):
                def step(j):
                    pe.wait_ge(s["ox_loaded"], j * 16 + 16)
                    for k in range(KD):
                        last = pe.transpose(PS[:, k // 4, (k % 4) * P:(k % 4 + 1) * P], xg[ou][:, k * P:(k + 1) * P], ident[:, :])
                    last.then_inc(s["oxT_psum"], 1)
                    pe.wait_ge(s["ow_loaded"], j * 48 + 48)
                    pe.wait_ge(s["oxT"], j + 1)
                    for k in range(KD):
                        last = pe.matmul(PS[:, 2, :], xgT[ou][:, k * P:(k + 1) * P], w13r[ou][:, k, :, :].rearrange("p a n -> p (a n)"),
                                         start=k == 0, stop=k == KD - 1)
                    last.then_inc(s["oup_psum"], 1)
                    pe.wait_ge(s["oact"], j + 1)
                    for k in range(2):
                        last = pe.transpose(PS[:, 4, k * P:(k + 1) * P], act_[ou][:, k * P:(k + 1) * P], ident[:, :])
                    last.then_inc(s["oactT_psum"], 1)
                    pe.wait_ge(s["oactT"], j + 1)
                    for b in range(2):
                        for k in range(2):
                            last = pe.matmul(PS[:, 5 + b, :], actT[ou][:, k * P:(k + 1) * P], w2r[ou][:, k, b * 512:(b + 1) * 512],
                                             start=k == 0, stop=k == 1)
                    last.then_inc(s["oy_psum"], 1)
                overflow(pe, step)

        y1, y2, gate, outb = [[slot[n][:, 0:D], slot[n][:, D:]] for n in (6, 9, 7, 8)]
        wpg_hi = RQKV_r[:, 0:KD * D].rearrange("p (k n) -> p k n", k=KD)
        hT_hi, hT_lo = [[RQKV_r[:, a:a + D] for a in (at, at + D)] for at in (8192, 10240)]
        wpg, wpg_lo = [r[:, 0:KD * D].rearrange("p (k n) -> p k n", k=KD) for r in (R2, R2_r)]
        bpg = R1[:, 8192:8192 + D]
        prodf = [R1[:, 9216:9216 + D], R1[:, 10240:10240 + D]]
        signals("f", ("ple_psum", "ple", "bpg_loaded", "w_hi", "w_lo", "hT_hi", "y_loaded0", "y_loaded1", "h1", "h", "hT_psum", "hT", "gate_psum", "gate", "sig",
                  "prod", "out", "stored0", "stored1") + tuple("w_loaded%d" % k for k in range(KD)), "f")
        with nc.Block() as block:
            @block.sync
            def _(sp):
                def load_y(t):
                    if t >= 2:
                        sp.wait_ge(s["fh"], t - 1)
                    for c, y_ in ((0, y1[t % 2]), (1, y2[t % 2])):
                        if t == 0 and c == 1:
                            continue
                        sp.dma_start(y_, y_d[c * S + t * P:c * S + (t + 1) * P, :]).then_inc(s["fy_loaded%d" % (t % 2)], 16)
                load_y(0)
                load_y(1)
                for t in range(NT + 1):
                    if t + 2 < NT:
                        load_y(t + 2)
                    if t >= 1:
                        sp.wait_ge(s["fout"], t)
                        sp.dma_start(out[(t - 1) * P:t * P, :], outb[(t - 1) % 2]).then_inc(s["fstored%d" % ((t - 1) % 2)], 16)
                for u in range(2):
                    sp.wait_ge(s["fstored%d" % u], 16 * (NT // 2))

            @block.scalar
            def _(act):
                act.dma_start(y2[0], y_d[S:S + P, :]).then_inc(s["fy_loaded0"], 16)
                for k in range(KD):
                    act.dma_start(wpg[:, k, :], w_pg[k * P:(k + 1) * P, :]).then_inc(s["fw_loaded%d" % k], 16)
                act.dma_start(bpg, row_bcast(b_pg)).then_inc(s["fbpg_loaded"], 16)

                def turned(t):
                    act.wait_ge(s["fhT_psum"], t + 1)
                    if t >= 2:
                        act.wait_ge(s["fgate_psum"], t - 1)
                    act.activation(hT_hi[t % 2].rearrange("p (b n) -> p b n", b=2), PS[:, 6 * (t % 2):6 * (t % 2) + 2, :], ACT.Copy).then_inc(s["fhT_hi"], 1)

                def ple_out(t):
                    act.wait_ge(s["fple_psum"], t - PLE_LATE + 1)
                    b = (2, 4)[(t - PLE_LATE) % 2]
                    act.activation(ple[:, t, :].rearrange("p (b n) -> p b n", b=2), PS[:, b:b + 2, :], ACT.Copy).then_inc(s["fple"], 1)
                ple_out(PLE_LATE)
                for k in range(KD):
                    if k == 2:
                        turned(0)
                        for t in range(PLE_LATE + 1, NT):
                            ple_out(t)
                    act.wait_ge(s["fw_loaded%d" % k], 16)
                    act.activation(wpg_hi[:, k, :], wpg[:, k, :], ACT.Copy).then_inc(s["fw_hi"], 1)
                for t in range(NT):
                    if t + 1 < NT:
                        turned(t + 1)
                    act.wait_ge(s["fgate"], t + 1)
                    act.activation(gate[t % 2], gate[t % 2], ACT.Sigmoid).then_inc(s["fsig"], 1)

            @block.vector
            def _(dve):
                def add_y(t):
                    u = t % 2
                    dve.wait_ge(s["fy_loaded%d" % u], 32 * (t // 2 + 1))
                    link(dve, "fh1", dve.scalar_tensor_tensor(h[:, t, :], y1[u], wts[:, t, 0:1], h[:, t, :], ALU.mult, ALU.add))
                    dve.scalar_tensor_tensor(h[:, t, :], y2[u], wts[:, t, 1:2], h[:, t, :], ALU.mult, ALU.add).then_inc(s["fh"], 1)

                def turned(t):
                    dve.wait_ge(s["fhT_hi"], t + 1)
                    if t >= 2:
                        dve.wait_ge(s["fgate_psum"], t - 1)
                    dve.tensor_tensor(hT_lo[t % 2].rearrange("p (b n) -> p b n", b=2), PS[:, 6 * (t % 2):6 * (t % 2) + 2, :],
                                      hT_hi[t % 2].bitcast(fp32).rearrange("p (b n) -> p b n", b=2), ALU.subtract).then_inc(s["fhT"], 1)
                add_y(0)
                add_y(1)
                for k in range(KD):
                    if k == 2:
                        turned(0)
                    dve.wait_ge(s["fw_hi"], k + 1)
                    dve.tensor_tensor(wpg_lo[:, k, :], wpg[:, k, :], wpg_hi[:, k, :].bitcast(fp32), ALU.subtract).then_inc(s["fw_lo"], 1)
                dve.wait_ge(s["fbpg_loaded"], 16)
                for t in range(NT + 1):
                    if t < NT:
                        if t + 2 < NT:
                            add_y(t + 2)
                        if t + 1 < NT:
                            turned(t + 1)
                        u = t % 2
                        dve.wait_ge(s["fgate_psum"], t + 1)
                        if t >= 2:
                            dve.wait_ge(s["fprod"], t - 1)
                        dve.tensor_tensor(gate[u].rearrange("p (b n) -> p b n", b=2), PS[:, 2 + 2 * u:4 + 2 * u, :], bpg.rearrange("p (b n) -> p b n", b=2),
                                          ALU.add).then_inc(s["fgate"], 1)
                        dve.wait_ge(s["fsig"], t + 1)
                        link(dve, "fprod", dve.tensor_tensor(prodf[u], gate[u], ple[:, t, :], ALU.mult))
                        if t >= 2:
                            dve.wait_ge(s["fstored%d" % u], 16 * (t // 2))
                        dve.tensor_tensor(outb[u], prodf[u], h[:, t, :], ALU.add).then_inc(s["fout"], 1)

            @block.tensor
            def _(pe):
                def turn(t):
                    pe.wait_ge(s["fh"], t + 1)
                    if t >= 2:
                        pe.wait_ge(s["fhT"], t - 1)
                    for k in range(KD):
                        last = pe.transpose(PS[:, 6 * (t % 2) + k // 4, (k % 4) * P:(k % 4 + 1) * P], h[:, t, k * P:(k + 1) * P], ident[:, :])
                    last.then_inc(s["fhT_psum"], 1)

                def product(bank, a_hi, a_lo, k, n, b_hi, b_lo):
                    a_hi, a_lo = a_hi[:, k * P:(k + 1) * P], a_lo[:, k * P:(k + 1) * P]
                    for b in range(2):
                        c = slice(b * 512, (b + 1) * 512)
                        pe.matmul(PS[:, bank + b, :], a_hi, b_hi[:, k, c], start=k == 0, stop=False)
                        pe.matmul(PS[:, bank + b, :], a_hi, b_lo[:, k, c], start=False, stop=False)
                        last = pe.matmul(PS[:, bank + b, :], a_lo, b_hi[:, k, c], start=False, stop=k == n - 1)
                    return last
                for t in range(PLE_LATE, NT):
                    if t >= PLE_LATE + 2:
                        turn(0)
                        pe.wait_ge(s["fple"], t - PLE_LATE - 1)
                    ple_product(pe, t, (2, 4)[(t - PLE_LATE) % 2]).then_inc(s["fple_psum"], 1)
                turn(1)
                pe.wait_ge(s["fple"], NT - PLE_LATE)
                for t in range(NT):
                    pe.wait_ge(s["fhT"], t + 1)
                    if t >= 2:
                        pe.wait_ge(s["fgate"], t - 1)
                    for k in range(KD):
                        if t == 0:
                            pe.wait_ge(s["fw_hi"], k + 1)
                            pe.wait_ge(s["fw_lo"], k + 1)
                        last = product(2 + 2 * (t % 2), hT_hi[t % 2], hT_lo[t % 2], k, KD, wpg_hi, wpg_lo)
                    last.then_inc(s["fgate_psum"], 1)
                    if t + 2 < NT:
                        turn(t + 2)


_INS = ['x', 'p', 'ln1', 'w_in', 'g_cq', 'g_ckv', 'w_uq', 'w_ukv', 'g_qh', 'g_kh', 'sg_ln_g', 'sg_ln_b',
        'sg_w', 'sg_b', 'lam_re', 'lam_im', 'log_dt', 'ssm_b_re', 'ssm_b_im', 'ssm_c_re', 'ssm_c_im',
        'ssm_d', 'w_glu', 'b_glu', 'g_mix', 'w_out', 'ln2', 'w_rg', 'b_rg', 'w_rexp', 'b_rexp', 'w1',
        'w3', 'w2', 'w_pg', 'b_pg', 'w_ple']
_OUTS = [((1, S, D), 'float32')]


def kernel(**inputs):
    import numpy as _np
    import concourse.bacc as _bacc
    from concourse import mybir as _mybir
    from concourse.bass_utils import run_bass_kernel_spmd as _run

    inv = (1.0 / (_np.float32(10000.0) ** (_np.arange(0, ROPE, 2, dtype=_np.float32) / _np.float32(ROPE)))).astype(_np.float32)
    ang = _np.arange(S, dtype=_np.float32)[:, None] * inv[None, :]
    laid = {name: inputs[name] for name in _INS}
    laid["rope_cos"], laid["rope_sin"] = _np.cos(ang), _np.sin(ang)

    nc = _bacc.Bacc("TRN2", target_bir_lowering=False, num_devices=1)
    arrays, args = {}, []
    for name, a in laid.items():
        a = _np.ascontiguousarray(a)
        arrays[f"in_{name}_dram"] = a
        args.append(nc.dram_tensor(f"in_{name}_dram", a.shape, _mybir.dt.from_np(a.dtype), kind="ExternalInput").ap())
    for i, (shape, dtype) in enumerate(_OUTS):
        dt = _mybir.dt.from_np(_np.dtype(dtype))
        args.append(nc.dram_tensor(f"out_{i}_dram", shape, dt, kind="ExternalOutput").ap())
    trunk_kernel(nc, *args)
    r = _run(nc, [arrays], core_ids=[0])
    return r.results[0]["out_0_dram"]
```
